# Optimizing a Trainium2 kernel written in Bass

```python
import math
import jax, jax.numpy as jnp
from jax import lax
import numpy as np

D_MODEL = 1024
BATCH = 1
SEQ = 512
DEPTH = 2

CHUNK = 64
Q_BLOCK = 128
DIFF_HEADS = 4
DIFF_QK_DIM = 64
DIFF_V_DIM = 2 * DIFF_QK_DIM
DIFF_QK_WIDTH = DIFF_HEADS * 2 * DIFF_QK_DIM
DIFF_WIDTH = DIFF_HEADS * DIFF_V_DIM
SSM_WIDTH = D_MODEL - DIFF_WIDTH
SSM_GROUP = 16
SSM_GROUPS = SSM_WIDTH // SSM_GROUP
SSM_STATE = 64
EVEN_IN = 2 * DIFF_QK_WIDTH + DIFF_WIDTH + SSM_WIDTH
FOX_HEAD_DIM = 64
FOX_HEADS = D_MODEL // FOX_HEAD_DIM
FOX_IN = 3 * D_MODEL + FOX_HEADS
D_FF = 4 * D_MODEL
ROPE_THETA = 10000.0
LN_EPS = 1e-5
RMS_EPS = 1e-6
DEEPNORM_ALPHA = (2 * DEPTH) ** 0.25
DEEPNORM_BETA = (8 * DEPTH) ** -0.25
N_EVEN = (DEPTH + 1) // 2
N_ODD = DEPTH // 2

kernel_name = "hybrid_diffattn_s5_fox_deepnorm"

def layer_norm(x, g, b):
    xf = x.astype(jnp.float32)
    mu = jnp.mean(xf, axis=-1, keepdims=True)
    var = jnp.mean(jnp.square(xf - mu), axis=-1, keepdims=True)
    return ((xf - mu) * lax.rsqrt(var + LN_EPS) * g + b).astype(x.dtype)

def rope_tables(seq, dim):
    inv = ROPE_THETA ** (-jnp.arange(0, dim, 2, dtype=jnp.float32) / dim)
    ang = jnp.arange(seq, dtype=jnp.float32)[:, None] * inv[None, :]
    return jnp.cos(ang), jnp.sin(ang)

def apply_rope(x, cos, sin):
    x1, x2 = jnp.split(x, 2, axis=-1)
    c = cos[None, :, None, :].astype(x.dtype)
    s = sin[None, :, None, :].astype(x.dtype)
    return jnp.concatenate([x1 * c - x2 * s, x1 * s + x2 * c], axis=-1)

def diff_attention(q, k, v, lam):
    bsz, h, _, s, d = q.shape
    nb = s // Q_BLOCK
    scale = d ** -0.5
    k_chunk = jnp.arange(s) // CHUNK

    def block(i):
        q0 = i * Q_BLOCK
        qb = lax.dynamic_slice_in_dim(q, q0, Q_BLOCK, axis=3)
        logits = jnp.einsum('bhcqd,bhckd->bhcqk', qb, k).astype(jnp.float32) * scale
        q_chunk = (q0 + jnp.arange(Q_BLOCK)) // CHUNK
        mask = k_chunk[None, :] <= q_chunk[:, None]
        p = jax.nn.softmax(jnp.where(mask, logits, -jnp.inf), axis=-1)
        p_diff = p[:, :, 0] - lam * p[:, :, 1]
        return jnp.einsum('bhqk,bhkv->bhqv', p_diff.astype(v.dtype), v)

    out = lax.map(block, jnp.arange(nb))
    return out.transpose(1, 0, 3, 2, 4).reshape(bsz, s, h, v.shape[-1])

def s5_mixer(u, a_re, a_im, log_dt, b_re, b_im, c_re, c_im, d_skip, glu_w, glu_b):
    bsz, s, _ = u.shape
    f32 = jnp.float32
    uf = u.astype(f32)
    ug = uf.reshape(bsz, s, SSM_GROUPS, SSM_GROUP)
    a_re = a_re.astype(f32)
    a_im = a_im.astype(f32)
    dt = jnp.exp(log_dt.astype(f32))[:, None]
    mag = jnp.exp(a_re * dt)
    ab_re = mag * jnp.cos(a_im * dt)
    ab_im = mag * jnp.sin(a_im * dt)
    den = jnp.square(a_re) + jnp.square(a_im)
    nr = ab_re - 1.0
    ni = ab_im
    g_re = (nr * a_re + ni * a_im) / den
    g_im = (ni * a_re - nr * a_im) / den
    b_re = b_re.astype(f32)
    b_im = b_im.astype(f32)
    bb_re = g_re[..., None] * b_re - g_im[..., None] * b_im
    bb_im = g_re[..., None] * b_im + g_im[..., None] * b_re
    bu_re = jnp.einsum('bsgh,gph->bsgp', ug, bb_re)
    bu_im = jnp.einsum('bsgh,gph->bsgp', ug, bb_im)
    a_seq_re = jnp.broadcast_to(ab_re[None, None], (1, s, SSM_GROUPS, SSM_STATE))
    a_seq_im = jnp.broadcast_to(ab_im[None, None], (1, s, SSM_GROUPS, SSM_STATE))

    def combine(left, right):
        a1r, a1i, b1r, b1i = left
        a2r, a2i, b2r, b2i = right
        return (a2r * a1r - a2i * a1i,
                a2r * a1i + a2i * a1r,
                a2r * b1r - a2i * b1i + b2r,
                a2r * b1i + a2i * b1r + b2i)

    _, _, x_re, x_im = lax.associative_scan(combine, (a_seq_re, a_seq_im, bu_re, bu_im), axis=1)
    y = (jnp.einsum('bsgp,ghp->bsgh', x_re, c_re.astype(f32))
         - jnp.einsum('bsgp,ghp->bsgh', x_im, c_im.astype(f32)))
    y = y.reshape(bsz, s, SSM_WIDTH) + d_skip.astype(f32) * uf
    y = jax.nn.gelu(y)
    y = y * jax.nn.sigmoid(y @ glu_w.astype(f32) + glu_b.astype(f32))
    return y.astype(u.dtype)

def even_mixer(h, w_in, lam_vecs, subln_g, a_re, a_im, log_dt, b_re, b_im, c_re, c_im,
               d_skip, glu_w, glu_b, w_out, lam_init, cos, sin):
    bsz, s, _ = h.shape
    proj = h @ w_in
    q, k, v, u = jnp.split(proj, [DIFF_QK_WIDTH, 2 * DIFF_QK_WIDTH,
                                  2 * DIFF_QK_WIDTH + DIFF_WIDTH], axis=-1)
    q = apply_rope(q.reshape(bsz, s, 2 * DIFF_HEADS, DIFF_QK_DIM), cos, sin)
    k = apply_rope(k.reshape(bsz, s, 2 * DIFF_HEADS, DIFF_QK_DIM), cos, sin)
    q = q.reshape(bsz, s, DIFF_HEADS, 2, DIFF_QK_DIM).transpose(0, 2, 3, 1, 4)
    k = k.reshape(bsz, s, DIFF_HEADS, 2, DIFF_QK_DIM).transpose(0, 2, 3, 1, 4)
    v = v.reshape(bsz, s, DIFF_HEADS, DIFF_V_DIM).transpose(0, 2, 1, 3)
    lv = lam_vecs.astype(jnp.float32)
    lam = jnp.exp(jnp.sum(lv[0] * lv[1])) - jnp.exp(jnp.sum(lv[2] * lv[3])) + lam_init
    attn = diff_attention(q, k, v, lam).astype(jnp.float32)
    attn = attn * lax.rsqrt(jnp.mean(jnp.square(attn), axis=-1, keepdims=True) + RMS_EPS)
    attn = (attn * subln_g.astype(jnp.float32) * (1.0 - lam_init)).astype(h.dtype)
    y_ssm = s5_mixer(u, a_re, a_im, log_dt, b_re, b_im, c_re, c_im, d_skip, glu_w, glu_b)
    mixed = jnp.concatenate([attn.reshape(bsz, s, DIFF_WIDTH), y_ssm], axis=-1)
    return mixed @ w_out

def fox_attention(q, k, v, fcum):
    bsz, h, s, d = q.shape
    nb = s // Q_BLOCK
    scale = d ** -0.5
    k_pos = jnp.arange(s)

    def block(i):
        q0 = i * Q_BLOCK
        qb = lax.dynamic_slice_in_dim(q, q0, Q_BLOCK, axis=2)
        fq = lax.dynamic_slice_in_dim(fcum, q0, Q_BLOCK, axis=2)
        logits = (jnp.einsum('bhqd,bhkd->bhqk', qb, k).astype(jnp.float32) * scale
                  + fq[..., None] - fcum[:, :, None, :])
        q_pos = q0 + jnp.arange(Q_BLOCK)
        mask = k_pos[None, :] <= q_pos[:, None]
        p = jax.nn.softmax(jnp.where(mask, logits, -jnp.inf), axis=-1)
        return jnp.einsum('bhqk,bhkd->bhqd', p.astype(v.dtype), v)

    out = lax.map(block, jnp.arange(nb))
    return out.transpose(1, 0, 3, 2, 4).reshape(bsz, s, h * d)

def odd_mixer(h, w_in, b_f, w_out):
    bsz, s, _ = h.shape
    proj = h @ w_in
    q, k, v, f_logit = jnp.split(proj, [D_MODEL, 2 * D_MODEL, 3 * D_MODEL], axis=-1)
    q = q.reshape(bsz, s, FOX_HEADS, FOX_HEAD_DIM).transpose(0, 2, 1, 3)
    k = k.reshape(bsz, s, FOX_HEADS, FOX_HEAD_DIM).transpose(0, 2, 1, 3)
    v = v.reshape(bsz, s, FOX_HEADS, FOX_HEAD_DIM).transpose(0, 2, 1, 3)
    log_f = jax.nn.log_sigmoid(f_logit.astype(jnp.float32) + b_f.astype(jnp.float32))
    fcum = jnp.cumsum(log_f, axis=1).transpose(0, 2, 1)
    return fox_attention(q, k, v, fcum) @ w_out

def squared_relu_mlp(h, w1, w2):
    return jnp.square(jax.nn.relu(h @ w1)) @ w2

def setup_inputs(seed: int = 0) -> dict:
    key = jax.random.key(seed)
    ks = iter(jax.random.split(key, 32))
    f32 = jnp.float32
    D = D_MODEL
    E, O, L = N_EVEN, N_ODD, DEPTH

    def nrm(shape, scale):
        return jax.random.normal(next(ks), shape, f32) * scale

    x = nrm((BATCH, SEQ, D), 1.0)
    ab_w_in = nrm((E, D, EVEN_IN), D ** -0.5)
    ab_lambda = nrm((E, 4, DIFF_QK_DIM), 0.1)
    ab_subln_g = 1.0 + nrm((E, DIFF_HEADS, DIFF_V_DIM), 0.02)
    n_idx = jnp.arange(SSM_STATE, dtype=f32)
    ssm_a_re = -0.5 + nrm((E, SSM_GROUPS, SSM_STATE), 0.01)
    ssm_a_im = math.pi * n_idx + nrm((E, SSM_GROUPS, SSM_STATE), 0.01)
    ssm_log_dt = jax.random.uniform(next(ks), (E, SSM_GROUPS), f32,
                                    math.log(1e-3), math.log(1e-1))
    ssm_b_re = nrm((E, SSM_GROUPS, SSM_STATE, SSM_GROUP), (2 * SSM_GROUP) ** -0.5)
    ssm_b_im = nrm((E, SSM_GROUPS, SSM_STATE, SSM_GROUP), (2 * SSM_GROUP) ** -0.5)
    ssm_c_re = nrm((E, SSM_GROUPS, SSM_GROUP, SSM_STATE), SSM_STATE ** -0.5)
    ssm_c_im = nrm((E, SSM_GROUPS, SSM_GROUP, SSM_STATE), SSM_STATE ** -0.5)
    ssm_d = nrm((E, SSM_WIDTH), 1.0)
    ssm_glu_w = nrm((E, SSM_WIDTH, SSM_WIDTH), SSM_WIDTH ** -0.5)
    ssm_glu_b = nrm((E, SSM_WIDTH), 0.01)
    ab_w_out = nrm((E, D, D), DEEPNORM_BETA * D ** -0.5)
    fox_w_in = nrm((O, D, FOX_IN), D ** -0.5)
    fox_b_f = jax.random.uniform(next(ks), (O, FOX_HEADS), f32, 1.0, 5.0)
    fox_w_out = nrm((O, D, D), DEEPNORM_BETA * D ** -0.5)
    ln1_g = 1.0 + nrm((L, D), 0.02)
    ln1_b = nrm((L, D), 0.02)
    ffn_w1 = nrm((L, D, D_FF), D ** -0.5)
    ffn_w2 = nrm((L, D_FF, D), DEEPNORM_BETA * D_FF ** -0.5)
    ln2_g = 1.0 + nrm((L, D), 0.02)
    ln2_b = nrm((L, D), 0.02)
    return {"x": x, "ab_w_in": ab_w_in, "ab_lambda": ab_lambda, "ab_subln_g": ab_subln_g,
            "ssm_a_re": ssm_a_re, "ssm_a_im": ssm_a_im, "ssm_log_dt": ssm_log_dt,
            "ssm_b_re": ssm_b_re, "ssm_b_im": ssm_b_im, "ssm_c_re": ssm_c_re,
            "ssm_c_im": ssm_c_im, "ssm_d": ssm_d, "ssm_glu_w": ssm_glu_w,
            "ssm_glu_b": ssm_glu_b, "ab_w_out": ab_w_out, "fox_w_in": fox_w_in,
            "fox_b_f": fox_b_f, "fox_w_out": fox_w_out, "ln1_g": ln1_g, "ln1_b": ln1_b,
            "ffn_w1": ffn_w1, "ffn_w2": ffn_w2, "ln2_g": ln2_g, "ln2_b": ln2_b}

def reference(x, ab_w_in, ab_lambda, ab_subln_g, ssm_a_re, ssm_a_im, ssm_log_dt,
              ssm_b_re, ssm_b_im, ssm_c_re, ssm_c_im, ssm_d, ssm_glu_w, ssm_glu_b,
              ab_w_out, fox_w_in, fox_b_f, fox_w_out, ln1_g, ln1_b, ffn_w1, ffn_w2,
              ln2_g, ln2_b):
    seq = x.shape[1]
    cos, sin = rope_tables(seq, DIFF_QK_DIM)
    h = x
    for l in range(DEPTH):
        if l % 2 == 0:
            i = l // 2
            lam_init = 0.8 - 0.6 * math.exp(-0.3 * l)
            mix = even_mixer(h, ab_w_in[i], ab_lambda[i], ab_subln_g[i], ssm_a_re[i],
                             ssm_a_im[i], ssm_log_dt[i], ssm_b_re[i], ssm_b_im[i],
                             ssm_c_re[i], ssm_c_im[i], ssm_d[i], ssm_glu_w[i],
                             ssm_glu_b[i], ab_w_out[i], lam_init, cos, sin)
        else:
            i = l // 2
            mix = odd_mixer(h, fox_w_in[i], fox_b_f[i], fox_w_out[i])
        h = layer_norm(DEEPNORM_ALPHA * h + mix, ln1_g[l], ln1_b[l])
        h = layer_norm(DEEPNORM_ALPHA * h + squared_relu_mlp(h, ffn_w1[l], ffn_w2[l]),
                       ln2_g[l], ln2_b[l])
    return h


_drawn_inputs = setup_inputs


def setup_inputs(seed=0):
    import zlib

    import numpy as np

    out = dict(_drawn_inputs(seed))
    spreads = {}
    factors = {'ab_lambda': 2.984,
     'ab_subln_g': 78.598,
     'ssm_a_re': 64.0,
     'ssm_a_im': 57.056,
     'ssm_log_dt': 57.688,
     'ssm_b_re': 64.0,
     'ssm_b_im': 64.0,
     'ssm_c_re': 64.0,
     'ssm_c_im': 64.0,
     'ssm_glu_b': 200.0,
     'ssm_glu_w': 19.559,
     'ssm_d': 3.147}
    for name, (base, spread) in spreads.items():
        noise = np.random.default_rng([zlib.crc32(name.encode()), seed]).standard_normal(out[name].shape)
        drawn = base * np.exp(spread * noise) if base else spread * noise
        out[name] = __import__('jax').numpy.asarray(drawn.astype(out[name].dtype))
    for name, factor in factors.items():
        out[name] = (out[name] * factor).astype(out[name].dtype)
    return out
```

```python
import math
from contextlib import ExitStack

import numpy as np
import concourse.bass as bass
from concourse import mybir

F32 = mybir.dt.float32
F32R = mybir.dt.float32r
BF16 = mybir.dt.bfloat16
I32 = mybir.dt.int32
ALU = mybir.AluOpType
ACT = mybir.ActivationFunctionType
AX = mybir.AxisListType

P = 128
D = 1024
S = 512
KB = D // P
TT = S // P
D_FF = 4 * D
SLAB_K = 4
COLS = 512
HEADS_STAGE = 8
DH = 64
ALPHA = 4.0 ** 0.25
LN_EPS = 1e-5
RMS_EPS = 1e-6
LAM_INIT = 0.8 - 0.6 * math.exp(-0.3 * 0)
NEG = -1.0e30
GROUPS = 32
GCH = 16
NSTATE = 64
L = 8
NCH = S // L
GB = 8
NB = GROUPS // GB
M15 = 2 * L - 1

C_ID, C_SW64, C_SW32, C_TRI, C_MASK0, C_MASK1, C_CC, C_SS, C_SGN = 0, 128, 256, 384, 896, 1024, 1152, 1664, 2176
C_N = 2177
S_LNG, S_LNB, S_ARE, S_AIM, S_LDT, S_D, S_GLUB, S_BF = 0, 32, 64, 96, 128, 160, 164, 168
S_N = 184

SL_U, SL_Q, SL_K, SL_V, SL_GLU, SL_OUT0, SL_MLP0 = 0, 2, 4, 6, 8, 9, 13
SL_L1 = 45
SL_OUT1, SL_MLP1, SL_END = 57, 61, 93


def group_table():
    groups = []
    for s in (SL_U, SL_Q, SL_K, SL_V):
        groups.append([s, s + 1])
    groups.append([SL_GLU])
    groups += [[SL_OUT0, SL_OUT0 + 1], [SL_OUT0 + 2, SL_OUT0 + 3]]
    for c in range(8):
        n = SL_MLP0 + 4 * c
        groups += [[n, n + 1], [n + 2], [n + 3]]
    for s in range(SL_L1, SL_OUT1, 2):
        groups.append([s, s + 1])
    groups += [[SL_OUT1, SL_OUT1 + 1], [SL_OUT1 + 2, SL_OUT1 + 3]]
    for c in range(8):
        n = SL_MLP1 + 4 * c
        groups += [[n, n + 1], [n + 2], [n + 3]]
    slab_event, bank_event, e = {}, {}, 0
    for g, slabs in enumerate(groups):
        if len(slabs) == 2:
            e += 1
            slab_event[slabs[0]] = e
        for t in range(4):
            e += 1
            bank_event[g, t] = e
        slab_event[slabs[-1]] = e
    return groups, slab_event, bank_event


GROUP_SLABS, SLAB_EVENT, BANK_EVENT = group_table()
G_U, G_Q, G_K, G_V, G_GLU, G_OUT0, G_MLP0, G_L1, G_OUT1, G_MLP1 = 0, 1, 2, 3, 4, 5, 7, 31, 37, 39
EVAC_DVE_LN = [8, 72, 80, 144]
CHUNK_EVENTS = 13


def wait(eng, sem, value, r=0, per=0):
    if isinstance(r, int):
        if value + per * r > 0:
            eng.wait_ge(sem, value + per * r)
    else:
        eng.wait_ge(sem, r * per + value)


def trunk(nc, t):
    with ExitStack() as ctx:
        def sb(name, shape, dt=F32):
            return ctx.enter_context(nc.sbuf_tensor(name, shape, dt))

        def sem(name):
            return ctx.enter_context(nc.semaphore(name))

        slab_raw = sb("slab_raw", [P, 2, SLAB_K, COLS])
        slab_hi = sb("slab_hi", [P, 2, SLAB_K, COLS], F32R)
        slab_lo = sb("slab_lo", [P, 2, SLAB_K, COLS], F32R)
        act_hi = sb("act_hi", [P, KB, S], F32R)
        act_lo = sb("act_lo", [P, KB, S], F32R)
        hid_hi = sb("hid_hi", [P, 4, S], F32R)
        hid_lo = sb("hid_lo", [P, 4, S], F32R)
        resid = sb("resid", [P, TT, D])
        acc = sb("acc", [P, TT, D])
        const = sb("const", [P, C_MASK0])
        consth = sb("consth", [P, 3, P], BF16)
        sgn = sb("sgn", [P, 1])
        small = sb("small", [P, S_N])
        stats = sb("stats", [P, TT, 12])
        mv = sb("mv", [P, TT, 2])
        lns = sb("lns", [P, 5, TT])
        gw_hi = sb("gw_hi", [P, KB, 16], F32R)
        gw_lo = sb("gw_lo", [P, KB, 16], F32R)
        arena = sb("arena", [P, 17920])

        def view(off, *shape):
            n = int(np.prod(shape))
            assert off + n <= 17920
            v = arena[:, off:off + n]
            if len(shape) == 2:
                return v.rearrange("p (a b) -> p a b", a=shape[0])
            if len(shape) == 3:
                return v.rearrange("p (a b c) -> p a b c", a=shape[0], b=shape[1])
            return v

        ident = const[:, C_ID:C_ID + P]
        swap64 = const[:, C_SW64:C_SW64 + P]
        swap32 = const[:, C_SW32:C_SW32 + P]
        tri = const[:, C_TRI:C_TRI + S]
        ident_h, mask_h = consth[:, 0, :], [consth[:, 1, :], consth[:, 2, :]]

        q_all = view(0, 8, S)
        k_all = view(4096, 8, S)
        e_buf = view(8192, 4, S)
        pt_buf = view(10240, 2, S)
        q_slot = view(11264, 2, S)
        o_stage = view(12288, TT, P)
        sub_g = view(12800, S)
        neg_max = view(13312, 16)
        z_sum = view(13328, 16)
        z_rec = view(13344, 16)
        coef = view(13360, 16)
        lam = view(13376, 8)
        rms = view(13384, 5, TT)
        lam_in = view(13440, 4, DH)
        lam_pr = view(13696, 2, DH)
        sq_scr = sb("sq_scr", [P, P])
        logf = view(13824, 4, TT, 16)
        fcum = view(14080, 2, S)
        gate_w = view(15104, KB, 16)
        ln_row = view(15232, 2, D)
        rot_x = acc[:, 2:4, :].rearrange("p a (b n) -> p (a b) n", n=S)
        rot_t = view(8192, 2, S)
        rot_c = view(10240, 2, S)
        consth_f = view(12288, 2, P)
        v_nat = acc[:, 0:2, :].rearrange("p a (b n) -> p (a b) n", n=COLS)
        tmp_a = view(8192, 2, S)
        tmp_b = view(9216, 2, S)

        banks = [ctx.enter_context(nc.psum_tensor(f"bank{i}", [P, 512], F32)) for i in range(8)]

        def norm_bank(k):
            return banks[(k + 4) % 8]

        def bank_set(g):
            return banks[4 * (g % 2):4 * (g % 2) + 4]

        slab_landed = [sem(f"slab_landed{i}") for i in range(2)]
        slab_hi_ready = sem("slab_hi_ready")
        slab_lo_ready = sem("slab_lo_ready")
        pe_event = sem("pe_event")
        const_in, small_in, x_in = sem("const_in"), sem("small_in"), sem("x_in")
        xt_in = [sem(f"xt_in{i}") for i in range(2)]
        y_in = [sem(f"y_in{i}") for i in range(NB)]
        consth_ready = sem("consth_ready")
        evac_act = sem("evac_act")
        evac_dve = sem("evac_dve")
        act_hi_done = sem("act_hi_done")
        act_ready = sem("act_ready")
        relu_done = sem("relu_done")
        hid_hi_done = sem("hid_hi_done")
        sq_done = sem("sq_done")
        hid_ready = sem("hid_ready")
        dve_step = sem("dve_step")
        act_step = sem("act_step")
        pool_step = sem("pool_step")
        ln_var = sem("ln_var")
        ln_seed = sem("ln_seed")
        xhat_ready = sem("xhat_ready")
        ln_psum = sem("ln_psum")
        ln_full = sem("ln_full")
        ln_split = sem("ln_split")
        row_in = sem("row_in")
        acc_init = sem("acc_init")
        resid_ready = sem("resid_ready")
        out_ready = sem("out_ready")
        out_done = sem("out_done")
        rot_copied, rot_swapped, rot_done = sem("rot_copied"), sem("rot_swapped"), sem("rot_done")
        at_q, at_s, at_m, at_e, at_p, at_t, at_c, at_v, at_z, at_o, at_sq, at_n, at_x = (
            sem("at_" + n) for n in ("q", "s", "m", "e", "p", "t", "c", "v", "z", "o", "sq", "n", "x"))
        at_nv = sem("at_nv")
        at_ns = sem("at_ns")
        at_w = sem("at_w")
        lam_dma, lam_sum, lam_exp, lam_done, subg_in = (
            sem("lam_dma"), sem("lam_sum"), sem("lam_exp"), sem("lam_done"), sem("subg_in"))
        rope_in = sem("rope_in")
        gate_in, gate_mm, gate_z, gate_log, gate_cum, gate_row = (
            sem("gate_in"), sem("gate_mm"), sem("gate_z"), sem("gate_log"), sem("gate_cum"), sem("gate_row"))
        decay_in, ones_set = sem("decay_in"), sem("ones_set")
        gate_w_split, gate_w_hi = sem("gate_w_split"), sem("gate_w_hi")
        evac_q1, evac_k1 = sem("evac_q1"), sem("evac_k1")
        fx_q, fx_s, fx_m, fx_e, fx_t, fx_c, fx_v, fx_o, fx_x, fx_h = (sem("fx_" + n) for n in "qsmetcvoxh")

        xt = acc[:, :, :].rearrange("p a (b n) -> p (a b) n", n=S)
        u_t = view(13824, 4, S)
        b_ri, b_ir = view(15872, GROUPS, GCH), view(16384, GROUPS, GCH)
        c_ri, c_ir = view(16896, GROUPS, GCH), view(17408, GROUPS, GCH)
        f_tab = view(0, GB, M15, GCH)
        t_mat = view(1920, GB, P)
        bst_mat = view(2944, GB, P)
        ca_mat = view(3968, GB, L, GCH)
        e_cos, e_sin, r_tab = view(4992, GB, NCH), view(5504, GB, NCH), view(6016, GB, NCH)
        s_buf, y_buf, x_buf = view(6528, GB, NCH), view(7040, GB, NCH), view(7552, GB, NCH)
        prod1, prod2 = view(8064, GB, L, GCH), view(9088, GB, L, GCH)
        u8 = view(10112, GROUPS, NCH)
        y8 = view(12160, GB, NCH)
        prev_r, prev_i = view(12672, GROUPS, L), view(12928, GROUPS, L)
        slot = view(13184, 20, GROUPS)
        slot_i = arena[:, 13184 + 19 * 32:13184 + 20 * 32].bitcast(I32)
        accf = acc[:, :, :].rearrange("p a n -> p (a n)")
        bb1 = accf[:, 0:512].rearrange("p (g h) -> p g h", g=GROUPS)
        bb2 = accf[:, 512:1024].rearrange("p (g h) -> p g h", g=GROUPS)
        pow_r = accf[:, 1024:1312].rearrange("p (g e) -> p g e", g=GROUPS)
        pow_i = accf[:, 1312:1600].rearrange("p (g e) -> p g e", g=GROUPS)
        phase = accf[:, 1600:1984].rearrange("p (e g) -> p e g", g=GROUPS)
        y_t = accf[:, 2048:4096].rearrange("p (b n) -> p b n", b=4)
        ssm_in, u_ready, u8_in, ss_sin_in, ss_sin, ss_f, ss_t, ss_tc, ss_s, ss_sc, ss_sw, ss_y, ss_x, ss_yw, ss_out = (
            sem("ss_" + n) for n in ("in", "u", "u8", "sini", "sin", "f", "t", "tc", "s", "sc", "sw", "y", "x", "yw", "out"))
        ss_scan, ss_out_t = sem("ss_scan"), sem("ss_out_t")
        glu_in, glu_y, glu_hi, glu_rhs, glu_sig, glu_full, glu_act = (
            sem("glu_" + n) for n in ("in", "y", "hi", "rhs", "sig", "full", "act"))
        stem_hi, u_out, y_out = sem("stem_hi"), sem("u_out"), sem("y_out")

        block = ctx.enter_context(nc.Block())

        def w_src(w, kh, c0):
            return w.rearrange("(k p) n -> p k n", p=P)[:, kh * SLAB_K:(kh + 1) * SLAB_K, c0:c0 + COLS]

        def slab_source(n):
            if n < SL_GLU:
                col = {SL_U: 3, SL_Q: 0, SL_K: 1, SL_V: 2}[n - n % 2]
                return w_src(t["ab_w_in"], n % 2, col * COLS)
            if n == SL_GLU:
                return w_src(t["ssm_glu_w"], 0, 0)
            if n < SL_MLP0:
                j = n - SL_OUT0
                return w_src(t["ab_w_out"], j % 2, (j // 2) * COLS)
            if n < SL_OUT1:
                j = n - SL_L1
                half, part, kh = j // 6, (j % 6) // 2, j % 2
                return w_src(t["fox_w_in"], kh, part * D + half * COLS)
            j = n - SL_OUT1
            return w_src(t["fox_w_out"], j % 2, (j // 2) * COLS)

        def ssm_sp(sp):
            sp.wait_ge(u_ready, 4)
            sp.dma_start(t["u_scratch"].rearrange("(b p) n -> p b n", p=P), u_t[:, :, :]).then_inc(u_out, 16)
            sp.wait_ge(act_ready, 12)
            sp.wait_ge(u_out, 16)
            for j in range(L):
                src = t["u_scratch"].rearrange("(g h) n -> h g n", h=GCH)[:, :, j * NCH:(j + 1) * NCH]
                sp.dma_start(u8[j * GCH:(j + 1) * GCH, :, :], src).then_inc(u8_in, 16)
            for b in range(NB):
                sp.wait_ge(ss_out, b + 1)
                sp.dma_start(t["y_scratch"][b], y8[:, :, :].rearrange("p g c -> p (g c)")).then_inc(y_out, 16)
                sp.wait_ge(y_out, 16 * (b + 1))
                for g in range(GB):
                    src = t["y_scratch"][b].rearrange("(i h) (g c) -> h i g c", h=GCH, g=GB)[:, :, g, :]
                    dst = y_t[g * GCH:(g + 1) * GCH, b, :].rearrange("h (i c) -> h i c", i=L)
                    sp.dma_start(dst, src).then_inc(y_in[b], 16)

        @block.sync
        def _(sp):
            def slab(n, src, r=0, per=0):
                wait(sp, slab_hi_ready, n - 1, r, per)
                wait(sp, slab_lo_ready, n - 1, r, per)
                sp.dma_start(slab_raw[:, n % 2, :, :], src).then_inc(slab_landed[n % 2], 16)

            def mlp_slabs(l, n0, r):
                w1, w2 = t["ffn_w1"][l], t["ffn_w2"][l]
                for c in range(2):
                    for kh in range(2):
                        cols = bass.ds(r * (2 * COLS) + c * COLS, COLS)
                        src = w1.rearrange("(k p) n -> p k n", p=P)[:, kh * SLAB_K:(kh + 1) * SLAB_K, cols]
                        slab(n0 + 4 * c + kh, src, r, 8)
                    for g in range(2):
                        rows = bass.ds(r * (2 * SLAB_K) + c * SLAB_K, SLAB_K)
                        src = w2.rearrange("(k p) n -> p k n", p=P)[:, rows, g * COLS:(g + 1) * COLS]
                        slab(n0 + 4 * c + 2 + g, src, r, 8)

            for kb in range(2):
                sp.dma_start(xt[:, 4 * kb:4 * kb + 4, :], t["xt"][:, 4 * kb:4 * kb + 4, :]).then_inc(xt_in[kb], 16)
                slab(kb, slab_source(kb))
            sp.dma_start(const[:, :], t["const"][:, 0:C_MASK0]).then_inc(const_in, 16)
            sp.dma_start(small[:, :], t["small"]).then_inc(small_in, 16)
            sp.dma_start(sgn[:, :], t["const"][:, C_SGN:C_SGN + 1], allow_slow_non_contiguous=True).then_inc(const_in, 16)
            slab(2, slab_source(2))
            slab(3, slab_source(3))
            sp.dma_start(consth_f, t["const"][:, C_MASK0:C_CC]).then_inc(const_in, 16)
            sp.dma_start(rot_c[:, :, :], t["const"][:, C_CC:C_SGN].rearrange("p (a n) -> p a n", a=2)).then_inc(rope_in, 16)
            sp.dma_start(sub_g[:, :], t["ab_subln_g"].rearrange("a h v -> a (h v)").broadcast_to([P, S])).then_inc(subg_in, 16)
            sp.dma_start(lam_in[:, :, :], t["ab_lambda"].broadcast_to([P, 4, DH])).then_inc(lam_dma, 16)
            sp.dma_start(resid[:, :, :], t["x"][0].rearrange("(a p) n -> p a n", p=P)).then_inc(x_in, 16)
            for n in range(4, SL_OUT0 + 1):
                slab(n, slab_source(n))
            sp.dma_start(view(15872, 4, GROUPS * GCH), t["ssm_bc"]).then_inc(ssm_in, 16)
            ssm_sp(sp)
            for n in range(SL_OUT0 + 1, SL_OUT0 + 3):
                slab(n, slab_source(n))
            slab(SL_OUT0 + 3, slab_source(SL_OUT0 + 3))
            with sp.Fori(0, 4) as r:
                mlp_slabs(0, SL_MLP0, r)
            slab(SL_L1, slab_source(SL_L1))
            slab(SL_L1 + 1, slab_source(SL_L1 + 1))
            sp.dma_start(gate_w[:, :, :], t["fox_w_in"].rearrange("(k p) n -> p k n", p=P)[:, :, 3 * D:3 * D + 16]).then_inc(gate_in, 16)

            def decay_rows(half):
                hs = slice(8 * half, 8 * half + 8)
                sp.dma_start(q_all[DH:DH + 1, :, :], fcum[hs, 0, :]).then_inc(decay_in, 16)
                sp.dma_start(k_all[DH + 1:DH + 2, :, :], fcum[hs, 1, :]).then_inc(decay_in, 16)

            sp.wait_ge(ones_set, 2)
            sp.wait_ge(gate_cum, 2)
            decay_rows(0)
            for n in range(SL_L1 + 2, SL_L1 + 8):
                slab(n, slab_source(n))
            sp.wait_ge(fx_s, 32)
            decay_rows(1)
            for n in range(SL_L1 + 8, SL_MLP1):
                slab(n, slab_source(n))
            with sp.Fori(0, 3) as r:
                mlp_slabs(1, SL_MLP1, r)
            mlp_slabs(1, SL_MLP1, 3)
            for i in range(TT):
                sp.wait_ge(out_ready, i + 1)
                sp.dma_start(t["out"][i * P:(i + 1) * P, :], acc[:, i, :]).then_inc(out_done, 16)
            sp.wait_ge(out_done, 16 * TT)

        @block.tensor
        def _(pe):
            mm = nc.tensor.matmul

            def three(out, a_hi, a_lo, b_hi, b_lo, first, last):
                mm(out, a_hi, b_hi, start=first, stop=False)
                mm(out, a_hi, b_lo, start=False, stop=False)
                return mm(out, a_lo, b_hi, start=False, stop=last)

            def slab_wait(n, r=0):
                wait(pe, slab_hi_ready, n + 1, r, 8)
                wait(pe, slab_lo_ready, n + 1, r, 8)

            def weights_left(g, n, kh, nk, r=0, a=None, out_set=None):
                slab_wait(n, r)
                a_hi, a_lo = a or (act_hi, act_lo)
                for c in range(4):
                    for k in range(SLAB_K):
                        cs = slice(c * P, (c + 1) * P)
                        ins = three(bank_set(g)[c][:, :], slab_hi[:, n % 2, k, cs], slab_lo[:, n % 2, k, cs],
                                    a_hi[:, kh * SLAB_K + k, :], a_lo[:, kh * SLAB_K + k, :],
                                    kh == 0 and k == 0, kh == nk - 1 and k == SLAB_K - 1)
                    if kh == nk - 1:
                        ins.then_inc(pe_event, 1)
                if kh < nk - 1:
                    ins.then_inc(pe_event, 1)

            def weights_right(g, n, kh, nk, a, base, r=0):
                slab_wait(n, r)
                a_hi, a_lo = a
                for tt in range(TT):
                    for k in range(SLAB_K):
                        ts = slice(tt * P, (tt + 1) * P)
                        ins = three(bank_set(g)[tt][:, :], a_hi[:, base + k, ts], a_lo[:, base + k, ts],
                                    slab_hi[:, n % 2, k, :], slab_lo[:, n % 2, k, :],
                                    kh == 0 and k == 0, kh == nk - 1 and k == SLAB_K - 1)
                    if kh == nk - 1:
                        ins.then_inc(pe_event, 1)
                if kh < nk - 1:
                    ins.then_inc(pe_event, 1)

            def swap_rotary(g, j):
                for c in range(4):
                    pe.wait_ge(rot_copied, 4 * j + c + 1)
                    mm(bank_set(g)[c][:, :], swap32, rot_x[:, c, :], start=True, stop=True).then_inc(rot_swapped, 1)

            act = (act_hi, act_lo)
            for kh in range(2):
                pe.wait_ge(act_ready, 4 * kh + 4)
                weights_left(G_U, SL_U + kh, kh, 2)
            weights_left(G_Q, SL_Q, 0, 2)
            weights_left(G_Q, SL_Q + 1, 1, 2)
            pe.wait_ge(u_ready, 4)
            weights_left(G_K, SL_K, 0, 2)
            pe.wait_ge(const_in, 48)
            swap_rotary(G_Q, 0)
            weights_left(G_K, SL_K + 1, 1, 2)
            pe.wait_ge(rot_done, 4)
            weights_right(G_V, SL_V, 0, 2, act, 0)
            swap_rotary(G_K, 1)
            weights_right(G_V, SL_V + 1, 1, 2, act, SLAB_K)

            def scores(j, out, qs, ks, i, layer):
                n = P * (i + 1)
                mm(out[:, n - P:n], ident_h, mask_h[layer], start=True, stop=False, skip_group_check=True)
                return mm(out[:, 0:n], qs, ks, start=False, stop=True, skip_group_check=True)

            def diff_head(r):
                def S_(i):
                    wait(pe, at_q, 2, r, 2)
                    if i < 2:
                        wait(pe, at_e, 0, r, 8)
                    else:
                        wait(pe, at_e, 2 * (i - 1), r, 8)
                    n = P * (i + 1)
                    for m in range(2):
                        ks = k_all[0:DH, bass.ds(r * 2 + m, 1), 0:n].rearrange("p a n -> p (a n)")
                        ins = scores(i, banks[2 * (i % 2) + m], q_slot[0:DH, m, i * P:(i + 1) * P], ks, i, 0)
                    ins.then_inc(at_s, 1)

                def T_(i):
                    wait(pe, at_p, i + 1, r, 4)
                    wait(pe, at_c, i - 1 if i >= 2 else 0, r, 4)
                    for j in range(i + 1):
                        ins = nc.tensor.transpose(banks[4 + i % 2][:, j * P:(j + 1) * P],
                                                  e_buf[:, 2 * (i % 2), j * P:(j + 1) * P], ident)
                    ins.then_inc(at_t, 1)

                def V_(i):
                    wait(pe, at_c, i + 1, r, 4)
                    wait(pe, at_o, i, r, 4)
                    for j in range(i + 1):
                        vs = v_nat[:, j, bass.ds(r * P, P)]
                        ins = mm(banks[6][:, 0:P], pt_buf[:, i % 2, j * P:(j + 1) * P], vs,
                                 start=(j == 0), stop=(j == i))
                    ins.then_inc(at_v, 1)

                S_(0)
                S_(1)
                for i in range(TT):
                    T_(i)
                    if i + 2 < TT:
                        S_(i + 2)
                    if i:
                        V_(i - 1)
                V_(TT - 1)
                wait(pe, at_n, TT, r, TT)
                wait(pe, act_ready, 8, r, 1)
                for i in range(TT):
                    ins = nc.tensor.transpose(banks[7][:, i * P:(i + 1) * P], o_stage[:, i, :], ident)
                ins.then_inc(at_x, 1)

            pe.wait_ge(evac_act, 4)
            pe.wait_ge(rot_done, 8)
            pe.wait_ge(consth_ready, 3)
            diff_head(0)
            with pe.Fori(1, 4) as r:
                diff_head(r)

            def ssm_batch(r):
                wait(pe, ss_f, 1, r, 1)
                wait(pe, ss_tc, 0, r, 1)
                for g in range(GB):
                    c1 = c_ri[:, bass.ds(r * GB + g, 1), :].rearrange("p a h -> p (a h)")
                    for i in range(L):
                        lhs = f_tab[:, g, L - 1 - i:2 * L - 1 - i, :].rearrange("p j h -> p (j h)")
                        col = (g % 4) * P + i * GCH
                        ins = mm(banks[g // 4][:, col:col + GCH], lhs, c1, start=True, stop=True)
                ins.then_inc(ss_t, 1)
                for g in range(GB):
                    ins = nc.tensor.transpose(banks[2 + g // 4][:, (g % 4) * P:(g % 4 + 1) * P],
                                              f_tab[:, g, 0:L, :].rearrange("p j h -> p (j h)"), ident)
                ins.then_inc(ss_t, 1)
                wait(pe, ss_tc, 1, r, 1)
                wait(pe, ss_sc, 0, r, 1)
                for g in range(GB):
                    us = u8[:, bass.ds(r * GB + g, 1), :].rearrange("p a c -> p (a c)")
                    ins = mm(banks[4][:, g * NCH:(g + 1) * NCH], bst_mat[:, g, :], us, start=True, stop=True)
                ins.then_inc(ss_s, 1)
                wait(pe, ss_sc, 1, r, 1)
                mm(banks[5][:, :], swap64, s_buf[:, :, :].rearrange("p g c -> p (g c)"),
                   start=True, stop=True).then_inc(ss_sw, 1)
                wait(pe, ss_scan, 1, r, 1)
                mm(banks[6][:, :], swap64, y_buf[:, :, :].rearrange("p g c -> p (g c)"),
                   start=True, stop=True).then_inc(ss_yw, 1)
                wait(pe, ss_x, 1, r, 1)
                wait(pe, ss_out, 0, r, 1)
                for g in range(GB):
                    us = u8[:, bass.ds(r * GB + g, 1), :].rearrange("p a c -> p (a c)")
                    out = banks[7][:, g * NCH:(g + 1) * NCH]
                    mm(out, t_mat[:, g, :], us, start=True, stop=False)
                    ins = mm(out, ca_mat[:, g, :, :].rearrange("p i h -> p (i h)"), x_buf[:, g, :], start=False, stop=True)
                ins.then_inc(ss_y, 1)

            pe.wait_ge(act_ready, 12)
            pe.wait_ge(u8_in, 16 * L)
            ssm_batch(0)
            with pe.Fori(1, 4) as r:
                ssm_batch(r)

            pe.wait_ge(glu_rhs, 4)
            weights_left(G_GLU, SL_GLU, 0, 1, a=(hid_hi, hid_lo))

            def out_projection(g0, n0, lo, hi, ready):
                pe.wait_ge(act_ready, ready)
                for h in range(2):
                    weights_right(g0 + h, n0 + 2 * h, 0, 2, lo, 0)
                    weights_right(g0 + h, n0 + 2 * h + 1, 1, 2, hi, SLAB_K)

            out_projection(G_OUT0, SL_OUT0, act, act, 16)

            def norm_transposes(l):
                pe.wait_ge(evac_dve, EVAC_DVE_LN[l])
                for i in range(TT):
                    pe.wait_ge(xhat_ready, 4 * l + i + 1)
                    for k in range(KB):
                        ins = nc.tensor.transpose(norm_bank(k)[:, i * P:(i + 1) * P],
                                                  resid[:, i, k * P:(k + 1) * P], ident)
                        if i == TT - 1:
                            ins.then_inc(ln_psum, 1)

            def mlp(g0, n0, r, d0, h0, ready):
                for c in range(2):
                    g, n, rr = g0 + 3 * c, n0 + 4 * c, r
                    dv = d0 + 8 * c
                    wait(pe, evac_dve, dv - 4, rr, 16)
                    for kh in range(2):
                        if isinstance(r, int) and r == 0 and c == 0:
                            pe.wait_ge(act_ready, ready + 4 * kh)
                        weights_left(g, n + kh, kh, 2, rr)
                    wait(pe, evac_dve, dv, rr, 16)
                    slab_wait(n + 2, rr)
                    for half in range(2):
                        if half:
                            wait(pe, relu_done, h0 + 4 * c + 4, rr, 8)
                            slab_wait(n + 3, rr)
                        for k in range(SLAB_K):
                            if half == 0:
                                wait(pe, hid_ready, h0 + 4 * c + k + 1, rr, 8)
                            for tt in range(TT):
                                ts = slice(tt * P, (tt + 1) * P)
                                ins = three(bank_set(g + 1 + half)[tt][:, :], hid_hi[:, k, ts], hid_lo[:, k, ts],
                                            slab_hi[:, (n + 2 + half) % 2, k, :], slab_lo[:, (n + 2 + half) % 2, k, :],
                                            k == 0, k == SLAB_K - 1)
                                if k == SLAB_K - 1:
                                    ins.then_inc(pe_event, 1)

            norm_transposes(0)
            mlp(G_MLP0, SL_MLP0, 0, 8, 0, 20)
            with pe.Fori(1, 4) as r:
                mlp(G_MLP0, SL_MLP0, r, 8, 0, 20)
            norm_transposes(1)

            def fox_pair_pe(pe, half, r):
                u0 = 32 * half

                def S_(j):
                    hh, i = j // TT, j % TT
                    wait(pe, fx_q, 8 * half + hh + 1, r, 2)
                    wait(pe, fx_e, u0 + (j - 1 if j >= 2 else 0), r, 8)
                    ks = k_all[0:DH + 2, bass.ds(r * 2 + hh, 1), 0:P * (i + 1)].rearrange("p a n -> p (a n)")
                    scores(j, banks[j % 2], q_slot[0:DH + 2, hh, i * P:(i + 1) * P], ks, i, 1).then_inc(fx_s, 1)

                def T_(j):
                    wait(pe, fx_e, u0 + j + 1, r, 8)
                    wait(pe, fx_c, u0 + (j - 1 if j >= 2 else 0), r, 8)
                    for b in range(j % TT + 1):
                        ins = nc.tensor.transpose(banks[2 + j % 2][:, b * P:(b + 1) * P],
                                                  e_buf[:, j % 4, b * P:(b + 1) * P], ident)
                    ins.then_inc(fx_t, 1)

                def V_(j):
                    wait(pe, fx_c, u0 + j + 1, r, 8)
                    wait(pe, fx_o, u0 + (j - 1 if j >= 2 else 0), r, 8)
                    for b in range(j % TT + 1):
                        vs = v_nat[:, b, bass.ds(r * P + (j // TT) * DH, DH)]
                        ins = mm(banks[4 + j % 2][:, 0:DH], pt_buf[:, j % 2, b * P:(b + 1) * P], vs,
                                 start=(b == 0), stop=(b == j % TT))
                    ins.then_inc(fx_v, 1)

                S_(0)
                S_(1)
                for j in range(8):
                    T_(j)
                    if j + 2 < 8:
                        S_(j + 2)
                    if j:
                        V_(j - 1)
                V_(7)
                wait(pe, fx_o, u0 + 8, r, 8)
                wait(pe, act_ready, 32 + 4 * half, r, 1)
                for i in range(TT):
                    ins = nc.tensor.transpose(banks[6][:, i * P:(i + 1) * P], o_stage[:, i, :], ident)
                ins.then_inc(fx_x, 1)

            def decay_gate():
                pe.wait_ge(gate_in, 16)
                pe.wait_ge(gate_w_split, 2)
                pe.wait_ge(act_ready, 32)
                for i in range(TT):
                    ts = slice(i * P, (i + 1) * P)
                    for k in range(KB):
                        ins = three(banks[0][:, i * 16:(i + 1) * 16], act_hi[:, k, ts], act_lo[:, k, ts],
                                    gw_hi[:, k, :], gw_lo[:, k, :], k == 0, k == KB - 1)
                ins.then_inc(gate_mm, 1)
                pe.wait_ge(gate_log, 1)
                for i in range(TT):
                    ins = mm(banks[1][0:16, i * P:S], logf[:, 3, i, :], tri[:, 0:S - i * P],
                             start=(i == 0), stop=(i == TT - 1), skip_group_check=True)
                ins.then_inc(gate_mm, 1)
                pe.wait_ge(gate_cum, 2)

            decay_gate()
            for half in range(2):
                n0, g0 = SL_L1 + 6 * half, G_L1 + 3 * half
                if half:
                    pe.wait_ge(act_ready, 36)
                weights_left(g0, n0, 0, 2)
                weights_left(g0, n0 + 1, 1, 2)
                weights_left(g0 + 1, n0 + 2, 0, 2)
                weights_left(g0 + 1, n0 + 3, 1, 2)
                pe.wait_ge(evac_q1, 4 * half + 4)
                weights_right(g0 + 2, n0 + 4, 0, 2, act, 0)
                weights_right(g0 + 2, n0 + 5, 1, 2, act, SLAB_K)
                pe.wait_ge(evac_act, 4 + 4 * half + 4)
                pe.wait_ge(evac_k1, 4 * half + 4)
                fox_pair_pe(pe, half, 0)
                with pe.Fori(1, 4) as r:
                    fox_pair_pe(pe, half, r)
            out_projection(G_OUT1, SL_OUT1, (hid_hi, hid_lo), act, 40)
            norm_transposes(2)
            mlp(G_MLP1, SL_MLP1, 0, EVAC_DVE_LN[2], 32, 44)
            with pe.Fori(1, 4) as r:
                mlp(G_MLP1, SL_MLP1, r, EVAC_DVE_LN[2], 32, 44)

        class Steps:

            def __init__(self, eng, sem_):
                self.eng, self.sem, self.count, self.r, self.per = eng, sem_, 0, 0, 0

            def step(self, ins):
                self.count += 1
                ins.then_inc(self.sem, 1)

            def settle(self):
                wait(self.eng, self.sem, self.count, self.r, self.per)

            def loop(self, n, body):
                start = self.count
                body(0)
                self.per = self.count - start
                with self.eng.Fori(1, n) as r:
                    self.count, self.r = start, r
                    body(r)
                self.count, self.r, self.per = start + n * self.per, 0, 0

        @block.vector
        def _(dve):
            st = Steps(dve, dve_step)
            tt_, ts_, stt = nc.vector.tensor_tensor, nc.vector.tensor_scalar, nc.vector.scalar_tensor_tensor

            def split(n, r=0):
                wait(dve, slab_hi_ready, n + 1, r, 8)
                tt_(slab_lo[:, n % 2, :, :], slab_raw[:, n % 2, :, :], slab_hi[:, n % 2, :, :].bitcast(F32),
                    ALU.subtract).then_inc(slab_lo_ready, 1)

            for kb in range(2):
                ks = slice(4 * kb, 4 * kb + 4)
                dve.wait_ge(stem_hi, kb + 1)
                tt_(act_lo[:, ks, :], xt[:, ks, :], act_hi[:, ks, :].bitcast(F32), ALU.subtract).then_inc(act_ready, 4)
                split(kb)
            dve.wait_ge(const_in, 48)
            nc.vector.tensor_copy(ident_h, ident).then_inc(consth_ready, 1)
            for m in range(2):
                nc.vector.tensor_copy(mask_h[m], consth_f[:, m, :]).then_inc(consth_ready, 1)

            dve.wait_ge(lam_dma, 16)
            pairs = lam_in[:, :, :].rearrange("p (a b) d -> p a b d", b=2)
            st.step(tt_(lam_pr[:, :, :], pairs[:, :, 0, :], pairs[:, :, 1, :], ALU.mult))
            st.settle()
            nc.vector.tensor_reduce(lam[:, 0:2], lam_pr[:, :, :], AX.X, ALU.add).then_inc(lam_sum, 1)
            dve.wait_ge(lam_exp, 1)
            st.step(tt_(lam[:, 4:5], lam[:, 3:4], lam[:, 2:3], ALU.subtract))
            st.settle()
            st.step(ts_(lam[:, 5:6], lam[:, 4:5], -LAM_INIT, None, ALU.add))
            dve.wait_ge(subg_in, 16)
            st.step(ts_(sub_g[:, :], sub_g[:, :], 1.0 - LAM_INIT, None, ALU.mult))

            def rotary(g, j, dst):
                dve.wait_ge(rope_in, 16)
                for c in range(4):
                    dve.wait_ge(rot_swapped, 4 * j + c + 1)
                    st.step(tt_(rot_t[:, 0, :], rot_x[:, c, :], rot_c[:, 0, :], ALU.mult))
                    st.step(tt_(rot_t[:, 1, :], bank_set(g)[c][:, :], rot_c[:, 1, :], ALU.mult))
                    st.settle()
                    st.step(tt_(dst[0:DH, 2 * c, :], rot_t[0:DH, 0, :], rot_t[0:DH, 1, :], ALU.add))
                    tt_(dst[0:DH, 2 * c + 1, :], rot_t[DH:P, 0, :], rot_t[DH:P, 1, :], ALU.add).then_inc(rot_done, 1)
                    dve.wait_ge(rot_done, 4 * j + c + 1)

            split(2)
            split(3)
            split(4)
            split(5)
            rotary(G_Q, 0, q_all)
            split(6)
            split(7)
            rotary(G_K, 1, k_all)
            split(8)
            split(9)

            def rsqrt_newton(y, x, tmp, out):
                st.step(tt_(tmp, y, y, ALU.mult))
                st.settle()
                st.step(stt(tmp, tmp, -0.5, x, ALU.mult, ALU.mult))
                st.settle()
                return stt(out, tmp, 1.5, y, ALU.add, ALU.mult)

            def diff_head(r):
                def M_(i):
                    wait(dve, at_s, i + 1, r, 4)
                    for m in range(2):
                        col = 2 * i + m
                        nc.vector.tensor_reduce(neg_max[:, col:col + 1], banks[2 * (i % 2) + m][:, 0:P * (i + 1)],
                                                AX.X, ALU.max, negate=True).then_inc(at_m, 1)

                def D_(i):
                    wait(dve, at_e, 2 * i + 2, r, 8)
                    c, n = 2 * i, P * (i + 1)
                    st.step(nc.vector.reciprocal(z_rec[:, c:c + 2], z_sum[:, c:c + 2]))
                    st.settle()
                    st.step(stt(coef[:, i:i + 1], z_sum[:, c:c + 1], z_rec[:, c + 1:c + 2], lam[:, 5:6], ALU.mult, ALU.mult))
                    st.settle()
                    stt(e_buf[:, 2 * (i % 2), 0:n], e_buf[:, 2 * (i % 2) + 1, 0:n], coef[:, i:i + 1],
                        e_buf[:, 2 * (i % 2), 0:n], ALU.mult, ALU.add).then_inc(at_p, 1)

                def C_(i):
                    wait(dve, at_t, i + 1, r, 4)
                    wait(dve, at_v, i - 1 if i >= 2 else 0, r, 4)
                    n = P * (i + 1)
                    nc.vector.tensor_copy(pt_buf[:, i % 2, 0:n], banks[4 + i % 2][:, 0:n]).then_inc(at_c, 1)

                def O_(i):
                    wait(dve, at_v, i + 1, r, 4)
                    wait(dve, at_x, 0, r, 1)
                    ts_(o_stage[:, i, :], banks[6][:, 0:P], z_rec[:, 2 * i:2 * i + 1], None, ALU.mult).then_inc(at_o, 1)

                M_(0)
                M_(1)
                for i in range(TT):
                    D_(i)
                    if i + 2 < TT:
                        M_(i + 2)
                    C_(i)
                    if i:
                        O_(i - 1)
                O_(TT - 1)
                wait(dve, at_nv, 1, r, 1)
                st.step(ts_(rms[:, 2, :], rms[:, 0, :], 1.0 / (2 * DH), RMS_EPS, ALU.mult, ALU.add))
                st.settle()
                st.step(rsqrt_newton(rms[:, 1, :], rms[:, 2, :], rms[:, 3, :], rms[:, 4, :]))
                st.settle()
                for i in range(TT):
                    stt(o_stage[:, i, :], o_stage[:, i, :], rms[:, 4, i:i + 1], sub_g[:, bass.ds(r * P, P)],
                        ALU.mult, ALU.mult).then_inc(at_n, 1)
                wait(dve, at_ns, 1, r, 1)
                tt_(act_lo[:, bass.ds(r, 1), :], banks[7][:, :].unsqueeze(1), act_hi[:, bass.ds(r, 1), :].bitcast(F32),
                    ALU.subtract).then_inc(act_ready, 1)

            st.loop(4, diff_head)

            dve.wait_ge(ssm_in, 16)
            a_re, a_im, ldt = (small[:, o:o + GROUPS] for o in (S_ARE, S_AIM, S_LDT))
            sl = [slot[:, i, :] for i in range(20)]

            def do(ins):
                st.step(ins)
                st.settle()

            def exp_parts(z, w, pm, f, k):
                do(ts_(f, z, -88.0, 88.7, ALU.max, ALU.min))
                do(ts_(k, f, 1.4426950408889634, 12582912.0, ALU.mult, ALU.add))
                do(ts_(k, k, -12582912.0, None, ALU.add))
                do(stt(f, k, -0.693359375, f, ALU.mult, ALU.add))
                do(stt(f, k, 2.12194440e-4, f, ALU.mult, ALU.add))
                do(ts_(pm, f, 1.0 / 5040, None, ALU.mult))
                for cf in (1.0 / 720, 1.0 / 120, 1.0 / 24, 1.0 / 6, 0.5, 1.0):
                    do(stt(pm, pm, cf, f, ALU.add, ALU.mult))
                do(ts_(slot_i, k, 127.0, None, ALU.add))
                do(ts_(slot_i, slot_i, 23, None, ALU.logical_shift_left))
                do(nc.vector.tensor_copy(w, slot_i.bitcast(F32)))

            dt, th, mag, magm1, s_, c_, cm1, ar, ai, gr, gi = sl[0:11]
            exp_parts(ldt, sl[11], sl[12], sl[13], sl[14])
            do(stt(dt, sl[12], 1.0, sl[11], ALU.add, ALU.mult))
            do(tt_(sl[15], a_re, dt, ALU.mult))
            exp_parts(sl[15], sl[11], sl[12], sl[13], sl[14])
            do(tt_(magm1, sl[12], sl[11], ALU.mult))
            do(tt_(mag, magm1, sl[11], ALU.add))
            do(ts_(sl[13], sl[11], -1.0, None, ALU.add))
            do(tt_(magm1, magm1, sl[13], ALU.add))
            do(tt_(th, a_im, dt, ALU.mult))
            do(ts_(sl[14], th, 1.0 / (2 * math.pi), 12582912.0, ALU.mult, ALU.add))
            do(ts_(sl[14], sl[14], -12582912.0, None, ALU.add))
            for piece in (6.28125, 1.9340515e-3, 1.2556659e-6):
                do(stt(th, sl[14], -piece, th, ALU.mult, ALU.add))
            do(ts_(th, th, -3.1415925, 3.1415925, ALU.max, ALU.min))
            ts_(sl[16], th, 0.5, None, ALU.mult).then_inc(ss_sin_in, 1)
            dve.wait_ge(ss_sin, 2)
            do(stt(cm1, c_, -2.0, c_, ALU.mult, ALU.mult))
            do(ts_(c_, cm1, 1.0, None, ALU.add))
            do(tt_(ar, mag, c_, ALU.mult))
            do(tt_(ai, mag, s_, ALU.mult))
            do(tt_(sl[11], mag, cm1, ALU.mult))
            do(tt_(sl[11], sl[11], magm1, ALU.add))
            do(tt_(sl[12], a_re, a_re, ALU.mult))
            do(tt_(sl[13], a_im, a_im, ALU.mult))
            do(tt_(sl[12], sl[12], sl[13], ALU.add))
            do(nc.vector.reciprocal(sl[12], sl[12]))
            do(tt_(gr, sl[11], a_re, ALU.mult))
            do(tt_(sl[13], ai, a_im, ALU.mult))
            do(tt_(gr, gr, sl[13], ALU.add))
            do(tt_(gr, gr, sl[12], ALU.mult))
            do(tt_(gi, ai, a_re, ALU.mult))
            do(tt_(sl[13], sl[11], a_im, ALU.mult))
            do(tt_(gi, gi, sl[13], ALU.subtract))
            do(tt_(gi, gi, sl[12], ALU.mult))
            do(ts_(gi, gi, sgn[:, 0:1], None, ALU.mult))

            def over_h(v):
                return v.unsqueeze(2).broadcast_to([P, GROUPS, GCH])

            flat = prod1.rearrange("p a b c -> p (a b c)")[:, 0:512].rearrange("p (g h) -> p g h", g=GROUPS)
            do(tt_(bb1, b_ri, over_h(gr), ALU.mult))
            do(tt_(flat, b_ir, over_h(gi), ALU.mult))
            do(tt_(bb1, bb1, flat, ALU.add))
            do(tt_(bb2, b_ir, over_h(gr), ALU.mult))
            do(tt_(flat, b_ri, over_h(gi), ALU.mult))
            do(tt_(bb2, bb2, flat, ALU.subtract))
            do(ts_(sl[17][:, 0:1], sgn[:, 0:1], -1.0, None, ALU.mult))
            do(ts_(c_ri, c_ri, sl[17][:, 0:1], None, ALU.mult))
            do(ts_(c_ir, c_ir, sl[17][:, 0:1], None, ALU.mult))

            def cmul(dr, di, xr, xi, yr, yi, t1, t2):
                do(tt_(t1, xr, yr, ALU.mult))
                do(tt_(t2, xi, yi, ALU.mult))
                do(tt_(dr, t1, t2, ALU.subtract))
                do(tt_(t1, xr, yi, ALU.mult))
                do(tt_(t2, xi, yr, ALU.mult))
                do(tt_(di, t1, t2, ALU.add))

            do(nc.vector.memset(pow_r[:, :, 0], 1.0))
            do(nc.vector.memset(pow_i[:, :, 0], 0.0))
            do(nc.vector.tensor_copy(pow_r[:, :, 1], ar))
            do(nc.vector.tensor_copy(pow_i[:, :, 1], ai))
            for n in (1, 2, 4):
                t1 = prod1.rearrange("p a b c -> p (a b c)")[:, 0:GROUPS * n].rearrange("p (g e) -> p g e", g=GROUPS)
                t2 = prod2.rearrange("p a b c -> p (a b c)")[:, 0:GROUPS * n].rearrange("p (g e) -> p g e", g=GROUPS)
                br = pow_r[:, :, n:n + 1].broadcast_to([P, GROUPS, n])
                bi = pow_i[:, :, n:n + 1].broadcast_to([P, GROUPS, n])
                cmul(pow_r[:, :, n + 1:2 * n + 1], pow_i[:, :, n + 1:2 * n + 1],
                     pow_r[:, :, 1:n + 1], pow_i[:, :, 1:n + 1], br, bi, t1, t2)
            do(ts_(pow_i, pow_i, sgn[:, 0:1], None, ALU.mult))
            for e in range(L):
                st.step(nc.vector.tensor_copy(prev_r[:, :, e], pow_r[:, :, L - 1 - e]))
                st.step(nc.vector.tensor_copy(prev_i[:, :, e], pow_i[:, :, L - 1 - e]))
            cr, ci = phase[:, 0:6, :], phase[:, 6:12, :]
            cmul(sl[11], sl[12], c_, s_, c_, s_, sl[13], sl[14])
            cmul(sl[15], sl[16], sl[11], sl[12], sl[11], sl[12], sl[13], sl[14])
            cmul(cr[:, 0, :], ci[:, 0, :], sl[15], sl[16], sl[15], sl[16], sl[13], sl[14])
            for n in range(5):
                cmul(cr[:, n + 1, :], ci[:, n + 1, :], cr[:, n, :], ci[:, n, :], cr[:, n, :], ci[:, n, :], sl[13], sl[14])
            for _ in range(3):
                do(tt_(mag, mag, mag, ALU.mult))
            do(nc.vector.memset(f_tab[:, :, L:M15, :], 0.0))
            do(nc.vector.memset(r_tab[:, :, 0], 0.0))
            do(nc.vector.memset(x_buf[:, :, 0], 0.0))

            def ssm_batch(r):
                gs = bass.ds(r * GB, GB)

                def over(v, shape, ax):
                    return v.unsqueeze(ax).broadcast_to(shape)

                full = [P, GB, L, GCH]
                wait(dve, ss_y, 0, r, 1)
                st.settle()
                st.step(tt_(prod1, over(prev_r[:, gs, :], full, 3), over(bb1[:, gs, :], full, 2), ALU.mult))
                st.step(tt_(prod2, over(prev_i[:, gs, :], full, 3), over(bb2[:, gs, :], full, 2), ALU.mult))
                st.settle()
                tt_(f_tab[:, :, 0:L, :], prod1, prod2, ALU.add).then_inc(ss_f, 1)
                wait(dve, ss_f, 1, r, 1)
                st.step(tt_(prod1, over(pow_r[:, gs, 1:L + 1], full, 3), over(c_ri[:, gs, :], full, 2), ALU.mult))
                st.step(tt_(prod2, over(pow_i[:, gs, 1:L + 1], full, 3), over(c_ir[:, gs, :], full, 2), ALU.mult))
                st.settle()
                do(tt_(ca_mat, prod1, prod2, ALU.add))
                do(nc.vector.memset(e_cos[:, :, 0], 1.0))
                do(nc.vector.memset(e_sin[:, :, 0], 0.0))
                for lv in range(6):
                    n = 1 << lv
                    t1 = prod1.rearrange("p a b c -> p (a b c)")[:, 0:GB * n].rearrange("p (g e) -> p g e", g=GB)
                    t2 = prod2.rearrange("p a b c -> p (a b c)")[:, 0:GB * n].rearrange("p (g e) -> p g e", g=GB)
                    br = cr[:, lv, gs].unsqueeze(2).broadcast_to([P, GB, n])
                    bi = ci[:, lv, gs].unsqueeze(2).broadcast_to([P, GB, n])
                    cmul(e_cos[:, :, n:2 * n], e_sin[:, :, n:2 * n], e_cos[:, :, 0:n], e_sin[:, :, 0:n], br, bi, t1, t2)
                do(ts_(e_sin, e_sin, sgn[:, 0:1], -1.0, ALU.mult, ALU.mult))
                do(nc.vector.tensor_copy(r_tab[:, :, 1:NCH], mag[:, gs].unsqueeze(2).broadcast_to([P, GB, NCH - 1])))
                h1 = prod1.rearrange("p a b c -> p (a b c)")[:, 0:GB * NCH].rearrange("p (g c) -> p g c", g=GB)
                h2 = prod2.rearrange("p a b c -> p (a b c)")[:, 0:GB * NCH].rearrange("p (g c) -> p g c", g=GB)
                wait(dve, ss_sw, 1, r, 1)
                st.step(tt_(h1, s_buf, e_cos, ALU.mult))
                st.step(tt_(h2, banks[5][:, :].rearrange("p (g c) -> p g c", g=GB), e_sin, ALU.mult))
                st.settle()
                do(tt_(h1, h1, h2, ALU.add))
                nc.vector.tensor_tensor_scan(y_buf.rearrange("p g c -> p (g c)"), r_tab.rearrange("p g c -> p (g c)"),
                                             h1.rearrange("p g c -> p (g c)"), 0.0, ALU.mult, ALU.add).then_inc(ss_scan, 1)
                wait(dve, ss_yw, 1, r, 1)
                wait(dve, ss_scan, 1, r, 1)
                n = NCH - 1
                st.step(tt_(h1[:, :, 0:n], y_buf[:, :, 0:n], e_cos[:, :, 0:n], ALU.mult))
                st.step(tt_(h2[:, :, 0:n], banks[6][:, :].rearrange("p (g c) -> p g c", g=GB)[:, :, 0:n],
                            e_sin[:, :, 0:n], ALU.mult))
                st.settle()
                tt_(x_buf[:, :, 1:NCH], h1[:, :, 0:n], h2[:, :, 0:n], ALU.subtract).then_inc(ss_x, 1)

            st.loop(NB, ssm_batch)

            for b in range(4):
                dve.wait_ge(y_in[b], 16 * GB)
                stt(y_t[:, b, :], u_t[:, b, :], small[:, S_D + b:S_D + b + 1], y_t[:, b, :],
                    ALU.mult, ALU.add).then_inc(glu_in, 1)
            for b in range(4):
                dve.wait_ge(glu_hi, b + 1)
                tt_(hid_lo[:, b, :], y_t[:, b, :], hid_hi[:, b, :].bitcast(F32), ALU.subtract).then_inc(glu_rhs, 1)
            for b in range(4):
                dve.wait_ge(glu_sig, b + 1)
                dve.wait_ge(glu_act, max(b - 1, 0)) if b > 1 else None
                yv = y_t[:, b, :].rearrange("p (i c) -> p c i", i=L)
                sv = tmp_a[:, b % 2, :].rearrange("p (i c) -> p c i", i=L)
                tt_(tmp_b[:, b % 2, :].rearrange("p (c i) -> p c i", i=L), yv, sv, ALU.mult).then_inc(glu_full, 1)
                dve.wait_ge(glu_act, b + 1)
                tt_(act_lo[:, 4 + b, :], tmp_b[:, b % 2, :], act_hi[:, 4 + b, :].bitcast(F32), ALU.subtract).then_inc(act_ready, 1)

            def evac_out(g):
                for i in range(TT):
                    h = g - (G_OUT0 if g < G_L1 else G_OUT1)
                    dve.wait_ge(pe_event, BANK_EVENT[g, i])
                    cs = slice(h * COLS, (h + 1) * COLS)
                    stt(acc[:, i, cs], resid[:, i, cs], ALPHA, bank_set(g)[i][:, :], ALU.mult, ALU.add).then_inc(evac_dve, 1)

            def out_projection(g0, n0):
                split(n0 + 2)
                evac_out(g0)
                split(n0 + 3)
                split(n0 + 4)
                evac_out(g0 + 1)
                split(n0 + 5)

            split(SL_OUT0 + 1)
            dve.wait_ge(x_in, 16)
            out_projection(G_OUT0, SL_OUT0)

            def layer_norm(l):
                dve.wait_ge(evac_dve, EVAC_DVE_LN[l])
                for i in range(TT):
                    for h in range(2):
                        st.step(nc.vector.bn_stats(stats[:, i, 6 * h:6 * h + 6], acc[:, i, h * 512:(h + 1) * 512]))
                st.settle()
                for i in range(TT):
                    nc.vector.bn_aggr(mv[:, i, :], stats[:, i, :]).then_inc(ln_var, 1)
                dve.wait_ge(ln_var, 4 * l + 4)
                dve.wait_ge(ln_seed, 2 * l + 2)
                do(ts_(lns[:, 2, :], mv[:, :, 1], LN_EPS, None, ALU.add))
                do(rsqrt_newton(lns[:, 1, :], lns[:, 2, :], lns[:, 3, :], lns[:, 4, :]))
                for i in range(TT):
                    ts_(resid[:, i, :], acc[:, i, :], mv[:, i, 0:1], lns[:, 4, i:i + 1],
                        ALU.subtract, ALU.mult).then_inc(xhat_ready, 1)

            def norm_split(l):
                for k in range(KB):
                    dve.wait_ge(act_hi_done, 8 * l + k + 1)
                    do(ts_(tmp_a[:, k % 2, :], norm_bank(k)[:, :], small[:, S_LNG + 8 * l + k:S_LNG + 8 * l + k + 1],
                           small[:, S_LNB + 8 * l + k:S_LNB + 8 * l + k + 1], ALU.mult, ALU.add))
                    tt_(act_lo[:, k, :], tmp_a[:, k % 2, :], act_hi[:, k, :].bitcast(F32), ALU.subtract).then_inc(act_ready, 1)

            def mlp(g0, n0, h0, a0, r, last=False):
                for c in range(2):
                    g, n = g0 + 3 * c, n0 + 4 * c
                    split(n + 2, r)
                    for k in range(4):
                        wait(dve, relu_done, h0 + 4 * c + k + 1, r, 8)
                        tt_(tmp_b[:, k % 2, :], tmp_a[:, k % 2, :], tmp_a[:, k % 2, :], ALU.mult).then_inc(sq_done, 1)
                        wait(dve, sq_done, h0 + 4 * c + k + 1, r, 8)
                        wait(dve, hid_hi_done, h0 + 4 * c + k + 1, r, 8)
                        tt_(hid_lo[:, k, :], tmp_b[:, k % 2, :], hid_hi[:, k, :].bitcast(F32),
                            ALU.subtract).then_inc(hid_ready, 1)
                    split(n + 3, r)
                    for half in range(2):
                        if not (last and c == 1):
                            split(n + 4 + half, r)
                        if isinstance(r, int) and r == 0 and c == 0 and half == 0:
                            dve.wait_ge(acc_init, 4 + h0 // 8)
                        for i in range(TT):
                            wait(dve, pe_event, BANK_EVENT[g + 1 + half, i], r, 2 * CHUNK_EVENTS)
                            cs = slice(half * COLS, (half + 1) * COLS)
                            tt_(acc[:, i, cs], acc[:, i, cs], bank_set(g + 1 + half)[i][:, :], ALU.add).then_inc(evac_dve, 1)

            layer_norm(0)
            norm_split(0)
            mlp(G_MLP0, SL_MLP0, 0, 0, 0)
            with dve.Fori(1, 4) as r:
                mlp(G_MLP0, SL_MLP0, 0, 0, r)
            layer_norm(1)
            norm_split(1)

            dve.wait_ge(gate_w_hi, 1)
            tt_(gw_lo[:, :, :], gate_w[:, :, :], gw_hi[:, :, :].bitcast(F32), ALU.subtract).then_inc(gate_w_split, 2)
            dve.wait_ge(gate_mm, 1)
            bf = small[:, S_BF:S_BF + 16].unsqueeze(1).broadcast_to([P, TT, 16])
            do(tt_(logf[:, 0, :, :], banks[0][:, 0:64].rearrange("p (a h) -> p a h", a=TT), bf, ALU.add))
            stt(logf[:, 1, :, :], logf[:, 0, :, :], -1.0, logf[:, 0, :, :], ALU.mult, ALU.max).then_inc(gate_z, 1)
            dve.wait_ge(gate_z, 3)
            stt(logf[:, 3, :, :], logf[:, 0, :, :], 0.0, logf[:, 2, :, :], ALU.min, ALU.subtract).then_inc(gate_log, 1)
            dve.wait_ge(gate_mm, 2)
            nc.vector.tensor_copy(fcum[0:16, 0, :], banks[1][0:16, :]).then_inc(gate_cum, 1)
            ts_(fcum[0:16, 1, :], banks[1][0:16, :], -1.0, None, ALU.mult).then_inc(gate_cum, 1)

            def fox_pair(half, r):
                u0 = 32 * half

                def M_(j):
                    wait(dve, fx_s, u0 + j + 1, r, 8)
                    nc.vector.tensor_reduce(neg_max[:, j:j + 1], banks[j % 2][:, 0:P * (j % TT + 1)],
                                            AX.X, ALU.max, negate=True).then_inc(fx_m, 1)

                def C_(j):
                    wait(dve, fx_t, u0 + j + 1, r, 8)
                    wait(dve, fx_v, u0 + (j - 1 if j >= 2 else 0), r, 8)
                    n = P * (j % TT + 1)
                    nc.vector.tensor_copy(pt_buf[:, j % 2, 0:n], banks[2 + j % 2][:, 0:n]).then_inc(fx_c, 1)

                def O_(j):
                    wait(dve, fx_v, u0 + j + 1, r, 8)
                    wait(dve, fx_x, 4 * half, r, 1)
                    st.step(nc.vector.reciprocal(z_rec[:, j:j + 1], z_sum[:, j:j + 1]))
                    st.settle()
                    ts_(o_stage[:, j % TT, (j // TT) * DH:(j // TT + 1) * DH], banks[4 + j % 2][:, 0:DH],
                        z_rec[:, j:j + 1], None, ALU.mult).then_inc(fx_o, 1)

                M_(0)
                M_(1)
                for j in range(8):
                    if j + 2 < 8:
                        M_(j + 2)
                    C_(j)
                    if j:
                        O_(j - 1)
                O_(7)
                wait(dve, fx_h, 4 * half + 1, r, 1)
                hi, lo, b0 = (hid_hi, hid_lo, 0) if half == 0 else (act_hi, act_lo, 4)
                tt_(lo[:, bass.ds(r + b0, 1), :], banks[6][:, :].unsqueeze(1), hi[:, bass.ds(r + b0, 1), :].bitcast(F32),
                    ALU.subtract).then_inc(act_ready, 1)

            for half in range(2):
                n0, g0 = SL_L1 + 6 * half, G_L1 + 3 * half
                split(n0 + 2)
                split(n0 + 3)
                split(n0 + 4)
                for c in range(4):
                    dve.wait_ge(pe_event, BANK_EVENT[g0 + 1, c])
                    st.step(nc.vector.tensor_copy(k_all[0:DH, 2 * c, :], bank_set(g0 + 1)[c][0:DH, :]))
                    nc.vector.tensor_copy(k_all[0:DH, 2 * c + 1, :], bank_set(g0 + 1)[c][DH:P, :]).then_inc(evac_k1, 1)
                split(n0 + 5)
                split(n0 + 6)
                split(n0 + 7)
                st.settle()
                st.loop(4, lambda r: fox_pair(half, r))

            dve.wait_ge(resid_ready, 4)
            out_projection(G_OUT1, SL_OUT1)
            layer_norm(2)
            norm_split(2)
            mlp(G_MLP1, SL_MLP1, 32, 0, 0)
            with dve.Fori(1, 3) as r:
                mlp(G_MLP1, SL_MLP1, 32, 0, r)
            mlp(G_MLP1, SL_MLP1, 32, 0, 3, last=True)
            layer_norm(3)
            dve.wait_ge(row_in, 32 * 4)
            for i in range(TT):
                dve.wait_ge(xhat_ready, 12 + i + 1)
                do(tt_(acc[:, i, :], resid[:, i, :], ln_row[:, 0, :], ALU.mult))
                tt_(acc[:, i, :], acc[:, i, :], ln_row[:, 1, :], ALU.add).then_inc(out_ready, 1)

        @block.scalar
        def _(sc):
            act = nc.scalar.activation

            def split(n, r=0):
                if isinstance(r, int):
                    sc.wait_ge(slab_landed[n % 2], 16 * ((n + 8 * r) // 2 + 1))
                else:
                    wait(sc, slab_landed[n % 2], 16 * (n // 2 + 1), r, 64)
                if n >= 2:
                    wait(sc, pe_event, SLAB_EVENT[n - 2], r, 2 * CHUNK_EVENTS)
                act(slab_hi[:, n % 2, :, :], slab_raw[:, n % 2, :, :], ACT.Copy).then_inc(slab_hi_ready, 1)

            for kb in range(2):
                ks = slice(4 * kb, 4 * kb + 4)
                sc.wait_ge(xt_in[kb], 16)
                act(act_hi[:, ks, :], xt[:, ks, :], ACT.Copy).then_inc(stem_hi, 1)
                split(kb)
            sc.wait_ge(lam_sum, 1)
            act(lam[:, 2:4], lam[:, 0:2], ACT.Exp).then_inc(lam_exp, 1)
            split(2)
            for c in range(4):
                sc.wait_ge(pe_event, BANK_EVENT[G_U, c])
                act(u_t[:, c, :].rearrange("p (j n) -> p j n", j=L),
                    bank_set(G_U)[c][:, :].rearrange("p (n j) -> p j n", j=L), ACT.Copy).then_inc(u_ready, 1)
            split(3)
            split(4)
            sc.wait_ge(act_ready, 8)
            for c in range(4):
                sc.wait_ge(pe_event, BANK_EVENT[G_Q, c])
                act(rot_x[:, c, :], bank_set(G_Q)[c][:, :], ACT.Copy, scale=DH ** -0.5).then_inc(rot_copied, 1)
            split(5)
            split(6)
            for c in range(4):
                sc.wait_ge(pe_event, BANK_EVENT[G_K, c])
                sc.wait_ge(rot_done, c + 1)
                act(rot_x[:, c, :], bank_set(G_K)[c][:, :], ACT.Copy).then_inc(rot_copied, 1)
            split(7)
            split(8)
            for i in range(TT):
                sc.wait_ge(pe_event, BANK_EVENT[G_V, i])
                act(v_nat[:, i, :], bank_set(G_V)[i][:, :], ACT.Copy).then_inc(evac_act, 1)
            split(9)

            def diff_head(r):
                def E_(i):
                    n = P * (i + 1)
                    for m in range(2):
                        wait(sc, at_m, 2 * i + m + 1, r, 8)
                        wait(sc, at_t, i - 1 if i >= 2 else 0, r, 4)
                        col = 2 * i + m
                        act(e_buf[:, 2 * (i % 2) + m, 0:n], banks[2 * (i % 2) + m][:, 0:n], ACT.Exp,
                            bias=neg_max[:, col:col + 1], accum_out=z_sum[:, col:col + 1]).then_inc(at_e, 1)

                def Q_(i):
                    wait(sc, at_o, i + 1, r, 4)
                    wait(sc, at_sq, i, r, 4)
                    act(sq_scr[:, :], o_stage[:, i, :], ACT.Square, accum_out=rms[:, 0, i:i + 1]).then_inc(at_sq, 1)

                E_(0)
                for i in range(1, TT):
                    E_(i)
                for i in range(TT):
                    Q_(i)
                wait(sc, at_sq, 4, r, 4)
                act(rms[:, 1, :], rms[:, 0, :], ACT.Ln, bias=RMS_EPS, scale=1.0 / (2 * DH)).then_inc(at_w, 1)
                wait(sc, at_w, 1, r, 1)
                act(rms[:, 1, :], rms[:, 1, :], ACT.Exp, scale=-0.5).then_inc(at_nv, 1)
                wait(sc, at_x, 1, r, 1)
                act(act_hi[:, bass.ds(r, 1), :], banks[7][:, :].unsqueeze(1), ACT.Copy).then_inc(at_ns, 1)

            diff_head(0)
            with sc.Fori(1, 4) as r:
                diff_head(r)

            sc.wait_ge(ss_sin_in, 1)
            act(slot[:, 4, :], slot[:, 1, :], ACT.Sin).then_inc(ss_sin, 1)
            act(slot[:, 5, :], slot[:, 16, :], ACT.Sin).then_inc(ss_sin, 1)

            def ssm_batch(r):
                wait(sc, ss_t, 1, r, 2)
                wait(sc, ss_y, 0, r, 1)
                for b in range(2):
                    act(t_mat[:, 4 * b:4 * b + 4, :].rearrange("p g n -> p (g n)"), banks[b][:, :],
                        ACT.Copy).then_inc(ss_out_t, 1)
                wait(sc, ss_t, 2, r, 2)
                act(bst_mat[:, 0:4, :].rearrange("p g n -> p (g n)"), banks[2][:, :], ACT.Copy).then_inc(ss_out_t, 1)
                wait(sc, ss_out_t, 3, r, 3)
                act(bst_mat[:, 4:8, :].rearrange("p g n -> p (g n)"), banks[3][:, :], ACT.Copy).then_inc(ss_tc, 1)
                wait(sc, ss_s, 1, r, 1)
                act(s_buf[:, :, :].rearrange("p g c -> p (g c)"), banks[4][:, :], ACT.Copy).then_inc(ss_sc, 1)
                wait(sc, ss_y, 1, r, 1)
                wait(sc, y_out, 0, r, 16)
                act(y8[:, :, :].rearrange("p g c -> p (g c)"), banks[7][:, :], ACT.Copy).then_inc(ss_out, 1)

            ssm_batch(0)
            with sc.Fori(1, 4) as r:
                ssm_batch(r)

            for b in range(4):
                sc.wait_ge(glu_in, b + 1)
                act(y_t[:, b, :], y_t[:, b, :], ACT.Gelu_apprx_tanh).then_inc(glu_y, 1)
            for b in range(4):
                sc.wait_ge(glu_y, b + 1)
                act(hid_hi[:, b, :], y_t[:, b, :], ACT.Copy).then_inc(glu_hi, 1)
            for b in range(4):
                sc.wait_ge(pe_event, BANK_EVENT[G_GLU, b])
                if b > 1:
                    sc.wait_ge(glu_full, b - 1)
                act(tmp_a[:, b % 2, :], bank_set(G_GLU)[b][:, :], ACT.Sigmoid,
                    bias=small[:, S_GLUB + b:S_GLUB + b + 1]).then_inc(glu_sig, 1)
                sc.wait_ge(glu_full, b + 1)
                act(act_hi[:, 4 + b, :], tmp_b[:, b % 2, :], ACT.Copy).then_inc(glu_act, 1)
            for n in range(SL_OUT0 + 1, SL_MLP0 + 2):
                split(n)

            def norm_seed(l):
                sc.wait_ge(ln_var, 4 * l + 4)
                act(lns[:, 0, :], mv[:, :, 1], ACT.Ln, bias=LN_EPS).then_inc(ln_seed, 1)
                sc.wait_ge(ln_seed, 2 * l + 1)
                act(lns[:, 1, :], lns[:, 0, :], ACT.Exp, scale=-0.5).then_inc(ln_seed, 1)

            def norm_hi(l):
                for k in range(KB):
                    sc.wait_ge(ln_psum, 8 * l + k + 1)
                    act(act_hi[:, k, :], norm_bank(k)[:, :], ACT.Identity,
                        scale=small[:, S_LNG + 8 * l + k:S_LNG + 8 * l + k + 1],
                        bias=small[:, S_LNB + 8 * l + k:S_LNB + 8 * l + k + 1]).then_inc(act_hi_done, 1)

            def mlp(g0, n0, h0, r, last=False):
                for c in range(2):
                    g, n = g0 + 3 * c, n0 + 4 * c
                    split(n + 2, r)
                    for k in range(4):
                        m = h0 + 4 * c + k + 1
                        wait(sc, pe_event, BANK_EVENT[g, k], r, 2 * CHUNK_EVENTS)
                        wait(sc, sq_done, m - 2, r, 8)
                        wait(sc, hid_hi_done, m - 2, r, 8)
                        act(tmp_a[:, k % 2, :], bank_set(g)[k][:, :], ACT.Relu).then_inc(relu_done, 1)
                        wait(sc, relu_done, m, r, 8)
                        act(hid_hi[:, k, :], tmp_a[:, k % 2, :], ACT.Square).then_inc(hid_hi_done, 1)
                    split(n + 3, r)
                    if not (last and c == 1):
                        split(n + 4, r)
                        split(n + 5, r)

            norm_seed(0)
            norm_hi(0)
            mlp(G_MLP0, SL_MLP0, 0, 0)
            with sc.Fori(1, 4) as r:
                mlp(G_MLP0, SL_MLP0, 0, r)
            norm_seed(1)
            norm_hi(1)

            sc.wait_ge(gate_in, 16)
            act(gw_hi[:, :, :], gate_w[:, :, :], ACT.Copy).then_inc(gate_w_hi, 1)
            sc.wait_ge(gate_z, 1)
            act(logf[:, 2, :, :], logf[:, 1, :, :], ACT.Exp, scale=-1.0).then_inc(gate_z, 1)
            sc.wait_ge(gate_z, 2)
            act(logf[:, 2, :, :], logf[:, 2, :, :], ACT.Ln, bias=1.0).then_inc(gate_z, 1)

            def fox_pair(half, r):
                u0 = 32 * half
                for j in range(8):
                    n = P * (j % TT + 1)
                    wait(sc, fx_m, u0 + j + 1, r, 8)
                    wait(sc, fx_t, u0 + (j - 3 if j >= 4 else 0), r, 8)
                    wait(sc, fx_o, u0, r, 8)
                    act(e_buf[:, j % 4, 0:n], banks[j % 2][:, 0:n], ACT.Exp, bias=neg_max[:, j:j + 1],
                        accum_out=z_sum[:, j:j + 1]).then_inc(fx_e, 1)
                wait(sc, fx_x, 4 * half + 1, r, 1)
                hi, b0 = (hid_hi, 0) if half == 0 else (act_hi, 4)
                act(hi[:, bass.ds(r + b0, 1), :], banks[6][:, :].unsqueeze(1), ACT.Copy).then_inc(fx_h, 1)

            for half in range(2):
                n0, g0 = SL_L1 + 6 * half, G_L1 + 3 * half
                split(n0 + 2)
                for c in range(4):
                    sc.wait_ge(pe_event, BANK_EVENT[g0, c])
                    act(q_all[0:DH, 2 * c, :], bank_set(g0)[c][0:DH, :], ACT.Copy, scale=DH ** -0.5).then_inc(act_step, 1)
                    act(q_all[0:DH, 2 * c + 1, :], bank_set(g0)[c][DH:P, :], ACT.Copy, scale=DH ** -0.5).then_inc(evac_q1, 1)
                split(n0 + 3)
                split(n0 + 4)
                split(n0 + 5)
                split(n0 + 6)
                for i in range(TT):
                    sc.wait_ge(pe_event, BANK_EVENT[g0 + 2, i])
                    act(v_nat[:, i, :], bank_set(g0 + 2)[i][:, :], ACT.Copy).then_inc(evac_act, 1)
                split(n0 + 7)
                fox_pair(half, 0)
                with sc.Fori(1, 4) as r:
                    fox_pair(half, r)
            for n in range(SL_OUT1 + 2, SL_MLP1 + 2):
                split(n)
            norm_seed(2)
            norm_hi(2)
            mlp(G_MLP1, SL_MLP1, 32, 0)
            with sc.Fori(1, 3) as r:
                mlp(G_MLP1, SL_MLP1, 32, r)
            mlp(G_MLP1, SL_MLP1, 32, 3, last=True)
            norm_seed(3)

        @block.gpsimd
        def _(pool):
            st = Steps(pool, pool_step)

            def q_slots(q_sem, used, per_used, rows, base, used0, r):
                for m in range(2):
                    wait(pool, used, used0, r, per_used)
                    nc.gpsimd.tensor_copy(q_slot[0:rows, m, :].unsqueeze(1),
                                          q_all[0:rows, bass.ds(r * 2 + m, 1), :]).then_inc(q_sem, 1)

            pool.wait_ge(rot_done, 8)
            q_slots(at_q, at_s, 4, DH, 0, 0, 0)
            with pool.Fori(1, 4) as r:
                q_slots(at_q, at_s, 4, DH, 0, 0, r)

            def rows_in(l):
                st.settle()
                for j, name in enumerate(("g", "b")):
                    row = t["ln%d_%s" % (1 + l % 2, name)][l // 2:l // 2 + 1, :].broadcast_to([P, D])
                    pool.dma_start(ln_row[:, j, :], row).then_inc(row_in, 16)
                pool.wait_ge(row_in, 32 * (l + 1))

            def scaled_residual(l):
                rows_in(l)
                st.step(nc.gpsimd.tensor_scalar(ln_row[:, :, :], ln_row[:, :, :], ALPHA, None, ALU.mult))
                st.settle()
                for i in range(TT):
                    pool.wait_ge(xhat_ready, 4 * l + i + 1)
                    st.step(nc.gpsimd.tensor_tensor(acc[:, i, :], resid[:, i, :], ln_row[:, 0, :], ALU.mult))
                    st.settle()
                    nc.gpsimd.tensor_tensor(acc[:, i, :], acc[:, i, :], ln_row[:, 1, :], ALU.add).then_inc(acc_init, 1)

            pool.wait_ge(act_ready, 16)
            scaled_residual(0)
            pool.wait_ge(acc_init, 4)
            rows_in(1)
            pool.wait_ge(ln_psum, 16)
            for i in range(TT):
                st.step(nc.gpsimd.tensor_tensor(resid[:, i, :], resid[:, i, :], ln_row[:, 0, :], ALU.mult))
                st.settle()
                nc.gpsimd.tensor_tensor(resid[:, i, :], resid[:, i, :], ln_row[:, 1, :], ALU.add).then_inc(resid_ready, 1)
            pool.wait_ge(resid_ready, 4)
            nc.gpsimd.memset(q_all[DH:DH + 2, :, :], 1.0).then_inc(ones_set, 1)
            nc.gpsimd.memset(k_all[DH:DH + 2, :, :], 1.0).then_inc(ones_set, 1)
            for half in range(2):
                pool.wait_ge(evac_q1, 4 * half + 4)
                pool.wait_ge(decay_in, 32 * half + 32)
                q_slots(fx_q, fx_s, 8, DH + 2, 0, 32 * half, 0)
                with pool.Fori(1, 4) as r:
                    q_slots(fx_q, fx_s, 8, DH + 2, 0, 32 * half, r)
            scaled_residual(2)
            pool.wait_ge(acc_init, 8)
            rows_in(3)


ROPE_THETA = 10000.0


def constants():
    c = np.zeros((P, C_N), np.float32)
    i = np.arange(P)
    c[i, C_ID + i] = 1
    c[i, C_SW64 + (i + 64) % P] = 1
    c[i, C_SW32 + (i ^ 32)] = 1
    c[:, C_TRI:C_TRI + S] = np.arange(S)[None, :] >= i[:, None]
    c[:, C_MASK0:C_MASK0 + P] = np.where((i[None, :] // DH) > (i[:, None] // DH), NEG, 0)
    c[:, C_MASK1:C_MASK1 + P] = np.where(i[None, :] > i[:, None], NEG, 0)
    inv = (np.float32(ROPE_THETA) ** (-np.arange(0, DH, 2, dtype=np.float32) / np.float32(DH))).astype(np.float32)
    ang = np.arange(S, dtype=np.float32)[:, None] * inv[None, :]
    cos, sin = np.cos(ang).T.astype(np.float32), np.sin(ang).T.astype(np.float32)
    c[:, C_CC:C_CC + S] = np.tile(cos, (4, 1))
    c[:, C_SS:C_SS + S] = np.concatenate([-sin, sin, -sin, sin])
    c[:, C_SGN] = np.where(i < 64, -1, 1)
    return c


def kernel(**inputs):
    import numpy as _np
    import concourse.bacc as _bacc
    from concourse import mybir as _mybir
    from concourse.bass_utils import run_bass_kernel_spmd as _run

    nc = _bacc.Bacc("TRN2", target_bir_lowering=False, num_devices=1)
    a = {k: _np.asarray(v) for k, v in inputs.items()}

    def cols(v):
        return v.reshape(-1, P).T

    def per_state(v):
        return _np.concatenate([v.T, v.T])

    ln_g = _np.stack([a["ln1_g"], a["ln2_g"]], 1)
    ln_b = _np.stack([a["ln1_b"], a["ln2_b"]], 1)
    small = _np.concatenate([
        cols(ln_g), cols(ln_b), per_state(a["ssm_a_re"][0]), per_state(a["ssm_a_im"][0]),
        _np.broadcast_to(a["ssm_log_dt"][0], (P, GROUPS)), cols(a["ssm_d"][0]), cols(a["ssm_glu_b"][0]),
        _np.broadcast_to(a["fox_b_f"][0], (P, 16))], axis=1)
    b_re, b_im = (a[n][0].transpose(1, 0, 2).reshape(NSTATE, -1) for n in ("ssm_b_re", "ssm_b_im"))
    c_re, c_im = (a[n][0].transpose(2, 0, 1).reshape(NSTATE, -1) for n in ("ssm_c_re", "ssm_c_im"))
    ssm_bc = _np.stack([_np.concatenate(p) for p in ((b_re, b_im), (b_im, b_re), (c_re, c_im), (c_im, c_re))], 1)
    arrays = {
        "x": a["x"], "xt": a["x"][0].T.reshape(KB, P, S).transpose(1, 0, 2), "const": constants(), "small": small,
        "ssm_bc": ssm_bc, "ab_w_in": a["ab_w_in"][0], "ab_lambda": a["ab_lambda"], "ab_subln_g": a["ab_subln_g"],
        "ssm_glu_w": a["ssm_glu_w"][0], "ab_w_out": a["ab_w_out"][0], "fox_w_in": a["fox_w_in"][0],
        "fox_w_out": a["fox_w_out"][0], "ln1_g": a["ln1_g"], "ln1_b": a["ln1_b"], "ln2_g": a["ln2_g"],
        "ln2_b": a["ln2_b"], "ffn_w1": a["ffn_w1"], "ffn_w2": a["ffn_w2"],
    }
    arrays = {k: _np.ascontiguousarray(v) for k, v in arrays.items()}
    t = {k: nc.dram_tensor("in_" + k, v.shape, _mybir.dt.from_np(v.dtype), kind="ExternalInput").ap()
         for k, v in arrays.items()}
    t["u_scratch"] = nc.dram_tensor("u_scratch", (GROUPS * GCH, S), _mybir.dt.float32).ap()
    t["y_scratch"] = nc.dram_tensor("y_scratch", (NB, P, GB * NCH), _mybir.dt.float32).ap()
    t["out"] = nc.dram_tensor("out_0", (S, D), _mybir.dt.float32, kind="ExternalOutput").ap()
    trunk(nc, t)
    r = _run(nc, [{"in_" + k: v for k, v in arrays.items()}], core_ids=[0])
    return r.results[0]["out_0"].reshape(1, S, D)
```

```python
import math
from contextlib import ExitStack

import numpy as np
import concourse.bass as bass
from concourse import mybir

F32 = mybir.dt.float32
F32R = mybir.dt.float32r
BF16 = mybir.dt.bfloat16
I32 = mybir.dt.int32
ALU = mybir.AluOpType
ACT = mybir.ActivationFunctionType
AX = mybir.AxisListType

P = 128
D = 1024
S = 512
KB = D // P
TT = S // P
D_FF = 4 * D
SLAB_K = 4
COLS = 512
HEADS_STAGE = 8
DH = 64
ALPHA = 4.0 ** 0.25
LN_EPS = 1e-5
RMS_EPS = 1e-6
LAM_INIT = 0.8 - 0.6 * math.exp(-0.3 * 0)
NEG = -1.0e30
GROUPS = 32
GCH = 16
NSTATE = 64
L = 8
NCH = S // L
GB = 8
NB = GROUPS // GB
M15 = 2 * L - 1

C_ID, C_SW64, C_SW32, C_TRI, C_MASK0, C_MASK1, C_CC, C_SS, C_SGN = 0, 128, 256, 384, 896, 1024, 1152, 1664, 2176
C_N = 2177
S_LNG, S_LNB, S_ARE, S_AIM, S_LDT, S_D, S_GLUB, S_BF = 0, 32, 64, 96, 128, 160, 164, 168
S_N = 184

SL_U, SL_Q, SL_K, SL_V, SL_GLU, SL_OUT0, SL_MLP0 = 0, 2, 4, 6, 8, 9, 13
SL_L1 = 45
SL_OUT1, SL_MLP1, SL_END = 57, 61, 93


def group_table():
    groups = []
    for s in (SL_U, SL_Q, SL_K, SL_V):
        groups.append([s, s + 1])
    groups.append([SL_GLU])
    groups += [[SL_OUT0, SL_OUT0 + 1], [SL_OUT0 + 2, SL_OUT0 + 3]]
    for c in range(8):
        n = SL_MLP0 + 4 * c
        groups += [[n, n + 1], [n + 2], [n + 3]]
    for s in range(SL_L1, SL_OUT1, 2):
        groups.append([s, s + 1])
    groups += [[SL_OUT1, SL_OUT1 + 1], [SL_OUT1 + 2, SL_OUT1 + 3]]
    for c in range(8):
        n = SL_MLP1 + 4 * c
        groups += [[n, n + 1], [n + 2], [n + 3]]
    slab_event, bank_event, e = {}, {}, 0
    for g, slabs in enumerate(groups):
        if len(slabs) == 2:
            e += 1
            slab_event[slabs[0]] = e
        for t in range(4):
            e += 1
            bank_event[g, t] = e
        slab_event[slabs[-1]] = e
    return groups, slab_event, bank_event


GROUP_SLABS, SLAB_EVENT, BANK_EVENT = group_table()
G_U, G_Q, G_K, G_V, G_GLU, G_OUT0, G_MLP0, G_L1, G_OUT1, G_MLP1 = 0, 1, 2, 3, 4, 5, 7, 31, 37, 39
EVAC_DVE_LN = [8, 72, 80, 144]
CHUNK_EVENTS = 13


def wait(eng, sem, value, r=0, per=0):
    if isinstance(r, int):
        if value + per * r > 0:
            eng.wait_ge(sem, value + per * r)
    else:
        eng.wait_ge(sem, r * per + value)


def trunk(nc, t):
    with ExitStack() as ctx:
        def sb(name, shape, dt=F32):
            return ctx.enter_context(nc.sbuf_tensor(name, shape, dt))

        def sem(name):
            return ctx.enter_context(nc.semaphore(name))

        slab_raw = sb("slab_raw", [P, 2, SLAB_K, COLS])
        slab_hi = sb("slab_hi", [P, 2, SLAB_K, COLS], F32R)
        slab_lo = sb("slab_lo", [P, 2, SLAB_K, COLS], F32R)
        act_hi = sb("act_hi", [P, KB, S], F32R)
        act_lo = sb("act_lo", [P, KB, S], F32R)
        hid_hi = sb("hid_hi", [P, 4, S], F32R)
        hid_lo = sb("hid_lo", [P, 4, S], F32R)
        resid = sb("resid", [P, TT, D])
        acc = sb("acc", [P, TT, D])
        const = sb("const", [P, C_MASK0])
        consth = sb("consth", [P, 3, P], BF16)
        sgn = sb("sgn", [P, 1])
        small = sb("small", [P, S_N])
        stats = sb("stats", [P, TT, 12])
        mv = sb("mv", [P, TT, 2])
        lns = sb("lns", [P, 5, TT])
        gw_hi = sb("gw_hi", [P, KB, 16], F32R)
        gw_lo = sb("gw_lo", [P, KB, 16], F32R)
        arena = sb("arena", [P, 17920])

        def view(off, *shape):
            n = int(np.prod(shape))
            assert off + n <= 17920
            v = arena[:, off:off + n]
            if len(shape) == 2:
                return v.rearrange("p (a b) -> p a b", a=shape[0])
            if len(shape) == 3:
                return v.rearrange("p (a b c) -> p a b c", a=shape[0], b=shape[1])
            return v

        ident = const[:, C_ID:C_ID + P]
        swap64 = const[:, C_SW64:C_SW64 + P]
        swap32 = const[:, C_SW32:C_SW32 + P]
        tri = const[:, C_TRI:C_TRI + S]
        ident_h, mask_h = consth[:, 0, :], [consth[:, 1, :], consth[:, 2, :]]

        q_all = view(0, 8, S)
        k_all = view(4096, 8, S)
        e_buf = view(8192, 4, S)
        pt_buf = view(10240, 2, S)
        q_slot = view(11264, 2, S)
        o_stage = view(12288, TT, P)
        sub_g = view(12800, S)
        neg_max = view(13312, 16)
        z_sum = view(13328, 16)
        z_rec = view(13344, 16)
        coef = view(13360, 16)
        lam = view(13376, 8)
        rms = view(13384, 5, TT)
        lam_in = view(13440, 4, DH)
        lam_pr = view(13696, 2, DH)
        sq_scr = sb("sq_scr", [P, P])
        logf = view(13824, 4, TT, 16)
        fcum = view(14080, 2, S)
        gate_w = view(15104, KB, 16)
        ln_row = view(15232, 2, D)
        rot_x = acc[:, 2:4, :].rearrange("p a (b n) -> p (a b) n", n=S)
        rot_t = view(8192, 2, S)
        rot_c = view(10240, 2, S)
        consth_f = view(12288, 2, P)
        v_nat = acc[:, 0:2, :].rearrange("p a (b n) -> p (a b) n", n=COLS)
        tmp_a = view(8192, 2, S)
        tmp_b = view(9216, 2, S)

        banks = [ctx.enter_context(nc.psum_tensor(f"bank{i}", [P, 512], F32)) for i in range(8)]

        def norm_bank(k):
            return banks[(k + 4) % 8]

        def bank_set(g):
            return banks[4 * (g % 2):4 * (g % 2) + 4]

        slab_landed = [sem(f"slab_landed{i}") for i in range(2)]
        slab_hi_ready = sem("slab_hi_ready")
        slab_lo_ready = sem("slab_lo_ready")
        pe_event = sem("pe_event")
        const_in, x_in = sem("const_in"), sem("x_in")
        xt_in = [sem(f"xt_in{i}") for i in range(2)]
        y_in = [sem(f"y_in{i}") for i in range(NB)]
        consth_ready = sem("consth_ready")
        evac_act = sem("evac_act")
        evac_dve = sem("evac_dve")
        act_hi_done = sem("act_hi_done")
        act_ready = sem("act_ready")
        relu_done = sem("relu_done")
        hid_hi_done = sem("hid_hi_done")
        sq_done = sem("sq_done")
        hid_ready = sem("hid_ready")
        dve_step = sem("dve_step")
        act_step = sem("act_step")
        pool_step = sem("pool_step")
        ln_var = sem("ln_var")
        ln_seed = sem("ln_seed")
        xhat_ready = sem("xhat_ready")
        ln_psum = sem("ln_psum")
        ln_full = sem("ln_full")
        ln_split = sem("ln_split")
        row_in = sem("row_in")
        acc_init = sem("acc_init")
        resid_ready = sem("resid_ready")
        out_ready = sem("out_ready")
        out_done = sem("out_done")
        rot_copied, rot_swapped, rot_done = sem("rot_copied"), sem("rot_swapped"), sem("rot_done")
        at_q, at_s, at_m, at_e, at_p, at_t, at_c, at_v, at_z, at_o, at_sq, at_n, at_x = (
            sem("at_" + n) for n in ("q", "s", "m", "e", "p", "t", "c", "v", "z", "o", "sq", "n", "x"))
        at_nv = sem("at_nv")
        at_ns = sem("at_ns")
        at_w = sem("at_w")
        lam_dma, lam_sum, lam_exp, lam_done, subg_in = (
            sem("lam_dma"), sem("lam_sum"), sem("lam_exp"), sem("lam_done"), sem("subg_in"))
        rope_in = sem("rope_in")
        gate_in, gate_mm, gate_z, gate_log, gate_cum, gate_row = (
            sem("gate_in"), sem("gate_mm"), sem("gate_z"), sem("gate_log"), sem("gate_cum"), sem("gate_row"))
        decay_in, ones_set = sem("decay_in"), sem("ones_set")
        gate_w_split, gate_w_hi = sem("gate_w_split"), sem("gate_w_hi")
        evac_q1, evac_k1 = sem("evac_q1"), sem("evac_k1")
        fx_q, fx_s, fx_m, fx_e, fx_t, fx_c, fx_v, fx_o, fx_x, fx_h = (sem("fx_" + n) for n in "qsmetcvoxh")

        xt = acc[:, :, :].rearrange("p a (b n) -> p (a b) n", n=S)
        u_t = view(13824, 4, S)
        b_ri, b_ir = view(15872, GROUPS, GCH), view(16384, GROUPS, GCH)
        c_ri, c_ir = view(16896, GROUPS, GCH), view(17408, GROUPS, GCH)
        f_tab = view(0, GB, M15, GCH)
        t_mat = view(1920, GB, P)
        bst_mat = view(2944, GB, P)
        ca_mat = view(3968, GB, L, GCH)
        e_cos, e_sin, r_tab = view(4992, GB, NCH), view(5504, GB, NCH), view(6016, GB, NCH)
        s_buf, y_buf, x_buf = view(6528, GB, NCH), view(7040, GB, NCH), view(7552, GB, NCH)
        prod1, prod2 = view(8064, GB, L, GCH), view(9088, GB, L, GCH)
        u8 = view(10112, GROUPS, NCH)
        y8 = view(12160, GB, NCH)
        work1 = view(12672, GB, NCH)
        work2 = view(13184, GB, NCH)
        accf = acc[:, :, :].rearrange("p a n -> p (a n)")
        ca_mat = [ca_mat, accf[:, 0:1024].rearrange("p (g i h) -> p g i h", g=GB, i=L)]
        e_cos = [e_cos, accf[:, 1024:1536].rearrange("p (g c) -> p g c", g=GB)]
        e_sin = [e_sin, accf[:, 1536:2048].rearrange("p (g c) -> p g c", g=GB)]
        resf = resid[:, :, :].rearrange("p a n -> p (a n)")
        bb1 = resf[:, 0:512].rearrange("p (g h) -> p g h", g=GROUPS)
        bb2 = resf[:, 512:1024].rearrange("p (g h) -> p g h", g=GROUPS)
        pow_r = resf[:, 1024:1312].rearrange("p (g e) -> p g e", g=GROUPS)
        pow_i = resf[:, 1312:1600].rearrange("p (g e) -> p g e", g=GROUPS)
        prev_r = resf[:, 1600:1856].rearrange("p (g e) -> p g e", g=GROUPS)
        prev_i = resf[:, 1856:2112].rearrange("p (g e) -> p g e", g=GROUPS)
        phase = resf[:, 2112:2496].rearrange("p (e g) -> p e g", g=GROUPS)
        flat1, flat2 = resf[:, 2496:3008], resf[:, 3008:3264]
        slot = resf[:, 3264:3904].rearrange("p (i g) -> p i g", g=GROUPS)
        slot_i = resf[:, 3264 + 19 * 32:3264 + 20 * 32].bitcast(I32)
        y_t = accf[:, 2048:4096].rearrange("p (b n) -> p b n", b=4)
        ssm_in, u_ready, u8_in, ss_sin_in, ss_sin, ss_f, ss_t, ss_tc, ss_s, ss_sc, ss_sw, ss_y, ss_x, ss_yw, ss_out = (
            sem("ss_" + n) for n in ("in", "u", "u8", "sini", "sin", "f", "t", "tc", "s", "sc", "sw", "y", "x", "yw", "out"))
        ss_scan, ss_out_t, ss_ca, ss_par = sem("ss_scan"), sem("ss_out_t"), sem("ss_ca"), sem("ss_par")
        glu_in, glu_y, glu_hi, glu_rhs, glu_sig, glu_full, glu_act = (
            sem("glu_" + n) for n in ("in", "y", "hi", "rhs", "sig", "full", "act"))
        stem_hi, u_out, y_out = sem("stem_hi"), sem("u_out"), sem("y_out")

        block = ctx.enter_context(nc.Block())

        def w_src(w, kh, c0):
            return w.rearrange("(k p) n -> p k n", p=P)[:, kh * SLAB_K:(kh + 1) * SLAB_K, c0:c0 + COLS]

        def slab_source(n):
            if n < SL_GLU:
                col = {SL_U: 3, SL_Q: 0, SL_K: 1, SL_V: 2}[n - n % 2]
                return w_src(t["ab_w_in"], n % 2, col * COLS)
            if n == SL_GLU:
                return w_src(t["ssm_glu_w"], 0, 0)
            if n < SL_MLP0:
                j = n - SL_OUT0
                return w_src(t["ab_w_out"], j % 2, (j // 2) * COLS)
            if n < SL_OUT1:
                j = n - SL_L1
                half, part, kh = j // 6, (j % 6) // 2, j % 2
                return w_src(t["fox_w_in"], kh, part * D + half * COLS)
            j = n - SL_OUT1
            return w_src(t["fox_w_out"], j % 2, (j // 2) * COLS)

        def ssm_sp(sp):
            sp.wait_ge(u_ready, 4)
            sp.dma_start(t["u_scratch"].rearrange("(b p) n -> p b n", p=P), u_t[:, :, :]).then_inc(u_out, 16)
            sp.wait_ge(act_ready, 12)
            sp.wait_ge(u_out, 16)
            for j in range(L):
                src = t["u_scratch"].rearrange("(g h) n -> h g n", h=GCH)[:, :, j * NCH:(j + 1) * NCH]
                sp.dma_start(u8[j * GCH:(j + 1) * GCH, :, :], src).then_inc(u8_in, 16)
            for b in range(NB):
                if b == NB - 1:
                    sp.wait_ge(ss_x, NB)
                    sp.wait_ge(ss_ca, NB)
                    sp.dma_start(resid[:, :, :], t["x"][0].rearrange("(a p) n -> p a n", p=P)).then_inc(x_in, 16)
                sp.wait_ge(ss_out, b + 1)
                sp.dma_start(t["y_scratch"][b], y8[:, :, :].rearrange("p g c -> p (g c)")).then_inc(y_out, 16)
                sp.wait_ge(y_out, 16 * (b + 1))
                for g in range(GB):
                    src = t["y_scratch"][b].rearrange("(i h) (g c) -> h i g c", h=GCH, g=GB)[:, :, g, :]
                    dst = y_t[g * GCH:(g + 1) * GCH, b, :].rearrange("h (i c) -> h i c", i=L)
                    sp.dma_start(dst, src).then_inc(y_in[b], 16)

        @block.sync
        def _(sp):
            def slab(n, src, r=0, per=0):
                wait(sp, slab_hi_ready, n - 1, r, per)
                wait(sp, slab_lo_ready, n - 1, r, per)
                sp.dma_start(slab_raw[:, n % 2, :, :], src).then_inc(slab_landed[n % 2], 16)

            def mlp_slabs(l, n0, r):
                w1, w2 = t["ffn_w1"][l], t["ffn_w2"][l]
                for c in range(2):
                    for kh in range(2):
                        cols = bass.ds(r * (2 * COLS) + c * COLS, COLS)
                        src = w1.rearrange("(k p) n -> p k n", p=P)[:, kh * SLAB_K:(kh + 1) * SLAB_K, cols]
                        slab(n0 + 4 * c + kh, src, r, 8)
                    for g in range(2):
                        rows = bass.ds(r * (2 * SLAB_K) + c * SLAB_K, SLAB_K)
                        src = w2.rearrange("(k p) n -> p k n", p=P)[:, rows, g * COLS:(g + 1) * COLS]
                        slab(n0 + 4 * c + 2 + g, src, r, 8)

            for kb in range(2):
                sp.dma_start(xt[:, 4 * kb:4 * kb + 4, :], t["xt"][:, 4 * kb:4 * kb + 4, :]).then_inc(xt_in[kb], 16)
                slab(kb, slab_source(kb))
            sp.dma_start(const[:, :], t["const"][:, 0:C_MASK0]).then_inc(const_in, 16)
            sp.dma_start(small[:, :], t["small"]).then_inc(ssm_in, 16)
            sp.dma_start(view(15872, 4, GROUPS * GCH), t["ssm_bc"]).then_inc(ssm_in, 16)
            sp.dma_start(sgn[:, :], t["const"][:, C_SGN:C_SGN + 1], allow_slow_non_contiguous=True).then_inc(const_in, 16)
            slab(2, slab_source(2))
            slab(3, slab_source(3))
            sp.dma_start(consth_f, t["const"][:, C_MASK0:C_CC]).then_inc(const_in, 16)
            sp.dma_start(rot_c[:, :, :], t["const"][:, C_CC:C_SGN].rearrange("p (a n) -> p a n", a=2)).then_inc(rope_in, 16)
            sp.dma_start(sub_g[:, :], t["ab_subln_g"].rearrange("a h v -> a (h v)").broadcast_to([P, S])).then_inc(subg_in, 16)
            sp.dma_start(lam_in[:, :, :], t["ab_lambda"].broadcast_to([P, 4, DH])).then_inc(lam_dma, 16)
            for n in range(4, SL_OUT0 + 1):
                slab(n, slab_source(n))
            ssm_sp(sp)
            for n in range(SL_OUT0 + 1, SL_OUT0 + 3):
                slab(n, slab_source(n))
            slab(SL_OUT0 + 3, slab_source(SL_OUT0 + 3))
            with sp.Fori(0, 4) as r:
                mlp_slabs(0, SL_MLP0, r)
            slab(SL_L1, slab_source(SL_L1))
            slab(SL_L1 + 1, slab_source(SL_L1 + 1))
            sp.dma_start(gate_w[:, :, :], t["fox_w_in"].rearrange("(k p) n -> p k n", p=P)[:, :, 3 * D:3 * D + 16]).then_inc(gate_in, 16)

            def decay_rows(half):
                hs = slice(8 * half, 8 * half + 8)
                sp.dma_start(q_all[DH:DH + 1, :, :], fcum[hs, 0, :]).then_inc(decay_in, 16)
                sp.dma_start(k_all[DH + 1:DH + 2, :, :], fcum[hs, 1, :]).then_inc(decay_in, 16)

            sp.wait_ge(ones_set, 2)
            sp.wait_ge(gate_cum, 2)
            decay_rows(0)
            for n in range(SL_L1 + 2, SL_L1 + 8):
                slab(n, slab_source(n))
            sp.wait_ge(fx_s, 32)
            decay_rows(1)
            for n in range(SL_L1 + 8, SL_MLP1):
                slab(n, slab_source(n))
            with sp.Fori(0, 3) as r:
                mlp_slabs(1, SL_MLP1, r)
            mlp_slabs(1, SL_MLP1, 3)
            for i in range(TT):
                sp.wait_ge(out_ready, i + 1)
                sp.dma_start(t["out"][i * P:(i + 1) * P, :], acc[:, i, :]).then_inc(out_done, 16)
            sp.wait_ge(out_done, 16 * TT)

        @block.tensor
        def _(pe):
            mm = nc.tensor.matmul

            def three(out, a_hi, a_lo, b_hi, b_lo, first, last):
                mm(out, a_hi, b_hi, start=first, stop=False)
                mm(out, a_hi, b_lo, start=False, stop=False)
                return mm(out, a_lo, b_hi, start=False, stop=last)

            def slab_wait(n, r=0):
                wait(pe, slab_hi_ready, n + 1, r, 8)
                wait(pe, slab_lo_ready, n + 1, r, 8)

            def weights_left(g, n, kh, nk, r=0, a=None, out_set=None):
                slab_wait(n, r)
                a_hi, a_lo = a or (act_hi, act_lo)
                for c in range(4):
                    for k in range(SLAB_K):
                        cs = slice(c * P, (c + 1) * P)
                        ins = three(bank_set(g)[c][:, :], slab_hi[:, n % 2, k, cs], slab_lo[:, n % 2, k, cs],
                                    a_hi[:, kh * SLAB_K + k, :], a_lo[:, kh * SLAB_K + k, :],
                                    kh == 0 and k == 0, kh == nk - 1 and k == SLAB_K - 1)
                    if kh == nk - 1:
                        ins.then_inc(pe_event, 1)
                if kh < nk - 1:
                    ins.then_inc(pe_event, 1)

            def weights_right(g, n, kh, nk, a, base, r=0):
                slab_wait(n, r)
                a_hi, a_lo = a
                for tt in range(TT):
                    for k in range(SLAB_K):
                        ts = slice(tt * P, (tt + 1) * P)
                        ins = three(bank_set(g)[tt][:, :], a_hi[:, base + k, ts], a_lo[:, base + k, ts],
                                    slab_hi[:, n % 2, k, :], slab_lo[:, n % 2, k, :],
                                    kh == 0 and k == 0, kh == nk - 1 and k == SLAB_K - 1)
                    if kh == nk - 1:
                        ins.then_inc(pe_event, 1)
                if kh < nk - 1:
                    ins.then_inc(pe_event, 1)

            def swap_rotary(g, j):
                for c in range(4):
                    pe.wait_ge(rot_copied, 4 * j + c + 1)
                    mm(bank_set(g)[c][:, :], swap32, rot_x[:, c, :], start=True, stop=True).then_inc(rot_swapped, 1)

            act = (act_hi, act_lo)
            for kh in range(2):
                pe.wait_ge(act_ready, 4 * kh + 4)
                weights_left(G_U, SL_U + kh, kh, 2)
            weights_left(G_Q, SL_Q, 0, 2)
            weights_left(G_Q, SL_Q + 1, 1, 2)
            pe.wait_ge(u_ready, 4)
            weights_left(G_K, SL_K, 0, 2)
            pe.wait_ge(const_in, 48)
            swap_rotary(G_Q, 0)
            weights_left(G_K, SL_K + 1, 1, 2)
            pe.wait_ge(rot_done, 4)
            weights_right(G_V, SL_V, 0, 2, act, 0)
            swap_rotary(G_K, 1)
            weights_right(G_V, SL_V + 1, 1, 2, act, SLAB_K)

            def scores(out, qs, ks, i, layer):
                n = P * (i + 1)
                mm(out[:, n - P:n], ident_h, mask_h[layer], start=True, stop=False, skip_group_check=True)
                return mm(out[:, 0:n], qs, ks, start=False, stop=True, skip_group_check=True)

            def diff_head(r, first, last):
                def S_(i):
                    wait(pe, at_q, 2 * (i // TT) + 2, r, 2)
                    wait(pe, at_e, 2 * (i - 1), r, 8)
                    n = P * (i % TT + 1)
                    for m in range(2):
                        ks = k_all[0:DH, bass.ds(r * 2 + (2 * (i // TT) + m), 1), 0:n].rearrange("p a n -> p (a n)")
                        ins = scores(banks[2 * (i % 2) + m], q_slot[0:DH, m, n - P:n], ks, i % TT, 0)
                    ins.then_inc(at_s, 1)

                def T_(i):
                    wait(pe, at_p, i + 1, r, 4)
                    wait(pe, at_c, i - 1, r, 4)
                    for j in range(i + 1):
                        ins = nc.tensor.transpose(banks[4 + i % 2][:, j * P:(j + 1) * P],
                                                  e_buf[:, 2 * (i % 2), j * P:(j + 1) * P], ident)
                    ins.then_inc(at_t, 1)

                def V_(i):
                    wait(pe, at_c, i + 1, r, 4)
                    wait(pe, at_o, i, r, 4)
                    for j in range(i % TT + 1):
                        vs = v_nat[:, j, bass.ds(r * P + (i // TT) * P, P)]
                        ins = mm(banks[6][:, 0:P], pt_buf[:, i % 2, j * P:(j + 1) * P], vs,
                                 start=(j == 0), stop=(j == i % TT))
                    ins.then_inc(at_v, 1)

                def X_(k):
                    wait(pe, at_n, TT * (k + 1), r, TT)
                    wait(pe, act_ready, 8 + k, r, 1)
                    for i in range(TT):
                        ins = nc.tensor.transpose(banks[7][:, i * P:(i + 1) * P], o_stage[:, i, :], ident)
                    ins.then_inc(at_x, 1)

                if first:
                    S_(0)
                    S_(1)
                for i in range(TT):
                    T_(i)
                    if i + 2 < TT or not last:
                        S_(i + 2)
                    if i or not first:
                        V_(i - 1)
                    if i == 1 and not first:
                        X_(-1)
                if last:
                    V_(TT - 1)
                    X_(0)

            pe.wait_ge(evac_act, 4)
            pe.wait_ge(rot_done, 8)
            pe.wait_ge(consth_ready, 3)
            diff_head(0, True, False)
            with pe.Fori(1, 3) as r:
                diff_head(r, False, False)
            diff_head(3, False, True)

            def chunk_matrices(b):
                pe.wait_ge(ss_f, b + 1)
                if b:
                    pe.wait_ge(ss_out_t, 2 * b)
                    pe.wait_ge(ss_tc, 2 * b)
                for g in range(GB):
                    c1 = c_ri[:, b * GB + g, :]
                    for i in range(L):
                        lhs = f_tab[:, g, L - 1 - i:2 * L - 1 - i, :].rearrange("p j h -> p (j h)")
                        col = (g % 4) * P + i * GCH
                        ins = mm(banks[g // 4][:, col:col + GCH], lhs, c1, start=True, stop=True)
                ins.then_inc(ss_t, 1)
                for g in range(GB):
                    ins = nc.tensor.transpose(banks[2 + g // 4][:, (g % 4) * P:(g % 4 + 1) * P],
                                              f_tab[:, g, 0:L, :].rearrange("p j h -> p (j h)"), ident)
                ins.then_inc(ss_t, 1)

            def chunk_inputs(b):
                pe.wait_ge(ss_tc, 2 * b + 2)
                for g in range(GB):
                    ins = mm(banks[4][:, g * NCH:(g + 1) * NCH], bst_mat[:, g, :], u8[:, b * GB + g, :],
                             start=True, stop=True)
                ins.then_inc(ss_s, 1)
                pe.wait_ge(ss_sc, b + 1)
                mm(banks[5][:, :], swap64, s_buf[:, :, :].rearrange("p g c -> p (g c)"),
                   start=True, stop=True).then_inc(ss_sw, 1)

            pe.wait_ge(act_ready, 12)
            chunk_matrices(0)
            pe.wait_ge(u8_in, 16 * L)
            chunk_inputs(0)
            chunk_matrices(1)
            for b in range(NB):
                pe.wait_ge(ss_scan, b + 1)
                mm(banks[6][:, :], swap64, y_buf[:, :, :].rearrange("p g c -> p (g c)"),
                   start=True, stop=True).then_inc(ss_yw, 1)
                if b + 1 < NB:
                    chunk_inputs(b + 1)
                pe.wait_ge(ss_out_t, 2 * b + 2)
                pe.wait_ge(ss_ca, b + 1)
                pe.wait_ge(ss_x, b + 1)
                if b:
                    pe.wait_ge(ss_out, b)
                for g in range(GB):
                    out = banks[7][:, g * NCH:(g + 1) * NCH]
                    mm(out, t_mat[:, g, :], u8[:, b * GB + g, :], start=True, stop=False)
                    ins = mm(out, ca_mat[b % 2][:, g, :, :].rearrange("p i h -> p (i h)"), x_buf[:, g, :],
                             start=False, stop=True)
                ins.then_inc(ss_y, 1)
                if b + 2 < NB:
                    chunk_matrices(b + 2)

            pe.wait_ge(glu_rhs, 4)
            weights_left(G_GLU, SL_GLU, 0, 1, a=(hid_hi, hid_lo))

            def out_projection(g0, n0, lo, hi, ready):
                pe.wait_ge(act_ready, ready)
                for h in range(2):
                    weights_right(g0 + h, n0 + 2 * h, 0, 2, lo, 0)
                    weights_right(g0 + h, n0 + 2 * h + 1, 1, 2, hi, SLAB_K)

            out_projection(G_OUT0, SL_OUT0, act, act, 16)

            def norm_transposes(l):
                pe.wait_ge(evac_dve, EVAC_DVE_LN[l])
                for i in range(TT):
                    pe.wait_ge(xhat_ready, 4 * l + i + 1)
                    for k in range(KB):
                        ins = nc.tensor.transpose(norm_bank(k)[:, i * P:(i + 1) * P],
                                                  resid[:, i, k * P:(k + 1) * P], ident)
                        if i == TT - 1:
                            ins.then_inc(ln_psum, 1)

            def mlp(g0, n0, r, d0, h0, ready):
                for c in range(2):
                    g, n, rr = g0 + 3 * c, n0 + 4 * c, r
                    dv = d0 + 8 * c
                    wait(pe, evac_dve, dv - 4, rr, 16)
                    for kh in range(2):
                        if isinstance(r, int) and r == 0 and c == 0:
                            pe.wait_ge(act_ready, ready + 4 * kh)
                        weights_left(g, n + kh, kh, 2, rr)
                    wait(pe, evac_dve, dv, rr, 16)
                    slab_wait(n + 2, rr)
                    for half in range(2):
                        if half:
                            wait(pe, relu_done, h0 + 4 * c + 4, rr, 8)
                            slab_wait(n + 3, rr)
                        for k in range(SLAB_K):
                            if half == 0:
                                wait(pe, hid_ready, h0 + 4 * c + k + 1, rr, 8)
                            for tt in range(TT):
                                ts = slice(tt * P, (tt + 1) * P)
                                ins = three(bank_set(g + 1 + half)[tt][:, :], hid_hi[:, k, ts], hid_lo[:, k, ts],
                                            slab_hi[:, (n + 2 + half) % 2, k, :], slab_lo[:, (n + 2 + half) % 2, k, :],
                                            k == 0, k == SLAB_K - 1)
                                if k == SLAB_K - 1:
                                    ins.then_inc(pe_event, 1)

            norm_transposes(0)
            mlp(G_MLP0, SL_MLP0, 0, 8, 0, 20)
            with pe.Fori(1, 4) as r:
                mlp(G_MLP0, SL_MLP0, r, 8, 0, 20)
            norm_transposes(1)

            def fox_pair_pe(half, r, first, last):
                u0 = 32 * half

                def S_(j):
                    hh, i = j // TT, j % TT
                    wait(pe, fx_q, 8 * half + hh + 1, r, 2)
                    wait(pe, fx_e, u0 + j - 3, r, 8)
                    ks = k_all[0:DH + 2, bass.ds(r * 2 + hh, 1), 0:P * (i + 1)].rearrange("p a n -> p (a n)")
                    scores(banks[j % 4], q_slot[0:DH + 2, hh % 2, i * P:(i + 1) * P], ks, i, 1).then_inc(fx_s, 1)

                def T_(j):
                    wait(pe, fx_e, u0 + j + 1, r, 8)
                    wait(pe, fx_c, u0 + j - 1, r, 8)
                    for b in range(j % TT + 1):
                        ins = nc.tensor.transpose(banks[4 + j % 2][:, b * P:(b + 1) * P],
                                                  e_buf[:, j % 4, b * P:(b + 1) * P], ident)
                    ins.then_inc(fx_t, 1)

                def V_(j):
                    wait(pe, fx_c, u0 + j + 1, r, 8)
                    wait(pe, fx_o, u0 + j, r, 8)
                    for b in range(j % TT + 1):
                        vs = v_nat[:, b, bass.ds(r * P + (j // TT) * DH, DH)]
                        ins = mm(banks[6][:, 0:DH], pt_buf[:, j % 2, b * P:(b + 1) * P], vs,
                                 start=(b == 0), stop=(b == j % TT))
                    ins.then_inc(fx_v, 1)

                def X_(k):
                    wait(pe, fx_o, u0 + 8 * (k + 1), r, 8)
                    wait(pe, act_ready, 32 + 4 * half + k, r, 1)
                    for i in range(TT):
                        ins = nc.tensor.transpose(banks[7][:, i * P:(i + 1) * P], o_stage[:, i, :], ident)
                    ins.then_inc(fx_x, 1)

                if first:
                    for j in range(3):
                        S_(j)
                for j in range(8):
                    T_(j)
                    if j == 1 and not first:
                        X_(-1)
                    if j or not first:
                        V_(j - 1)
                    if j + 3 < 8 or not last:
                        S_(j + 3)
                if last:
                    V_(7)
                    X_(0)

            def decay_gate():
                pe.wait_ge(gate_in, 16)
                pe.wait_ge(gate_w_split, 2)
                pe.wait_ge(act_ready, 32)
                for i in range(TT):
                    ts = slice(i * P, (i + 1) * P)
                    for k in range(KB):
                        ins = three(banks[0][:, i * 16:(i + 1) * 16], act_hi[:, k, ts], act_lo[:, k, ts],
                                    gw_hi[:, k, :], gw_lo[:, k, :], k == 0, k == KB - 1)
                ins.then_inc(gate_mm, 1)
                pe.wait_ge(gate_log, 1)
                for i in range(TT):
                    ins = mm(banks[1][0:16, i * P:S], logf[:, 3, i, :], tri[:, 0:S - i * P],
                             start=(i == 0), stop=(i == TT - 1), skip_group_check=True)
                ins.then_inc(gate_mm, 1)
                pe.wait_ge(gate_cum, 2)

            decay_gate()
            for half in range(2):
                n0, g0 = SL_L1 + 6 * half, G_L1 + 3 * half
                if half:
                    pe.wait_ge(act_ready, 36)
                weights_left(g0, n0, 0, 2)
                weights_left(g0, n0 + 1, 1, 2)
                weights_left(g0 + 1, n0 + 2, 0, 2)
                weights_left(g0 + 1, n0 + 3, 1, 2)
                pe.wait_ge(evac_q1, 4 * half + 4)
                weights_right(g0 + 2, n0 + 4, 0, 2, act, 0)
                weights_right(g0 + 2, n0 + 5, 1, 2, act, SLAB_K)
                pe.wait_ge(evac_act, 4 + 4 * half + 4)
                pe.wait_ge(evac_k1, 4 * half + 4)
                fox_pair_pe(half, 0, True, False)
                with pe.Fori(1, 3) as r:
                    fox_pair_pe(half, r, False, False)
                fox_pair_pe(half, 3, False, True)
            out_projection(G_OUT1, SL_OUT1, (hid_hi, hid_lo), act, 40)
            norm_transposes(2)
            mlp(G_MLP1, SL_MLP1, 0, EVAC_DVE_LN[2], 32, 44)
            with pe.Fori(1, 4) as r:
                mlp(G_MLP1, SL_MLP1, r, EVAC_DVE_LN[2], 32, 44)

        class Steps:

            def __init__(self, eng, sem_):
                self.eng, self.sem, self.count, self.r, self.per = eng, sem_, 0, 0, 0

            def step(self, ins):
                self.count += 1
                ins.then_inc(self.sem, 1)

            def settle(self):
                wait(self.eng, self.sem, self.count, self.r, self.per)

            def pipelined(self, n, per_body, body):
                body(0, True, False)
                start = self.count
                with self.eng.Fori(1, n - 1) as r:
                    self.count, self.r, self.per = start - per_body, r, per_body
                    body(r, False, False)
                    assert self.count == start, self.count - start
                self.count, self.r, self.per = start + (n - 2) * per_body, 0, 0
                body(n - 1, False, True)

        @block.vector
        def _(dve):
            st = Steps(dve, dve_step)
            tt_, ts_, stt = nc.vector.tensor_tensor, nc.vector.tensor_scalar, nc.vector.scalar_tensor_tensor

            def split(n, r=0):
                wait(dve, slab_hi_ready, n + 1, r, 8)
                tt_(slab_lo[:, n % 2, :, :], slab_raw[:, n % 2, :, :], slab_hi[:, n % 2, :, :].bitcast(F32),
                    ALU.subtract).then_inc(slab_lo_ready, 1)

            for kb in range(2):
                ks = slice(4 * kb, 4 * kb + 4)
                dve.wait_ge(stem_hi, kb + 1)
                tt_(act_lo[:, ks, :], xt[:, ks, :], act_hi[:, ks, :].bitcast(F32), ALU.subtract).then_inc(act_ready, 4)
                split(kb)
            dve.wait_ge(const_in, 48)
            nc.vector.tensor_copy(ident_h, ident).then_inc(consth_ready, 1)
            for m in range(2):
                nc.vector.tensor_copy(mask_h[m], consth_f[:, m, :]).then_inc(consth_ready, 1)

            dve.wait_ge(lam_dma, 16)
            pairs = lam_in[:, :, :].rearrange("p (a b) d -> p a b d", b=2)
            st.step(tt_(lam_pr[:, :, :], pairs[:, :, 0, :], pairs[:, :, 1, :], ALU.mult))
            st.settle()
            nc.vector.tensor_reduce(lam[:, 0:2], lam_pr[:, :, :], AX.X, ALU.add).then_inc(lam_sum, 1)
            dve.wait_ge(lam_exp, 1)
            st.step(tt_(lam[:, 4:5], lam[:, 3:4], lam[:, 2:3], ALU.subtract))
            st.settle()
            st.step(ts_(lam[:, 5:6], lam[:, 4:5], -LAM_INIT, None, ALU.add))
            dve.wait_ge(subg_in, 16)
            st.step(ts_(sub_g[:, :], sub_g[:, :], 1.0 - LAM_INIT, None, ALU.mult))

            def rotary(g, j, dst):
                dve.wait_ge(rope_in, 16)
                for c in range(4):
                    dve.wait_ge(rot_swapped, 4 * j + c + 1)
                    st.step(tt_(rot_t[:, 0, :], rot_x[:, c, :], rot_c[:, 0, :], ALU.mult))
                    st.step(tt_(rot_t[:, 1, :], bank_set(g)[c][:, :], rot_c[:, 1, :], ALU.mult))
                    st.settle()
                    st.step(tt_(dst[0:DH, 2 * c, :], rot_t[0:DH, 0, :], rot_t[0:DH, 1, :], ALU.add))
                    tt_(dst[0:DH, 2 * c + 1, :], rot_t[DH:P, 0, :], rot_t[DH:P, 1, :], ALU.add).then_inc(rot_done, 1)
                    dve.wait_ge(rot_done, 4 * j + c + 1)

            dve.wait_ge(ssm_in, 32)
            a_re, a_im, ldt = (small[:, o:o + GROUPS] for o in (S_ARE, S_AIM, S_LDT))
            sl = [slot[:, i, :] for i in range(20)]

            def do(ins):
                st.step(ins)
                st.settle()

            def exp_parts(z, w, pm, f, k):
                do(ts_(f, z, -88.0, 88.7, ALU.max, ALU.min))
                do(ts_(k, f, 1.4426950408889634, 12582912.0, ALU.mult, ALU.add))
                do(ts_(k, k, -12582912.0, None, ALU.add))
                do(stt(f, k, -0.693359375, f, ALU.mult, ALU.add))
                do(stt(f, k, 2.12194440e-4, f, ALU.mult, ALU.add))
                do(ts_(pm, f, 1.0 / 5040, None, ALU.mult))
                for cf in (1.0 / 720, 1.0 / 120, 1.0 / 24, 1.0 / 6, 0.5, 1.0):
                    do(stt(pm, pm, cf, f, ALU.add, ALU.mult))
                do(ts_(slot_i, k, 127.0, None, ALU.add))
                do(ts_(slot_i, slot_i, 23, None, ALU.logical_shift_left))
                do(nc.vector.tensor_copy(w, slot_i.bitcast(F32)))

            dt, th, mag, magm1, s_, c_, cm1, ar, ai, gr, gi = sl[0:11]

            def cmul(dr, di, xr, xi, yr, yi, t1, t2):
                do(tt_(t1, xr, yr, ALU.mult))
                do(tt_(t2, xi, yi, ALU.mult))
                do(tt_(dr, t1, t2, ALU.subtract))
                do(tt_(t1, xr, yi, ALU.mult))
                do(tt_(t2, xi, yr, ALU.mult))
                do(tt_(di, t1, t2, ALU.add))

            def over_h(v):
                return v.unsqueeze(2).broadcast_to([P, GROUPS, GCH])

            cr, ci = phase[:, 0:6, :], phase[:, 6:12, :]

            def discretise_angles():
                exp_parts(ldt, sl[11], sl[12], sl[13], sl[14])
                do(stt(dt, sl[12], 1.0, sl[11], ALU.add, ALU.mult))
                do(tt_(sl[15], a_re, dt, ALU.mult))
                exp_parts(sl[15], sl[11], sl[12], sl[13], sl[14])
                do(tt_(magm1, sl[12], sl[11], ALU.mult))
                do(tt_(mag, magm1, sl[11], ALU.add))
                do(ts_(sl[13], sl[11], -1.0, None, ALU.add))
                do(tt_(magm1, magm1, sl[13], ALU.add))
                do(tt_(th, a_im, dt, ALU.mult))
                do(ts_(sl[14], th, 1.0 / (2 * math.pi), 12582912.0, ALU.mult, ALU.add))
                do(ts_(sl[14], sl[14], -12582912.0, None, ALU.add))
                for piece in (6.28125, 1.9340515e-3, 1.2556659e-6):
                    do(stt(th, sl[14], -piece, th, ALU.mult, ALU.add))
                do(ts_(th, th, -3.1415925, 3.1415925, ALU.max, ALU.min))
                ts_(sl[16], th, 0.5, None, ALU.mult).then_inc(ss_sin_in, 1)

            def discretise_inputs():
                dve.wait_ge(ss_sin, 2)
                do(stt(cm1, c_, -2.0, c_, ALU.mult, ALU.mult))
                do(ts_(c_, cm1, 1.0, None, ALU.add))
                do(tt_(ar, mag, c_, ALU.mult))
                do(tt_(ai, mag, s_, ALU.mult))
                do(tt_(sl[11], mag, cm1, ALU.mult))
                do(tt_(sl[11], sl[11], magm1, ALU.add))
                do(tt_(sl[12], a_re, a_re, ALU.mult))
                do(tt_(sl[13], a_im, a_im, ALU.mult))
                do(tt_(sl[12], sl[12], sl[13], ALU.add))
                do(nc.vector.reciprocal(sl[12], sl[12]))
                do(tt_(gr, sl[11], a_re, ALU.mult))
                do(tt_(sl[13], ai, a_im, ALU.mult))
                do(tt_(gr, gr, sl[13], ALU.add))
                do(tt_(gr, gr, sl[12], ALU.mult))
                do(tt_(gi, ai, a_re, ALU.mult))
                do(tt_(sl[13], sl[11], a_im, ALU.mult))
                do(tt_(gi, gi, sl[13], ALU.subtract))
                do(tt_(gi, gi, sl[12], ALU.mult))
                do(ts_(gi, gi, sgn[:, 0:1], None, ALU.mult))

                flat = flat1.rearrange("p (g h) -> p g h", g=GROUPS)
                do(tt_(bb1, b_ri, over_h(gr), ALU.mult))
                do(tt_(flat, b_ir, over_h(gi), ALU.mult))
                do(tt_(bb1, bb1, flat, ALU.add))
                do(tt_(bb2, b_ir, over_h(gr), ALU.mult))
                do(tt_(flat, b_ri, over_h(gi), ALU.mult))
                do(tt_(bb2, bb2, flat, ALU.subtract))
                do(ts_(sl[17][:, 0:1], sgn[:, 0:1], -1.0, None, ALU.mult))
                do(ts_(c_ri, c_ri, sl[17][:, 0:1], None, ALU.mult))
                do(ts_(c_ir, c_ir, sl[17][:, 0:1], None, ALU.mult))


            def power_tables():
                do(nc.vector.memset(pow_r[:, :, 0], 1.0))
                do(nc.vector.memset(pow_i[:, :, 0], 0.0))
                do(nc.vector.tensor_copy(pow_r[:, :, 1], ar))
                do(nc.vector.tensor_copy(pow_i[:, :, 1], ai))
                for n in (1, 2, 4):
                    t1 = flat1[:, 0:GROUPS * n].rearrange("p (g e) -> p g e", g=GROUPS)
                    t2 = flat2[:, 0:GROUPS * n].rearrange("p (g e) -> p g e", g=GROUPS)
                    br = pow_r[:, :, n:n + 1].broadcast_to([P, GROUPS, n])
                    bi = pow_i[:, :, n:n + 1].broadcast_to([P, GROUPS, n])
                    cmul(pow_r[:, :, n + 1:2 * n + 1], pow_i[:, :, n + 1:2 * n + 1],
                         pow_r[:, :, 1:n + 1], pow_i[:, :, 1:n + 1], br, bi, t1, t2)
                do(ts_(pow_i, pow_i, sgn[:, 0:1], None, ALU.mult))
                for e in range(L):
                    st.step(nc.vector.tensor_copy(prev_r[:, :, e], pow_r[:, :, L - 1 - e]))
                    st.step(nc.vector.tensor_copy(prev_i[:, :, e], pow_i[:, :, L - 1 - e]))
                cmul(sl[11], sl[12], c_, s_, c_, s_, sl[13], sl[14])
                cmul(sl[15], sl[16], sl[11], sl[12], sl[11], sl[12], sl[13], sl[14])
                cmul(cr[:, 0, :], ci[:, 0, :], sl[15], sl[16], sl[15], sl[16], sl[13], sl[14])
                for n in range(5):
                    cmul(cr[:, n + 1, :], ci[:, n + 1, :], cr[:, n, :], ci[:, n, :], cr[:, n, :], ci[:, n, :], sl[13], sl[14])
                for _ in range(3):
                    do(tt_(mag, mag, mag, ALU.mult))
                nc.vector.memset(sl[18][:, 0:1], 0.0).then_inc(ss_par, 1)

            split(2)
            discretise_angles()
            split(3)
            discretise_inputs()
            split(4)
            split(5)
            rotary(G_Q, 0, q_all)
            split(6)
            split(7)
            power_tables()
            rotary(G_K, 1, k_all)
            split(8)
            split(9)

            def rsqrt_newton(y, x, tmp, out):
                st.step(tt_(tmp, y, y, ALU.mult))
                st.settle()
                st.step(stt(tmp, tmp, -0.5, x, ALU.mult, ALU.mult))
                st.settle()
                return stt(out, tmp, 1.5, y, ALU.add, ALU.mult)

            def diff_head(r, first, last):
                def M_(i):
                    wait(dve, at_s, i + 1, r, 4)
                    for m in range(2):
                        col = 2 * (i % TT) + m
                        nc.vector.tensor_reduce(neg_max[:, col:col + 1], banks[2 * (i % 2) + m][:, 0:P * (i % TT + 1)],
                                                AX.X, ALU.max, negate=True).then_inc(at_m, 1)

                def D_(i):
                    wait(dve, at_e, 2 * i + 2, r, 8)
                    c, n = 2 * (i % TT), P * (i % TT + 1)
                    st.step(nc.vector.reciprocal(z_rec[:, c:c + 2], z_sum[:, c:c + 2]))
                    st.settle()
                    st.step(stt(coef[:, i % TT:i % TT + 1], z_sum[:, c:c + 1], z_rec[:, c + 1:c + 2], lam[:, 5:6],
                                ALU.mult, ALU.mult))
                    st.settle()
                    stt(e_buf[:, 2 * (i % 2), 0:n], e_buf[:, 2 * (i % 2) + 1, 0:n], coef[:, i % TT:i % TT + 1],
                        e_buf[:, 2 * (i % 2), 0:n], ALU.mult, ALU.add).then_inc(at_p, 1)

                def C_(i):
                    wait(dve, at_t, i + 1, r, 4)
                    wait(dve, at_v, i - 1, r, 4)
                    n = P * (i + 1)
                    nc.vector.tensor_copy(pt_buf[:, i % 2, 0:n], banks[4 + i % 2][:, 0:n]).then_inc(at_c, 1)

                def O_(i):
                    wait(dve, at_v, i + 1, r, 4)
                    if i >= 0:
                        wait(dve, at_x, 0, r, 1)
                    st.settle()
                    ts_(o_stage[:, i % TT, :], banks[6][:, 0:P], z_rec[:, 2 * (i % TT):2 * (i % TT) + 1], None,
                        ALU.mult).then_inc(at_o, 1)

                def N_(k):
                    wait(dve, at_nv, k + 1, r, 1)
                    st.step(ts_(rms[:, 2, :], rms[:, 0, :], 1.0 / (2 * DH), RMS_EPS, ALU.mult, ALU.add))
                    st.settle()
                    st.step(rsqrt_newton(rms[:, 1, :], rms[:, 2, :], rms[:, 3, :], rms[:, 4, :]))
                    st.settle()
                    for i in range(TT):
                        stt(o_stage[:, i, :], o_stage[:, i, :], rms[:, 4, i:i + 1], sub_g[:, bass.ds(r * P + k * P, P)],
                            ALU.mult, ALU.mult).then_inc(at_n, 1)

                def L_(k):
                    wait(dve, at_ns, k + 1, r, 1)
                    tt_(act_lo[:, bass.ds(r + k, 1), :], banks[7][:, :].unsqueeze(1),
                        act_hi[:, bass.ds(r + k, 1), :].bitcast(F32), ALU.subtract).then_inc(act_ready, 1)

                if first:
                    M_(0)
                    M_(1)
                    D_(0)
                for i in range(TT):
                    C_(i)
                    if i + 1 < TT or not last:
                        D_(i + 1)
                    if i + 2 < TT or not last:
                        M_(i + 2)
                    if i or not first:
                        O_(i - 1)
                    if i == 0 and not first:
                        N_(-1)
                    if i == 3 and not first:
                        L_(-1)
                if last:
                    O_(TT - 1)
                    N_(0)
                    L_(0)

            st.pipelined(4, 4 * 2 + 4, diff_head)

            def chunk_phases(b):
                ec, es, gs = e_cos[b % 2], e_sin[b % 2], slice(b * GB, (b + 1) * GB)
                do(nc.vector.memset(ec[:, :, 0], 1.0))
                do(nc.vector.memset(es[:, :, 0], 0.0))
                for lv in range(6):
                    n = 1 << lv
                    t1 = work1.rearrange("p g c -> p (g c)")[:, 0:GB * n].rearrange("p (g e) -> p g e", g=GB)
                    t2 = work2.rearrange("p g c -> p (g c)")[:, 0:GB * n].rearrange("p (g e) -> p g e", g=GB)
                    br = cr[:, lv, gs].unsqueeze(2).broadcast_to([P, GB, n])
                    bi = ci[:, lv, gs].unsqueeze(2).broadcast_to([P, GB, n])
                    cmul(ec[:, :, n:2 * n], es[:, :, n:2 * n], ec[:, :, 0:n], es[:, :, 0:n], br, bi, t1, t2)
                do(ts_(es, es, sgn[:, 0:1], -1.0, ALU.mult, ALU.mult))

            do(nc.vector.memset(r_tab[:, :, 0], 0.0))
            do(nc.vector.memset(x_buf[:, :, 0], 0.0))
            chunk_phases(0)
            for b in range(NB):
                ec, es = e_cos[b % 2], e_sin[b % 2]
                do(nc.vector.tensor_copy(r_tab[:, :, 1:NCH],
                                         mag[:, b * GB:(b + 1) * GB].unsqueeze(2).broadcast_to([P, GB, NCH - 1])))
                dve.wait_ge(ss_sw, b + 1)
                st.step(tt_(work1, s_buf, ec, ALU.mult))
                st.step(tt_(work2, banks[5][:, :].rearrange("p (g c) -> p g c", g=GB), es, ALU.mult))
                st.settle()
                do(tt_(work1, work1, work2, ALU.add))
                nc.vector.tensor_tensor_scan(y_buf.rearrange("p g c -> p (g c)"), r_tab.rearrange("p g c -> p (g c)"),
                                             work1.rearrange("p g c -> p (g c)"), 0.0, ALU.mult, ALU.add).then_inc(ss_scan, 1)
                dve.wait_ge(ss_scan, b + 1)
                if b + 1 < NB:
                    chunk_phases(b + 1)
                dve.wait_ge(ss_yw, b + 1)
                if b:
                    dve.wait_ge(ss_y, b)
                n = NCH - 1
                st.step(tt_(work1[:, :, 0:n], y_buf[:, :, 0:n], ec[:, :, 0:n], ALU.mult))
                st.step(tt_(work2[:, :, 0:n], banks[6][:, :].rearrange("p (g c) -> p g c", g=GB)[:, :, 0:n],
                            es[:, :, 0:n], ALU.mult))
                st.settle()
                tt_(x_buf[:, :, 1:NCH], work1[:, :, 0:n], work2[:, :, 0:n], ALU.subtract).then_inc(ss_x, 1)
            dve.wait_ge(ss_x, NB)

            for b in range(4):
                dve.wait_ge(y_in[b], 16 * GB)
                stt(y_t[:, b, :], u_t[:, b, :], small[:, S_D + b:S_D + b + 1], y_t[:, b, :],
                    ALU.mult, ALU.add).then_inc(glu_in, 1)
            for b in range(4):
                dve.wait_ge(glu_hi, b + 1)
                tt_(hid_lo[:, b, :], y_t[:, b, :], hid_hi[:, b, :].bitcast(F32), ALU.subtract).then_inc(glu_rhs, 1)
            for b in range(4):
                dve.wait_ge(glu_sig, b + 1)
                dve.wait_ge(glu_act, max(b - 1, 0)) if b > 1 else None
                yv = y_t[:, b, :].rearrange("p (i c) -> p c i", i=L)
                sv = tmp_a[:, b % 2, :].rearrange("p (i c) -> p c i", i=L)
                tt_(tmp_b[:, b % 2, :].rearrange("p (c i) -> p c i", i=L), yv, sv, ALU.mult).then_inc(glu_full, 1)
                dve.wait_ge(glu_act, b + 1)
                tt_(act_lo[:, 4 + b, :], tmp_b[:, b % 2, :], act_hi[:, 4 + b, :].bitcast(F32), ALU.subtract).then_inc(act_ready, 1)

            def evac_out(g):
                for i in range(TT):
                    h = g - (G_OUT0 if g < G_L1 else G_OUT1)
                    dve.wait_ge(pe_event, BANK_EVENT[g, i])
                    cs = slice(h * COLS, (h + 1) * COLS)
                    stt(acc[:, i, cs], resid[:, i, cs], ALPHA, bank_set(g)[i][:, :], ALU.mult, ALU.add).then_inc(evac_dve, 1)

            def out_projection(g0, n0):
                split(n0 + 2)
                evac_out(g0)
                split(n0 + 3)
                split(n0 + 4)
                evac_out(g0 + 1)
                split(n0 + 5)

            split(SL_OUT0 + 1)
            dve.wait_ge(x_in, 16)
            out_projection(G_OUT0, SL_OUT0)

            def layer_norm(l):
                dve.wait_ge(evac_dve, EVAC_DVE_LN[l])
                for i in range(TT):
                    for h in range(2):
                        st.step(nc.vector.bn_stats(stats[:, i, 6 * h:6 * h + 6], acc[:, i, h * 512:(h + 1) * 512]))
                st.settle()
                for i in range(TT):
                    nc.vector.bn_aggr(mv[:, i, :], stats[:, i, :]).then_inc(ln_var, 1)
                dve.wait_ge(ln_var, 4 * l + 4)
                dve.wait_ge(ln_seed, 2 * l + 2)
                do(ts_(lns[:, 2, :], mv[:, :, 1], LN_EPS, None, ALU.add))
                do(rsqrt_newton(lns[:, 1, :], lns[:, 2, :], lns[:, 3, :], lns[:, 4, :]))
                for i in range(TT):
                    ts_(resid[:, i, :], acc[:, i, :], mv[:, i, 0:1], lns[:, 4, i:i + 1],
                        ALU.subtract, ALU.mult).then_inc(xhat_ready, 1)

            def norm_split(l):
                for k in range(KB):
                    dve.wait_ge(act_hi_done, 8 * l + k + 1)
                    do(ts_(tmp_a[:, k % 2, :], norm_bank(k)[:, :], small[:, S_LNG + 8 * l + k:S_LNG + 8 * l + k + 1],
                           small[:, S_LNB + 8 * l + k:S_LNB + 8 * l + k + 1], ALU.mult, ALU.add))
                    tt_(act_lo[:, k, :], tmp_a[:, k % 2, :], act_hi[:, k, :].bitcast(F32), ALU.subtract).then_inc(act_ready, 1)

            def mlp(g0, n0, h0, a0, r, last=False):
                for c in range(2):
                    g, n = g0 + 3 * c, n0 + 4 * c
                    split(n + 2, r)
                    for k in range(4):
                        wait(dve, relu_done, h0 + 4 * c + k + 1, r, 8)
                        tt_(tmp_b[:, k % 2, :], tmp_a[:, k % 2, :], tmp_a[:, k % 2, :], ALU.mult).then_inc(sq_done, 1)
                        wait(dve, sq_done, h0 + 4 * c + k + 1, r, 8)
                        wait(dve, hid_hi_done, h0 + 4 * c + k + 1, r, 8)
                        tt_(hid_lo[:, k, :], tmp_b[:, k % 2, :], hid_hi[:, k, :].bitcast(F32),
                            ALU.subtract).then_inc(hid_ready, 1)
                    split(n + 3, r)
                    for half in range(2):
                        if not (last and c == 1):
                            split(n + 4 + half, r)
                        if isinstance(r, int) and r == 0 and c == 0 and half == 0:
                            dve.wait_ge(acc_init, 4 + h0 // 8)
                        for i in range(TT):
                            wait(dve, pe_event, BANK_EVENT[g + 1 + half, i], r, 2 * CHUNK_EVENTS)
                            cs = slice(half * COLS, (half + 1) * COLS)
                            tt_(acc[:, i, cs], acc[:, i, cs], bank_set(g + 1 + half)[i][:, :], ALU.add).then_inc(evac_dve, 1)

            layer_norm(0)
            norm_split(0)
            mlp(G_MLP0, SL_MLP0, 0, 0, 0)
            with dve.Fori(1, 4) as r:
                mlp(G_MLP0, SL_MLP0, 0, 0, r)
            layer_norm(1)
            norm_split(1)

            dve.wait_ge(gate_w_hi, 1)
            tt_(gw_lo[:, :, :], gate_w[:, :, :], gw_hi[:, :, :].bitcast(F32), ALU.subtract).then_inc(gate_w_split, 2)
            dve.wait_ge(gate_mm, 1)
            bf = small[:, S_BF:S_BF + 16].unsqueeze(1).broadcast_to([P, TT, 16])
            do(tt_(logf[:, 0, :, :], banks[0][:, 0:64].rearrange("p (a h) -> p a h", a=TT), bf, ALU.add))
            stt(logf[:, 1, :, :], logf[:, 0, :, :], -1.0, logf[:, 0, :, :], ALU.mult, ALU.max).then_inc(gate_z, 1)
            dve.wait_ge(gate_z, 3)
            stt(logf[:, 3, :, :], logf[:, 0, :, :], 0.0, logf[:, 2, :, :], ALU.min, ALU.subtract).then_inc(gate_log, 1)
            dve.wait_ge(gate_mm, 2)
            nc.vector.tensor_copy(fcum[0:16, 0, :], banks[1][0:16, :]).then_inc(gate_cum, 1)
            ts_(fcum[0:16, 1, :], banks[1][0:16, :], -1.0, None, ALU.mult).then_inc(gate_cum, 1)

            def fox_pair(half, r, first, last):
                u0 = 32 * half

                def M_(j):
                    wait(dve, fx_s, u0 + j + 1, r, 8)
                    nc.vector.tensor_reduce(neg_max[:, j % 8:j % 8 + 1], banks[j % 4][:, 0:P * (j % TT + 1)],
                                            AX.X, ALU.max, negate=True).then_inc(fx_m, 1)

                def C_(j):
                    wait(dve, fx_t, u0 + j + 1, r, 8)
                    wait(dve, fx_v, u0 + j - 1, r, 8)
                    n = P * (j % TT + 1)
                    nc.vector.tensor_copy(pt_buf[:, j % 2, 0:n], banks[4 + j % 2][:, 0:n]).then_inc(fx_c, 1)

                def O_(j):
                    wait(dve, fx_v, u0 + j + 1, r, 8)
                    if j >= 0:
                        wait(dve, fx_x, 4 * half, r, 1)
                    st.settle()
                    cs = slice((j // TT) % 2 * DH, ((j // TT) % 2 + 1) * DH)
                    ts_(o_stage[:, j % TT, cs], banks[6][:, 0:DH], z_rec[:, j % 8:j % 8 + 1], None,
                        ALU.mult).then_inc(fx_o, 1)

                def L_(k):
                    wait(dve, fx_h, 4 * half + k + 1, r, 1)
                    hi, lo, b0 = (hid_hi, hid_lo, 0) if half == 0 else (act_hi, act_lo, 4)
                    tt_(lo[:, bass.ds(r + (k + b0), 1), :], banks[7][:, :].unsqueeze(1),
                        hi[:, bass.ds(r + (k + b0), 1), :].bitcast(F32), ALU.subtract).then_inc(act_ready, 1)

                if first:
                    for j in range(3):
                        M_(j)
                for j in range(8):
                    C_(j)
                    if j or not first:
                        O_(j - 1)
                    st.step(nc.vector.reciprocal(z_rec[:, j:j + 1], z_sum[:, j:j + 1]))
                    if j + 3 < 8 or not last:
                        M_(j + 3)
                    if j == 3 and not first:
                        L_(-1)
                if last:
                    O_(7)
                    L_(0)

            for half in range(2):
                n0, g0 = SL_L1 + 6 * half, G_L1 + 3 * half
                split(n0 + 2)
                split(n0 + 3)
                split(n0 + 4)
                for c in range(4):
                    dve.wait_ge(pe_event, BANK_EVENT[g0 + 1, c])
                    st.step(nc.vector.tensor_copy(k_all[0:DH, 2 * c, :], bank_set(g0 + 1)[c][0:DH, :]))
                    nc.vector.tensor_copy(k_all[0:DH, 2 * c + 1, :], bank_set(g0 + 1)[c][DH:P, :]).then_inc(evac_k1, 1)
                split(n0 + 5)
                split(n0 + 6)
                split(n0 + 7)
                st.settle()
                st.pipelined(4, 8, lambda r, first, last: fox_pair(half, r, first, last))

            dve.wait_ge(resid_ready, 4)
            out_projection(G_OUT1, SL_OUT1)
            layer_norm(2)
            norm_split(2)
            mlp(G_MLP1, SL_MLP1, 32, 0, 0)
            with dve.Fori(1, 3) as r:
                mlp(G_MLP1, SL_MLP1, 32, 0, r)
            mlp(G_MLP1, SL_MLP1, 32, 0, 3, last=True)
            layer_norm(3)
            dve.wait_ge(row_in, 32 * 4)
            for i in range(TT):
                dve.wait_ge(xhat_ready, 12 + i + 1)
                do(tt_(acc[:, i, :], resid[:, i, :], ln_row[:, 0, :], ALU.mult))
                tt_(acc[:, i, :], acc[:, i, :], ln_row[:, 1, :], ALU.add).then_inc(out_ready, 1)

        @block.scalar
        def _(sc):
            act = nc.scalar.activation

            def split(n, r=0):
                if isinstance(r, int):
                    sc.wait_ge(slab_landed[n % 2], 16 * ((n + 8 * r) // 2 + 1))
                else:
                    wait(sc, slab_landed[n % 2], 16 * (n // 2 + 1), r, 64)
                if n >= 2:
                    wait(sc, pe_event, SLAB_EVENT[n - 2], r, 2 * CHUNK_EVENTS)
                act(slab_hi[:, n % 2, :, :], slab_raw[:, n % 2, :, :], ACT.Copy).then_inc(slab_hi_ready, 1)

            for kb in range(2):
                ks = slice(4 * kb, 4 * kb + 4)
                sc.wait_ge(xt_in[kb], 16)
                act(act_hi[:, ks, :], xt[:, ks, :], ACT.Copy).then_inc(stem_hi, 1)
                split(kb)
            sc.wait_ge(lam_sum, 1)
            act(lam[:, 2:4], lam[:, 0:2], ACT.Exp).then_inc(lam_exp, 1)
            split(2)
            for c in range(4):
                sc.wait_ge(pe_event, BANK_EVENT[G_U, c])
                act(u_t[:, c, :].rearrange("p (j n) -> p j n", j=L),
                    bank_set(G_U)[c][:, :].rearrange("p (n j) -> p j n", j=L), ACT.Copy).then_inc(u_ready, 1)
            split(3)
            sc.wait_ge(ss_sin_in, 1)
            act(slot[:, 4, :], slot[:, 1, :], ACT.Sin).then_inc(ss_sin, 1)
            act(slot[:, 5, :], slot[:, 16, :], ACT.Sin).then_inc(ss_sin, 1)
            split(4)
            sc.wait_ge(act_ready, 8)
            for c in range(4):
                sc.wait_ge(pe_event, BANK_EVENT[G_Q, c])
                act(rot_x[:, c, :], bank_set(G_Q)[c][:, :], ACT.Copy, scale=DH ** -0.5).then_inc(rot_copied, 1)
            split(5)
            split(6)
            for c in range(4):
                sc.wait_ge(pe_event, BANK_EVENT[G_K, c])
                sc.wait_ge(rot_done, c + 1)
                act(rot_x[:, c, :], bank_set(G_K)[c][:, :], ACT.Copy).then_inc(rot_copied, 1)
            split(7)
            split(8)
            for i in range(TT):
                sc.wait_ge(pe_event, BANK_EVENT[G_V, i])
                act(v_nat[:, i, :], bank_set(G_V)[i][:, :], ACT.Copy).then_inc(evac_act, 1)
            split(9)

            def diff_head(r, first, last):
                def E_(i):
                    n = P * (i % TT + 1)
                    for m in range(2):
                        wait(sc, at_m, 2 * i + m + 1, r, 8)
                        wait(sc, at_t, i - 1, r, 4)
                        col = 2 * (i % TT) + m
                        act(e_buf[:, 2 * (i % 2) + m, 0:n], banks[2 * (i % 2) + m][:, 0:n], ACT.Exp,
                            bias=neg_max[:, col:col + 1], accum_out=z_sum[:, col:col + 1]).then_inc(at_e, 1)

                def Q_(i):
                    wait(sc, at_o, i + 1, r, 4)
                    wait(sc, at_sq, i, r, 4)
                    act(sq_scr[:, :], o_stage[:, i % TT, :], ACT.Square,
                        accum_out=rms[:, 0, i % TT:i % TT + 1]).then_inc(at_sq, 1)

                def R_(k):
                    wait(sc, at_sq, TT * (k + 1), r, TT)
                    act(rms[:, 1, :], rms[:, 0, :], ACT.Ln, bias=RMS_EPS, scale=1.0 / (2 * DH)).then_inc(at_w, 1)
                    wait(sc, at_w, k + 1, r, 1)
                    act(rms[:, 1, :], rms[:, 1, :], ACT.Exp, scale=-0.5).then_inc(at_nv, 1)

                def H_(k):
                    wait(sc, at_x, k + 1, r, 1)
                    act(act_hi[:, bass.ds(r + k, 1), :], banks[7][:, :].unsqueeze(1), ACT.Copy).then_inc(at_ns, 1)

                if first:
                    E_(0)
                    E_(1)
                for i in range(TT):
                    if i or not first:
                        Q_(i - 1)
                    if i == 0 and not first:
                        R_(-1)
                    if i == 2 and not first:
                        H_(-1)
                    if i + 2 < TT or not last:
                        E_(i + 2)
                if last:
                    Q_(TT - 1)
                    R_(0)
                    H_(0)

            diff_head(0, True, False)
            with sc.Fori(1, 3) as r:
                diff_head(r, False, False)
            diff_head(3, False, True)

            def toeplitz_out(b):
                sc.wait_ge(ss_t, 2 * b + 1)
                for h in range(2):
                    act(t_mat[:, 4 * h:4 * h + 4, :].rearrange("p g n -> p (g n)"), banks[h][:, :],
                        ACT.Copy).then_inc(ss_out_t, 1)

            def inputs_out(b):
                sc.wait_ge(ss_t, 2 * b + 2)
                for h in range(2):
                    act(bst_mat[:, 4 * h:4 * h + 4, :].rearrange("p g n -> p (g n)"), banks[2 + h][:, :],
                        ACT.Copy).then_inc(ss_tc, 1)

            def chunk_inputs(b):
                sc.wait_ge(ss_s, b + 1)
                act(s_buf[:, :, :].rearrange("p g c -> p (g c)"), banks[4][:, :], ACT.Copy).then_inc(ss_sc, 1)

            toeplitz_out(0)
            inputs_out(0)
            chunk_inputs(0)
            for b in range(NB):
                if b + 1 < NB:
                    inputs_out(b + 1)
                    chunk_inputs(b + 1)
                sc.wait_ge(ss_y, b + 1)
                if b:
                    sc.wait_ge(y_out, 16 * b)
                act(y8[:, :, :].rearrange("p g c -> p (g c)"), banks[7][:, :], ACT.Copy).then_inc(ss_out, 1)
                if b + 1 < NB:
                    toeplitz_out(b + 1)

            for b in range(4):
                sc.wait_ge(glu_in, b + 1)
                act(y_t[:, b, :], y_t[:, b, :], ACT.Gelu_apprx_tanh).then_inc(glu_y, 1)
            for b in range(4):
                sc.wait_ge(glu_y, b + 1)
                act(hid_hi[:, b, :], y_t[:, b, :], ACT.Copy).then_inc(glu_hi, 1)
            for b in range(4):
                sc.wait_ge(pe_event, BANK_EVENT[G_GLU, b])
                if b > 1:
                    sc.wait_ge(glu_full, b - 1)
                act(tmp_a[:, b % 2, :], bank_set(G_GLU)[b][:, :], ACT.Sigmoid,
                    bias=small[:, S_GLUB + b:S_GLUB + b + 1]).then_inc(glu_sig, 1)
                sc.wait_ge(glu_full, b + 1)
                act(act_hi[:, 4 + b, :], tmp_b[:, b % 2, :], ACT.Copy).then_inc(glu_act, 1)
            for n in range(SL_OUT0 + 1, SL_MLP0 + 2):
                split(n)

            def norm_seed(l):
                sc.wait_ge(ln_var, 4 * l + 4)
                act(lns[:, 0, :], mv[:, :, 1], ACT.Ln, bias=LN_EPS).then_inc(ln_seed, 1)
                sc.wait_ge(ln_seed, 2 * l + 1)
                act(lns[:, 1, :], lns[:, 0, :], ACT.Exp, scale=-0.5).then_inc(ln_seed, 1)

            def norm_hi(l):
                for k in range(KB):
                    sc.wait_ge(ln_psum, 8 * l + k + 1)
                    act(act_hi[:, k, :], norm_bank(k)[:, :], ACT.Identity,
                        scale=small[:, S_LNG + 8 * l + k:S_LNG + 8 * l + k + 1],
                        bias=small[:, S_LNB + 8 * l + k:S_LNB + 8 * l + k + 1]).then_inc(act_hi_done, 1)

            def mlp(g0, n0, h0, r, last=False):
                for c in range(2):
                    g, n = g0 + 3 * c, n0 + 4 * c
                    split(n + 2, r)
                    for k in range(4):
                        m = h0 + 4 * c + k + 1
                        wait(sc, pe_event, BANK_EVENT[g, k], r, 2 * CHUNK_EVENTS)
                        wait(sc, sq_done, m - 2, r, 8)
                        wait(sc, hid_hi_done, m - 2, r, 8)
                        act(tmp_a[:, k % 2, :], bank_set(g)[k][:, :], ACT.Relu).then_inc(relu_done, 1)
                        wait(sc, relu_done, m, r, 8)
                        act(hid_hi[:, k, :], tmp_a[:, k % 2, :], ACT.Square).then_inc(hid_hi_done, 1)
                    split(n + 3, r)
                    if not (last and c == 1):
                        split(n + 4, r)
                        split(n + 5, r)

            norm_seed(0)
            norm_hi(0)
            mlp(G_MLP0, SL_MLP0, 0, 0)
            with sc.Fori(1, 4) as r:
                mlp(G_MLP0, SL_MLP0, 0, r)
            norm_seed(1)
            norm_hi(1)

            sc.wait_ge(gate_in, 16)
            act(gw_hi[:, :, :], gate_w[:, :, :], ACT.Copy).then_inc(gate_w_hi, 1)
            sc.wait_ge(gate_z, 1)
            act(logf[:, 2, :, :], logf[:, 1, :, :], ACT.Exp, scale=-1.0).then_inc(gate_z, 1)
            sc.wait_ge(gate_z, 2)
            act(logf[:, 2, :, :], logf[:, 2, :, :], ACT.Ln, bias=1.0).then_inc(gate_z, 1)

            def fox_pair(half, r, first, last):
                u0 = 32 * half

                def H_(k):
                    wait(sc, fx_x, 4 * half + k + 1, r, 1)
                    hi, b0 = (hid_hi, 0) if half == 0 else (act_hi, 4)
                    act(hi[:, bass.ds(r + (k + b0), 1), :], banks[7][:, :].unsqueeze(1), ACT.Copy).then_inc(fx_h, 1)

                for j in range(8):
                    n = P * (j % TT + 1)
                    wait(sc, fx_m, u0 + j + 1, r, 8)
                    wait(sc, fx_t, u0 + j - 3, r, 8)
                    act(e_buf[:, j % 4, 0:n], banks[j % 4][:, 0:n], ACT.Exp, bias=neg_max[:, j:j + 1],
                        accum_out=z_sum[:, j:j + 1]).then_inc(fx_e, 1)
                    if j == 4 and not first:
                        H_(-1)
                if last:
                    H_(0)

            for half in range(2):
                n0, g0 = SL_L1 + 6 * half, G_L1 + 3 * half
                split(n0 + 2)
                for c in range(4):
                    sc.wait_ge(pe_event, BANK_EVENT[g0, c])
                    act(q_all[0:DH, 2 * c, :], bank_set(g0)[c][0:DH, :], ACT.Copy, scale=DH ** -0.5).then_inc(act_step, 1)
                    act(q_all[0:DH, 2 * c + 1, :], bank_set(g0)[c][DH:P, :], ACT.Copy, scale=DH ** -0.5).then_inc(evac_q1, 1)
                split(n0 + 3)
                split(n0 + 4)
                split(n0 + 5)
                split(n0 + 6)
                for i in range(TT):
                    sc.wait_ge(pe_event, BANK_EVENT[g0 + 2, i])
                    act(v_nat[:, i, :], bank_set(g0 + 2)[i][:, :], ACT.Copy).then_inc(evac_act, 1)
                split(n0 + 7)
                fox_pair(half, 0, True, False)
                with sc.Fori(1, 3) as r:
                    fox_pair(half, r, False, False)
                fox_pair(half, 3, False, True)
            for n in range(SL_OUT1 + 2, SL_MLP1 + 2):
                split(n)
            norm_seed(2)
            norm_hi(2)
            mlp(G_MLP1, SL_MLP1, 32, 0)
            with sc.Fori(1, 3) as r:
                mlp(G_MLP1, SL_MLP1, 32, r)
            mlp(G_MLP1, SL_MLP1, 32, 3, last=True)
            norm_seed(3)

        @block.gpsimd
        def _(pool):
            st = Steps(pool, pool_step)

            def q_slots(q_sem, used, per_used, rows, used0, r):
                for m in range(2):
                    wait(pool, used, used0[m], r, per_used)
                    nc.gpsimd.tensor_copy(q_slot[0:rows, m, :].unsqueeze(1),
                                          q_all[0:rows, bass.ds(r * 2 + m, 1), :]).then_inc(q_sem, 1)

            pool.wait_ge(rot_done, 8)
            q_slots(at_q, at_s, 4, DH, (0, 0), 0)
            with pool.Fori(1, 4) as r:
                q_slots(at_q, at_s, 4, DH, (0, 0), r)

            def power_product(pr, pi, m1, m2, out):
                full = [P, GB, L, GCH]
                pool.wait_ge(pool_step, st.count)
                for prod, pw, m in ((prod1, pr, m1), (prod2, pi, m2)):
                    st.step(nc.gpsimd.tensor_tensor(prod, pw.unsqueeze(3).broadcast_to(full),
                                                    m.unsqueeze(2).broadcast_to(full), ALU.mult))
                st.settle()
                return nc.gpsimd.tensor_tensor(out, prod1, prod2, ALU.add)

            pool.wait_ge(act_ready, 12)
            pool.wait_ge(ss_par, 1)
            st.step(nc.gpsimd.memset(f_tab[:, :, L:M15, :], 0.0))
            for b in range(NB):
                gs = slice(b * GB, (b + 1) * GB)
                if b:
                    pool.wait_ge(ss_t, 2 * b)
                power_product(prev_r[:, gs, :], prev_i[:, gs, :], bb1[:, gs, :], bb2[:, gs, :],
                              f_tab[:, :, 0:L, :]).then_inc(ss_f, 1)
                if b >= 2:
                    pool.wait_ge(ss_y, b - 1)
                pool.wait_ge(ss_f, b + 1)
                power_product(pow_r[:, gs, 1:L + 1], pow_i[:, gs, 1:L + 1], c_ri[:, gs, :], c_ir[:, gs, :],
                              ca_mat[b % 2]).then_inc(ss_ca, 1)
                pool.wait_ge(ss_ca, b + 1)

            def rows_in(l):
                st.settle()
                for j, name in enumerate(("g", "b")):
                    row = t["ln%d_%s" % (1 + l % 2, name)][l // 2:l // 2 + 1, :].broadcast_to([P, D])
                    pool.dma_start(ln_row[:, j, :], row).then_inc(row_in, 16)
                pool.wait_ge(row_in, 32 * (l + 1))

            def scaled_residual(l):
                rows_in(l)
                st.step(nc.gpsimd.tensor_scalar(ln_row[:, :, :], ln_row[:, :, :], ALPHA, None, ALU.mult))
                st.settle()
                for i in range(TT):
                    pool.wait_ge(xhat_ready, 4 * l + i + 1)
                    st.step(nc.gpsimd.tensor_tensor(acc[:, i, :], resid[:, i, :], ln_row[:, 0, :], ALU.mult))
                    st.settle()
                    nc.gpsimd.tensor_tensor(acc[:, i, :], acc[:, i, :], ln_row[:, 1, :], ALU.add).then_inc(acc_init, 1)

            pool.wait_ge(act_ready, 16)
            scaled_residual(0)
            pool.wait_ge(acc_init, 4)
            rows_in(1)
            pool.wait_ge(ln_psum, 16)
            for i in range(TT):
                st.step(nc.gpsimd.tensor_tensor(resid[:, i, :], resid[:, i, :], ln_row[:, 0, :], ALU.mult))
                st.settle()
                nc.gpsimd.tensor_tensor(resid[:, i, :], resid[:, i, :], ln_row[:, 1, :], ALU.add).then_inc(resid_ready, 1)
            pool.wait_ge(resid_ready, 4)
            nc.gpsimd.memset(q_all[DH:DH + 2, :, :], 1.0).then_inc(ones_set, 1)
            nc.gpsimd.memset(k_all[DH:DH + 2, :, :], 1.0).then_inc(ones_set, 1)
            for half in range(2):
                pool.wait_ge(evac_q1, 4 * half + 4)
                pool.wait_ge(decay_in, 32 * half + 32)
                q_slots(fx_q, fx_s, 8, DH + 2, (32 * half, 32 * half), 0)
                with pool.Fori(1, 4) as r:
                    q_slots(fx_q, fx_s, 8, DH + 2, (32 * half - 4, 32 * half), r)
            scaled_residual(2)
            pool.wait_ge(acc_init, 8)
            rows_in(3)


ROPE_THETA = 10000.0


def constants():
    c = np.zeros((P, C_N), np.float32)
    i = np.arange(P)
    c[i, C_ID + i] = 1
    c[i, C_SW64 + (i + 64) % P] = 1
    c[i, C_SW32 + (i ^ 32)] = 1
    c[:, C_TRI:C_TRI + S] = np.arange(S)[None, :] >= i[:, None]
    c[:, C_MASK0:C_MASK0 + P] = np.where((i[None, :] // DH) > (i[:, None] // DH), NEG, 0)
    c[:, C_MASK1:C_MASK1 + P] = np.where(i[None, :] > i[:, None], NEG, 0)
    inv = (np.float32(ROPE_THETA) ** (-np.arange(0, DH, 2, dtype=np.float32) / np.float32(DH))).astype(np.float32)
    ang = np.arange(S, dtype=np.float32)[:, None] * inv[None, :]
    cos, sin = np.cos(ang).T.astype(np.float32), np.sin(ang).T.astype(np.float32)
    c[:, C_CC:C_CC + S] = np.tile(cos, (4, 1))
    c[:, C_SS:C_SS + S] = np.concatenate([-sin, sin, -sin, sin])
    c[:, C_SGN] = np.where(i < 64, -1, 1)
    return c


def kernel(**inputs):
    import numpy as _np
    import concourse.bacc as _bacc
    from concourse import mybir as _mybir
    from concourse.bass_utils import run_bass_kernel_spmd as _run

    nc = _bacc.Bacc("TRN2", target_bir_lowering=False, num_devices=1)
    a = {k: _np.asarray(v) for k, v in inputs.items()}

    def cols(v):
        return v.reshape(-1, P).T

    def per_state(v):
        return _np.concatenate([v.T, v.T])

    ln_g = _np.stack([a["ln1_g"], a["ln2_g"]], 1)
    ln_b = _np.stack([a["ln1_b"], a["ln2_b"]], 1)
    small = _np.concatenate([
        cols(ln_g), cols(ln_b), per_state(a["ssm_a_re"][0]), per_state(a["ssm_a_im"][0]),
        _np.broadcast_to(a["ssm_log_dt"][0], (P, GROUPS)), cols(a["ssm_d"][0]), cols(a["ssm_glu_b"][0]),
        _np.broadcast_to(a["fox_b_f"][0], (P, 16))], axis=1)
    b_re, b_im = (a[n][0].transpose(1, 0, 2).reshape(NSTATE, -1) for n in ("ssm_b_re", "ssm_b_im"))
    c_re, c_im = (a[n][0].transpose(2, 0, 1).reshape(NSTATE, -1) for n in ("ssm_c_re", "ssm_c_im"))
    ssm_bc = _np.stack([_np.concatenate(p) for p in ((b_re, b_im), (b_im, b_re), (c_re, c_im), (c_im, c_re))], 1)
    arrays = {
        "x": a["x"], "xt": a["x"][0].T.reshape(KB, P, S).transpose(1, 0, 2), "const": constants(), "small": small,
        "ssm_bc": ssm_bc, "ab_w_in": a["ab_w_in"][0], "ab_lambda": a["ab_lambda"], "ab_subln_g": a["ab_subln_g"],
        "ssm_glu_w": a["ssm_glu_w"][0], "ab_w_out": a["ab_w_out"][0], "fox_w_in": a["fox_w_in"][0],
        "fox_w_out": a["fox_w_out"][0], "ln1_g": a["ln1_g"], "ln1_b": a["ln1_b"], "ln2_g": a["ln2_g"],
        "ln2_b": a["ln2_b"], "ffn_w1": a["ffn_w1"], "ffn_w2": a["ffn_w2"],
    }
    arrays = {k: _np.ascontiguousarray(v) for k, v in arrays.items()}
    t = {k: nc.dram_tensor("in_" + k, v.shape, _mybir.dt.from_np(v.dtype), kind="ExternalInput").ap()
         for k, v in arrays.items()}
    t["u_scratch"] = nc.dram_tensor("u_scratch", (GROUPS * GCH, S), _mybir.dt.float32).ap()
    t["y_scratch"] = nc.dram_tensor("y_scratch", (NB, P, GB * NCH), _mybir.dt.float32).ap()
    t["out"] = nc.dram_tensor("out_0", (S, D), _mybir.dt.float32, kind="ExternalOutput").ap()
    trunk(nc, t)
    r = _run(nc, [{"in_" + k: v for k, v in arrays.items()}], core_ids=[0])
    return r.results[0]["out_0"].reshape(1, S, D)
```

```python
import math
from contextlib import ExitStack

import numpy as np
import concourse.bass as bass
from concourse import mybir

F32 = mybir.dt.float32
F32R = mybir.dt.float32r
BF16 = mybir.dt.bfloat16
I32 = mybir.dt.int32
ALU = mybir.AluOpType
ACT = mybir.ActivationFunctionType
AX = mybir.AxisListType

P = 128
D = 1024
S = 512
KB = D // P
TT = S // P
D_FF = 4 * D
SLAB_K = 4
COLS = 512
HEADS_STAGE = 8
DH = 64
ALPHA = 4.0 ** 0.25
LN_EPS = 1e-5
RMS_EPS = 1e-6
LAM_INIT = 0.8 - 0.6 * math.exp(-0.3 * 0)
NEG = -1.0e30
GROUPS = 32
GCH = 16
NSTATE = 64
L = 8
NCH = S // L
GB = 8
NB = GROUPS // GB
KD = 2 * L - 1

C_ID, C_SW64, C_SW32, C_MASK0, C_MASK1, C_CC, C_SS, C_SGN = 0, 128, 256, 384, 512, 640, 1152, 1664
C_N = 1665
S_LNG, S_LNB, S_ARE, S_AIM, S_LDT, S_D, S_GLUB, S_BF = 0, 32, 64, 96, 128, 160, 164, 168
S_N = 169

SL_U, SL_Q, SL_K, SL_V, SL_OUT0, SL_GLU, SL_MLP0 = 0, 2, 4, 6, 8, 9, 13
SL_L1 = 45
SL_OUT1, SL_MLP1, SL_END = 57, 61, 93
G_U, G_Q, G_K, G_V, G_GLU, G_OUT0, G_MLP0, G_L1, G_OUT1, G_MLP1 = 0, 1, 2, 3, 4, 5, 7, 31, 37, 39


def event_table():
    order = [(g, 2 * g + kh, kh) for g in (G_U, G_Q, G_K, G_V) for kh in range(2)]
    order += [(G_OUT0, SL_OUT0, 0), (G_GLU, SL_GLU, 1), (G_OUT0, SL_OUT0 + 2, 1)]
    order += [(G_OUT0 + 1, SL_OUT0 + 3, 0), (G_OUT0 + 1, SL_OUT0 + 4, 1)]
    for sl_mlp, g_mlp in ((SL_MLP0, G_MLP0), (SL_MLP1, G_MLP1)):
        if sl_mlp == SL_MLP1:
            order += [(G_L1 + j, SL_L1 + 2 * j + kh, kh) for j in range(8) for kh in range(2)]
        for c in range(8):
            n, g = sl_mlp + 4 * c, g_mlp + 3 * c
            order += [(g, n, 0), (g, n + 1, 1), (g + 1, n + 2, 1), (g + 2, n + 3, 1)]
    slab_event, bank_event, e = {}, {}, 0
    for g, n, ends in order:
        if ends:
            for t in range(4):
                bank_event[g, t] = e + t + 1
        e += 4 if ends else 1
        slab_event[n] = e
    assert sorted(slab_event) == list(range(SL_END))
    return slab_event, bank_event


SLAB_EVENT, BANK_EVENT = event_table()
EVAC_DVE_LN = [8, 72, 80, 144]
CHUNK_EVENTS = 13


def wait(eng, sem, value, r=0, per=0):
    if isinstance(r, int):
        if value + per * r > 0:
            eng.wait_ge(sem, value + per * r)
    else:
        eng.wait_ge(sem, r * per + value)


def trunk(nc, t):
    with ExitStack() as ctx:
        def sb(name, shape, dt=F32):
            return ctx.enter_context(nc.sbuf_tensor(name, shape, dt))

        def sem(name):
            return ctx.enter_context(nc.semaphore(name))

        slab_raw = sb("slab_raw", [P, 2, SLAB_K, COLS])

        def float32_over(name, n):
            with nc.sbuf_tensor(name, [P, n], F32) as storage:
                return storage

        ring_f32 = float32_over("ring_f32", 4 * SLAB_K * COLS)
        slab_hi = sb("slab_hi", [P, 2, SLAB_K, COLS], F32R)
        slab_lo = sb("slab_lo", [P, 2, SLAB_K, COLS], F32R)
        act_f32 = float32_over("act_f32", 2 * KB * S)
        act_hi = sb("act_hi", [P, KB, S], F32R)
        act_lo = sb("act_lo", [P, KB, S], F32R)
        hid_f32 = float32_over("hid_f32", 8 * S)
        hid_hi = sb("hid_hi", [P, 4, S], F32R)
        hid_lo = sb("hid_lo", [P, 4, S], F32R)
        resid = sb("resid", [P, TT, D])
        acc = sb("acc", [P, TT, D])
        const = sb("const", [P, C_MASK0])
        consth = sb("consth", [P, 3, P], BF16)
        sgn = sb("sgn", [P, 1])
        small = sb("small", [P, S_N])
        stats = sb("stats", [P, TT, 12])
        mv = sb("mv", [P, TT, 2])
        lns = sb("lns", [P, 5, TT])
        gw_hi = sb("gw_hi", [P, KB, 16], F32R)
        gw_lo = sb("gw_lo", [P, KB, 16], F32R)
        arena = sb("arena", [P, 17920])

        def view(off, *shape):
            n = int(np.prod(shape))
            assert off + n <= 17920
            v = arena[:, off:off + n]
            if len(shape) == 2:
                return v.rearrange("p (a b) -> p a b", a=shape[0])
            if len(shape) == 3:
                return v.rearrange("p (a b c) -> p a b c", a=shape[0], b=shape[1])
            return v

        ident = const[:, C_ID:C_ID + P]
        swap64 = const[:, C_SW64:C_SW64 + P]
        swap32 = const[:, C_SW32:C_SW32 + P]
        ident_h, mask_h = consth[:, 0, :], [consth[:, 1, :], consth[:, 2, :]]

        q_all = view(0, 8, S)
        k_all = view(4096, 8, S)
        e_buf = view(8192, 4, S)
        pt_buf = view(10240, 2, S)
        q_slot = view(11264, 2, S)
        o_stage = view(12288, TT, P)
        sub_g = view(12800, S)
        neg_max = view(13312, 16)
        z_sum = view(13328, 16)
        z_rec = view(13344, 16)
        coef = view(13360, 16)
        lam = view(13376, 8)
        rms = view(13384, 5, TT)
        lam_in = view(13440, 4, DH)
        lam_pr = view(13696, 2, DH)
        sq_scr = sb("sq_scr", [P, P])
        logf = view(10240, 2, S)
        fcum = view(14208, 2, S)
        ones = view(12288, S)
        gate_w = view(13824, KB, 16)
        ln_row = view(15232, 2, D)
        rot_x = acc[:, 2:4, :].rearrange("p a (b n) -> p (a b) n", n=S)
        rot_t = view(8192, 2, S)
        rot_c = view(10240, 2, S)
        consth_f = view(12288, 2, P)
        v_nat = acc[:, 0:2, :].rearrange("p a (b n) -> p (a b) n", n=COLS)
        tmp_a = view(8192, 2, S)
        tmp_b = view(9216, 2, S)

        banks = [ctx.enter_context(nc.psum_tensor(f"bank{i}", [P, 512], F32)) for i in range(8)]

        def norm_bank(k):
            return banks[(k + 4) % 8]

        def bank_set(g):
            return banks[4 * (g % 2):4 * (g % 2) + 4]

        slab_landed = [sem(f"slab_landed{i}") for i in range(2)]
        slab_hi_ready = sem("slab_hi_ready")
        slab_lo_ready = sem("slab_lo_ready")
        pe_event = sem("pe_event")
        const_in, x_in = sem("const_in"), sem("x_in")
        xt_in = [sem(f"xt_in{i}") for i in range(2)]
        y_in = [sem(f"y_in{i}") for i in range(NB)]
        consth_ready = sem("consth_ready")
        evac_act = sem("evac_act")
        evac_dve = sem("evac_dve")
        act_hi_done = sem("act_hi_done")
        act_ready = sem("act_ready")
        relu_done = sem("relu_done")
        hid_hi_done = sem("hid_hi_done")
        sq_done = sem("sq_done")
        hid_ready = sem("hid_ready")
        dve_step = sem("dve_step")
        act_step = sem("act_step")
        pool_step = sem("pool_step")
        ln_var = sem("ln_var")
        ln_rstd = [sem("ln_rstd_pool"), sem("ln_rstd_dve")]
        xhat_ready = sem("xhat_ready")
        ln_psum = sem("ln_psum")
        ln_full = sem("ln_full")
        ln_split = sem("ln_split")
        row_in = sem("row_in")
        acc_init = sem("acc_init")
        resid_ready = sem("resid_ready")
        out_ready, out_ready_pool = sem("out_ready"), sem("out_ready_pool")
        out_done = sem("out_done")
        rot_copied, rot_swapped, rot_done = sem("rot_copied"), sem("rot_swapped"), sem("rot_done")
        at_q, at_s, at_m, at_e, at_p, at_t, at_c, at_v, at_z, at_o, at_sq, at_n, at_x = (
            sem("at_" + n) for n in ("q", "s", "m", "e", "p", "t", "c", "v", "z", "o", "sq", "n", "x"))
        at_ns = sem("at_ns")
        lam_dma, lam_sum, lam_exp, lam_done, subg_in = (
            sem("lam_dma"), sem("lam_sum"), sem("lam_exp"), sem("lam_done"), sem("subg_in"))
        rope_in = sem("rope_in")
        gate_in, gate_mm, gate_z, gate_cum = (
            sem("gate_in"), sem("gate_mm"), sem("gate_z"), sem("gate_cum"))
        decay_in, ones_set = sem("decay_in"), sem("ones_set")
        gate_w_split, gate_w_hi = sem("gate_w_split"), sem("gate_w_hi")
        evac_q1, evac_k1 = sem("evac_q1"), sem("evac_k1")
        fx_q, fx_s, fx_m, fx_e, fx_t, fx_c, fx_v, fx_o, fx_x, fx_h = (sem("fx_" + n) for n in "qsmetcvoxh")

        xt = acc[:, :, :].rearrange("p a (b n) -> p (a b) n", n=S)
        u_t = view(13824, 4, S)
        b_ri, b_ir = view(15872, GROUPS, GCH), view(16384, GROUPS, GCH)
        c_ri, c_ir = view(16896, GROUPS, GCH), view(17408, GROUPS, GCH)
        HG = GROUPS // 2

        accf = acc[:, :, :].rearrange("p a n -> p (a n)")
        f_half = [hid_f32[:, 0:2048], hid_f32[:, 2048:4096]]
        f_scr = accf[:, 0:2048]
        ca_half = [act_f32[:, 2048:4096], act_f32[:, 6144:8192]]
        e_cos, e_sin = (ring_f32[:, o:o + 2048].rearrange("p (g c) -> p g c", g=GROUPS) for o in (2048, 6144))
        k_sb = view(4096, GROUPS, P)
        t_mat = view(0, GROUPS, P)
        u8 = accf[:, 2048:4096].rearrange("p (g c) -> p g c", g=GROUPS)
        r_tab = view(8192, GROUPS, NCH)
        s_buf = view(10240, GROUPS, NCH)
        y_buf = accf[:, 0:2048].rearrange("p (g c) -> p g c", g=GROUPS)
        x_buf, y8 = view(4096, GROUPS, NCH), view(6144, GROUPS, NCH)
        work1, work2 = view(12288, GB, NCH), view(12800, GB, NCH)
        work3, work4 = view(13312, GB, NCH), view(7680, GB, NCH)
        resf = resid[:, :, :].rearrange("p a n -> p (a n)")
        bb1 = resf[:, 0:512].rearrange("p (g h) -> p g h", g=GROUPS)
        pow_r = resf[:, 512:800].rearrange("p (g e) -> p g e", g=GROUPS)
        pow_i = resf[:, 800:1088].rearrange("p (g e) -> p g e", g=GROUPS)
        phase = resf[:, 1088:1472].rearrange("p (e g) -> p e g", g=GROUPS)
        mag8 = resf[:, 1472:1504]
        flat1 = resf[:, 1504:2016]
        slot = resf[:, 2048:2688].rearrange("p (i g) -> p i g", g=GROUPS)
        slot_i = resf[:, 2048 + 19 * 32:2048 + 20 * 32].bitcast(I32)
        prev_r = resf[:, 2688:2944].rearrange("p (g e) -> p g e", g=GROUPS)
        prev_i = resf[:, 2944:3200].rearrange("p (g e) -> p g e", g=GROUPS)
        bb2 = resf[:, 3200:3712].rearrange("p (g h) -> p g h", g=GROUPS)
        flat2 = resf[:, 3712:3968]
        pool_scr = resf[:, 2048:4096]
        y_t = view(10240, NB, S)
        ssm_in, bc_in, u_ready, u8_in, ss_sin_in, ss_sin, ss_par = (
            sem("ss_" + n) for n in ("in", "bc", "u", "u8", "sini", "sin", "par"))
        ss_f, ss_tr, ss_bst, ss_ca, ss_ph, ss_k, ss_kc = (sem("ss_" + n) for n in ("f", "tr", "bst", "ca", "ph", "k", "kc"))
        ss_s, ss_sc, ss_sw, ss_scan, ss_yw, ss_x, ss_y, ss_out = (
            sem("ss_" + n) for n in ("s", "sc", "sw", "scan", "yw", "x", "y", "out"))
        zero_set, zero_out = sem("zero_set"), sem("zero_out")
        k_out, t_in = [sem(f"k_out{i}") for i in range(2)], [sem(f"t_in{i}") for i in range(2)]
        glu_in, glu_y, glu_hi, glu_rhs, glu_sig, glu_full, glu_act = (
            sem("glu_" + n) for n in ("in", "y", "hi", "rhs", "sig", "full", "act"))
        stem_hi, u_out, y_out = sem("stem_hi"), sem("u_out"), sem("y_out")

        block = ctx.enter_context(nc.Block())

        def w_src(w, kh, c0):
            return w.rearrange("(k p) n -> p k n", p=P)[:, kh * SLAB_K:(kh + 1) * SLAB_K, c0:c0 + COLS]

        def slab_source(n):
            if n < SL_OUT0:
                col = {SL_U: 3, SL_Q: 0, SL_K: 1, SL_V: 2}[n - n % 2]
                return w_src(t["ab_w_in"], n % 2, col * COLS)
            if n == SL_GLU:
                return w_src(t["ssm_glu_w"], 0, 0)
            if n < SL_MLP0:
                kh, h = ((n - SL_OUT0) // 2, 0) if n < SL_OUT0 + 3 else (n - SL_OUT0 - 3, 1)
                return w_src(t["ab_w_out"], kh, h * COLS)
            if n < SL_OUT1:
                j = n - SL_L1
                half, part, kh = j // 6, (j % 6) // 2, j % 2
                return w_src(t["fox_w_in"], kh, part * D + half * COLS)
            j = n - SL_OUT1
            return w_src(t["fox_w_out"], j % 2, (j // 2) * COLS)

        def ssm_sp(sp):
            sp.wait_ge(u_ready, 4)
            sp.dma_start(t["u_scratch"].rearrange("(b p) n -> p b n", p=P), u_t[:, :, :]).then_inc(u_out, 16)
            sp.wait_ge(rot_done, 8)
            sp.wait_ge(u_out, 16)
            for j in range(L):
                src = t["u_scratch"].rearrange("(g h) n -> h g n", h=GCH)[:, :, j * NCH:(j + 1) * NCH]
                sp.dma_start(u8[j * GCH:(j + 1) * GCH, :, :], src).then_inc(u8_in, 16)
            sp.wait_ge(zero_out, 32)
            for h in range(2):
                gs = slice(HG * h, HG * (h + 1))
                sp.wait_ge(ss_kc, 4 * h + 4)
                sp.dma_start(t["k_scratch"][:, gs, (L - 1) * GCH:], k_sb[0:GCH, gs, :]).then_inc(k_out[h], 16)
                sp.wait_ge(k_out[h], 16)
                for j in range(L):
                    src = t["k_scratch"][:, gs, (L - 1 - j) * GCH:(2 * L - 1 - j) * GCH]
                    sp.dma_start(t_mat[j * GCH:(j + 1) * GCH, gs, :], src).then_inc(t_in[h], 16)
            for b in range(NB):
                sp.wait_ge(ss_out, b + 1)
                sp.dma_start(t["y_scratch"][b], y8[:, b * GB:(b + 1) * GB, :].rearrange("p g c -> p (g c)")).then_inc(y_out, 16)
                sp.wait_ge(y_out, 16 * (b + 1))
                for g in range(GB):
                    src = t["y_scratch"][b].rearrange("(i h) (g c) -> h i g c", h=GCH, g=GB)[:, :, g, :]
                    dst = y_t[g * GCH:(g + 1) * GCH, b, :].rearrange("h (i c) -> h i c", i=L)
                    sp.dma_start(dst, src).then_inc(y_in[b], 16)
            sp.dma_start(resid[:, :, :], t["x"][0].rearrange("(a p) n -> p a n", p=P)).then_inc(x_in, 16)

        @block.sync
        def _(sp):
            def slab(n, src, r=0, per=0):
                wait(sp, slab_hi_ready, n - 1, r, per)
                wait(sp, slab_lo_ready, n - 1, r, per)
                sp.dma_start(slab_raw[:, n % 2, :, :], src).then_inc(slab_landed[n % 2], 16)

            def mlp_slabs(l, n0, r):
                w1, w2 = t["ffn_w1"][l], t["ffn_w2"][l]
                for c in range(2):
                    for kh in range(2):
                        cols = bass.ds(r * (2 * COLS) + c * COLS, COLS)
                        src = w1.rearrange("(k p) n -> p k n", p=P)[:, kh * SLAB_K:(kh + 1) * SLAB_K, cols]
                        slab(n0 + 4 * c + kh, src, r, 8)
                    for g in range(2):
                        rows = bass.ds(r * (2 * SLAB_K) + c * SLAB_K, SLAB_K)
                        src = w2.rearrange("(k p) n -> p k n", p=P)[:, rows, g * COLS:(g + 1) * COLS]
                        slab(n0 + 4 * c + 2 + g, src, r, 8)

            sp.dma_start(small[:, :], t["small"]).then_inc(ssm_in, 16)
            sp.dma_start(sgn[:, :], t["const"][:, C_SGN:C_SGN + 1], allow_slow_non_contiguous=True).then_inc(ssm_in, 16)
            for kb in range(2):
                sp.dma_start(xt[:, 4 * kb:4 * kb + 4, :], t["xt"][:, 4 * kb:4 * kb + 4, :]).then_inc(xt_in[kb], 16)
                slab(kb, slab_source(kb))
            sp.dma_start(const[:, :], t["const"][:, 0:C_MASK0]).then_inc(const_in, 16)
            sp.dma_start(view(15872, 4, GROUPS * GCH), t["ssm_bc"]).then_inc(bc_in, 16)
            slab(2, slab_source(2))
            slab(3, slab_source(3))
            sp.dma_start(consth_f, t["const"][:, C_MASK0:C_CC]).then_inc(const_in, 16)
            sp.dma_start(rot_c[:, :, :], t["const"][:, C_CC:C_SGN].rearrange("p (a n) -> p a n", a=2)).then_inc(rope_in, 16)
            sp.dma_start(sub_g[:, :], t["ab_subln_g"].rearrange("a h v -> a (h v)").broadcast_to([P, S])).then_inc(subg_in, 16)
            sp.dma_start(lam_in[:, :, :], t["ab_lambda"].broadcast_to([P, 4, DH])).then_inc(lam_dma, 16)
            for n in range(4, SL_GLU + 1):
                slab(n, slab_source(n))
            ssm_sp(sp)
            for n in range(SL_OUT0 + 2, SL_MLP0):
                slab(n, slab_source(n))
            with sp.Fori(0, 4) as r:
                mlp_slabs(0, SL_MLP0, r)
            slab(SL_L1, slab_source(SL_L1))
            slab(SL_L1 + 1, slab_source(SL_L1 + 1))
            sp.dma_start(gate_w[:, :, :], t["fox_w_in"].rearrange("(k p) n -> p k n", p=P)[:, :, 3 * D:3 * D + 16]).then_inc(gate_in, 16)

            def decay_rows(half):
                hs = slice(8 * half, 8 * half + 8)
                sp.dma_start(q_all[DH:DH + 1, :, :], fcum[hs, 0, :]).then_inc(decay_in, 16)
                sp.dma_start(k_all[DH + 1:DH + 2, :, :], fcum[hs, 1, :]).then_inc(decay_in, 16)

            slab(SL_L1 + 2, slab_source(SL_L1 + 2))
            slab(SL_L1 + 3, slab_source(SL_L1 + 3))
            sp.wait_ge(ones_set, 2)
            sp.wait_ge(gate_cum, 2)
            decay_rows(0)
            for n in range(SL_L1 + 4, SL_L1 + 8):
                slab(n, slab_source(n))
            sp.wait_ge(fx_s, 32)
            decay_rows(1)
            for n in range(SL_L1 + 8, SL_MLP1):
                slab(n, slab_source(n))
            with sp.Fori(0, 3) as r:
                mlp_slabs(1, SL_MLP1, r)
            mlp_slabs(1, SL_MLP1, 3)
            for i in range(TT):
                sp.wait_ge(*((out_ready_pool, i + 1) if i < 2 else (out_ready, i - 1)))
                sp.dma_start(t["out"][i * P:(i + 1) * P, :], acc[:, i, :]).then_inc(out_done, 16)
            sp.wait_ge(out_done, 16 * TT)

        @block.tensor
        def _(pe):
            mm = nc.tensor.matmul

            def three(out, a_hi, a_lo, b_hi, b_lo, first, last):
                mm(out, a_hi, b_hi, start=first, stop=False)
                mm(out, a_hi, b_lo, start=False, stop=False)
                return mm(out, a_lo, b_hi, start=False, stop=last)

            def slab_wait(n, r=0):
                wait(pe, slab_hi_ready, n + 1, r, 8)
                wait(pe, slab_lo_ready, n + 1, r, 8)

            def weights_left(g, n, kh, nk, r=0, a=None, out_set=None):
                slab_wait(n, r)
                a_hi, a_lo = a or (act_hi, act_lo)
                for c in range(4):
                    for k in range(SLAB_K):
                        cs = slice(c * P, (c + 1) * P)
                        ins = three(bank_set(g)[c][:, :], slab_hi[:, n % 2, k, cs], slab_lo[:, n % 2, k, cs],
                                    a_hi[:, kh * SLAB_K + k, :], a_lo[:, kh * SLAB_K + k, :],
                                    kh == 0 and k == 0, kh == nk - 1 and k == SLAB_K - 1)
                    if kh == nk - 1:
                        ins.then_inc(pe_event, 1)
                if kh < nk - 1:
                    ins.then_inc(pe_event, 1)

            def weights_left_first(g, n, base):
                slab_wait(n)
                for j in range(SLAB_K):
                    pe.wait_ge(act_ready, base + j + 1)
                    for c, k in [(c, j) for c in range(j)] + [(j, k) for k in range(j + 1)]:
                        cs = slice(c * P, (c + 1) * P)
                        ins = three(bank_set(g)[c][:, :], slab_hi[:, n % 2, k, cs], slab_lo[:, n % 2, k, cs],
                                    act_hi[:, k, :], act_lo[:, k, :], k == 0, False)
                ins.then_inc(pe_event, 1)

            def weights_right(g, n, kh, nk, a, base, r=0):
                slab_wait(n, r)
                a_hi, a_lo = a
                for tt in range(TT):
                    for k in range(SLAB_K):
                        ts = slice(tt * P, (tt + 1) * P)
                        ins = three(bank_set(g)[tt][:, :], a_hi[:, base + k, ts], a_lo[:, base + k, ts],
                                    slab_hi[:, n % 2, k, :], slab_lo[:, n % 2, k, :],
                                    kh == 0 and k == 0, kh == nk - 1 and k == SLAB_K - 1)
                    if kh == nk - 1:
                        ins.then_inc(pe_event, 1)
                if kh < nk - 1:
                    ins.then_inc(pe_event, 1)

            def swap_rotary(g, j):
                for c in range(4):
                    pe.wait_ge(rot_copied, 4 * j + c + 1)
                    mm(bank_set(g)[c][:, :], swap32, rot_x[:, c, :], start=True, stop=True).then_inc(rot_swapped, 1)

            act = (act_hi, act_lo)
            for kh in range(2):
                pe.wait_ge(act_ready, 4 * kh + 4)
                weights_left(G_U, SL_U + kh, kh, 2)
            weights_left(G_Q, SL_Q, 0, 2)
            weights_left(G_Q, SL_Q + 1, 1, 2)
            pe.wait_ge(u_ready, 4)
            weights_left(G_K, SL_K, 0, 2)
            pe.wait_ge(const_in, 32)
            swap_rotary(G_Q, 0)
            weights_left(G_K, SL_K + 1, 1, 2)
            for q in range(8):
                if q % 4 == 0:
                    pe.wait_ge(ss_f, q // 4 + 1)
                if q < 4:
                    pe.wait_ge(rot_done, q + 1)
                else:
                    pe.wait_ge(ss_bst, q - 3)
                for g in range(4):
                    src = f_half[q // 4][:, ((q % 4) * 4 + g) * P:((q % 4) * 4 + g + 1) * P]
                    ins = nc.tensor.transpose(bank_set(G_Q)[q % 4][:, g * P:(g + 1) * P], src, ident)
                ins.then_inc(ss_tr, 1)
            pe.wait_ge(ss_bst, 8)
            weights_right(G_V, SL_V, 0, 2, act, 0)
            swap_rotary(G_K, 1)
            weights_right(G_V, SL_V + 1, 1, 2, act, SLAB_K)

            def scores(out, qs, ks, i, layer):
                n = P * (i + 1)
                mm(out[:, n - P:n], ident_h, mask_h[layer], start=True, stop=False, skip_group_check=True)
                return mm(out[:, 0:n], qs, ks, start=False, stop=True, skip_group_check=True)

            def diff_head(r, first, last):
                def S_(i):
                    wait(pe, at_q, 2 * (i // TT) + 2, r, 2)
                    wait(pe, at_e, 2 * (i - 1), r, 8)
                    n = P * (i % TT + 1)
                    for m in range(2):
                        ks = k_all[0:DH, bass.ds(r * 2 + (2 * (i // TT) + m), 1), 0:n].rearrange("p a n -> p (a n)")
                        ins = scores(banks[2 * (i % 2) + m], q_slot[0:DH, m, n - P:n], ks, i % TT, 0)
                    ins.then_inc(at_s, 1)

                def T_(i):
                    wait(pe, at_p, i + 1, r, 4)
                    wait(pe, at_c, i - 1, r, 4)
                    for j in range(i + 1):
                        ins = nc.tensor.transpose(banks[4 + i % 2][:, j * P:(j + 1) * P],
                                                  e_buf[:, 2 * (i % 2), j * P:(j + 1) * P], ident)
                    ins.then_inc(at_t, 1)

                def V_(i):
                    wait(pe, at_c, i + 1, r, 4)
                    wait(pe, at_o, i, r, 4)
                    for j in range(i % TT + 1):
                        vs = v_nat[:, j, bass.ds(r * P + (i // TT) * P, P)]
                        ins = mm(banks[6][:, 0:P], pt_buf[:, i % 2, j * P:(j + 1) * P], vs,
                                 start=(j == 0), stop=(j == i % TT))
                    ins.then_inc(at_v, 1)

                def X_(k):
                    wait(pe, at_n, TT * (k + 1), r, TT)
                    wait(pe, act_ready, 8 + k, r, 1)
                    for i in range(TT):
                        ins = nc.tensor.transpose(banks[7][:, i * P:(i + 1) * P], o_stage[:, i, :], ident)
                    ins.then_inc(at_x, 1)

                if first:
                    S_(0)
                    S_(1)
                for i in range(TT):
                    T_(i)
                    if i + 2 < TT or not last:
                        S_(i + 2)
                    if i or not first:
                        V_(i - 1)
                    if i == 1 and not first:
                        X_(-1)
                if last:
                    V_(TT - 1)
                    impulse_responses()
                    X_(0)

            def impulse_responses():
                pe.wait_ge(at_e, 32)
                for q in range(8):
                    if q % 4 == 0:
                        pe.wait_ge(ss_ca, q // 4 + 1)
                    if q >= 4:
                        pe.wait_ge(ss_kc, q - 3)
                    for g in range(4):
                        rhs = ca_half[q // 4][:, ((q % 4) * 4 + g) * P:((q % 4) * 4 + g + 1) * P]
                        ins = mm(banks[q % 4][0:GCH, g * P:(g + 1) * P], bb1[:, 4 * q + g, :], rhs, start=True, stop=True)
                    ins.then_inc(ss_k, 1)

            pe.wait_ge(evac_act, 4)
            pe.wait_ge(rot_done, 8)
            pe.wait_ge(consth_ready, 3)
            diff_head(0, True, False)
            with pe.Fori(1, 3) as r:
                diff_head(r, False, False)
            diff_head(3, False, True)

            def swapped(bank, src, b):
                return mm(bank[:, :], swap64, src[:, b * GB:(b + 1) * GB, :].rearrange("p g c -> p (g c)"),
                          start=True, stop=True)

            def swap_inputs(b):
                pe.wait_ge(ss_sc, b + 1)
                swapped(banks[4 + b], s_buf, b).then_inc(ss_sw, 1)

            def swap_states(b):
                pe.wait_ge(ss_scan, b + 1)
                swapped(banks[b], y_buf, b).then_inc(ss_yw, 1)

            pe.wait_ge(ss_kc, 8)
            pe.wait_ge(act_ready, 12)
            pe.wait_ge(u8_in, 16 * L)
            for b in range(NB):
                for g in range(b * GB, (b + 1) * GB):
                    col = (g - b * GB) * NCH
                    lhs = f_half[g // HG][:, (g % HG) * P:(g % HG + 1) * P]
                    ins = mm(banks[b][:, col:col + NCH], lhs, u8[:, g, :], start=True, stop=True)
                ins.then_inc(ss_s, 1)
                if b:
                    swap_inputs(b - 1)
            swap_inputs(NB - 1)
            swap_states(0)
            for b in range(NB):
                if b + 1 < NB:
                    swap_states(b + 1)
                if b % 2 == 0:
                    pe.wait_ge(t_in[b // 2], 16 * L)
                pe.wait_ge(ss_x, b + 1)
                for g in range(b * GB, (b + 1) * GB):
                    col = (g - b * GB) * NCH
                    out = banks[4 + b][:, col:col + NCH]
                    mm(out, t_mat[:, g, :], u8[:, g, :], start=True, stop=False)
                    ins = mm(out, ca_half[g // HG][:, (g % HG) * P:(g % HG + 1) * P], x_buf[:, g, :],
                             start=False, stop=True)
                ins.then_inc(ss_y, 1)

            pe.wait_ge(ss_out, NB)
            weights_right(G_OUT0, SL_OUT0, 0, 2, act, 0)
            pe.wait_ge(glu_rhs, 4)
            weights_left(G_GLU, SL_GLU, 0, 1, a=(hid_hi, hid_lo))
            pe.wait_ge(act_ready, 16)
            weights_right(G_OUT0, SL_OUT0 + 2, 1, 2, act, SLAB_K)
            weights_right(G_OUT0 + 1, SL_OUT0 + 3, 0, 2, act, 0)
            weights_right(G_OUT0 + 1, SL_OUT0 + 4, 1, 2, act, SLAB_K)

            def norm_transposes(l):
                pe.wait_ge(evac_dve, EVAC_DVE_LN[l] - 4)
                for i in range(TT):
                    pe.wait_ge(xhat_ready, 4 * l + i + 1)
                    for k in range(KB):
                        if i == 0 and k >= 4:
                            pe.wait_ge(evac_dve, EVAC_DVE_LN[l] + k - 7)
                        ins = nc.tensor.transpose(norm_bank(k)[:, i * P:(i + 1) * P],
                                                  resid[:, i, k * P:(k + 1) * P], ident)
                        if i == TT - 1:
                            ins.then_inc(ln_psum, 1)

            def mlp(g0, n0, r, d0, h0, ready):
                for c in range(2):
                    g, n, rr = g0 + 3 * c, n0 + 4 * c, r
                    dv = d0 + 8 * c
                    wait(pe, evac_dve, dv - 4, rr, 16)
                    for kh in range(2):
                        first = isinstance(r, int) and r == 0 and c == 0
                        if first and kh == 0:
                            weights_left_first(g, n, ready)
                            continue
                        if first:
                            pe.wait_ge(act_ready, ready + KB)
                        weights_left(g, n + kh, kh, 2, rr)
                    wait(pe, evac_dve, dv, rr, 16)
                    slab_wait(n + 2, rr)
                    for half in range(2):
                        if half:
                            wait(pe, relu_done, h0 + 4 * c + 4, rr, 8)
                            slab_wait(n + 3, rr)
                        for k in range(SLAB_K):
                            if half == 0:
                                wait(pe, hid_ready, h0 + 4 * c + k + 1, rr, 8)
                            for tt in range(TT):
                                ts = slice(tt * P, (tt + 1) * P)
                                ins = three(bank_set(g + 1 + half)[tt][:, :], hid_hi[:, k, ts], hid_lo[:, k, ts],
                                            slab_hi[:, (n + 2 + half) % 2, k, :], slab_lo[:, (n + 2 + half) % 2, k, :],
                                            k == 0, k == SLAB_K - 1)
                                if k == SLAB_K - 1:
                                    ins.then_inc(pe_event, 1)

            norm_transposes(0)
            mlp(G_MLP0, SL_MLP0, 0, 8, 0, 16)
            with pe.Fori(1, 4) as r:
                mlp(G_MLP0, SL_MLP0, r, 8, 0, 16)
            norm_transposes(1)

            def fox_pair_pe(half, r, first, last):
                u0 = 32 * half

                def S_(j):
                    hh, i = j // TT, j % TT
                    wait(pe, fx_q, 8 * half + hh + 1, r, 2)
                    wait(pe, fx_e, u0 + j - 3, r, 8)
                    ks = k_all[0:DH + 2, bass.ds(r * 2 + hh, 1), 0:P * (i + 1)].rearrange("p a n -> p (a n)")
                    scores(banks[j % 4], q_slot[0:DH + 2, hh % 2, i * P:(i + 1) * P], ks, i, 1).then_inc(fx_s, 1)

                def T_(j):
                    wait(pe, fx_e, u0 + j + 1, r, 8)
                    wait(pe, fx_c, u0 + j - 1, r, 8)
                    for b in range(j % TT + 1):
                        ins = nc.tensor.transpose(banks[4 + j % 2][:, b * P:(b + 1) * P],
                                                  e_buf[:, j % 4, b * P:(b + 1) * P], ident)
                    ins.then_inc(fx_t, 1)

                def V_(j):
                    wait(pe, fx_c, u0 + j + 1, r, 8)
                    wait(pe, fx_o, u0 + j, r, 8)
                    for b in range(j % TT + 1):
                        vs = v_nat[:, b, bass.ds(r * P + (j // TT) * DH, DH)]
                        ins = mm(banks[6][:, 0:DH], pt_buf[:, j % 2, b * P:(b + 1) * P], vs,
                                 start=(b == 0), stop=(b == j % TT))
                    ins.then_inc(fx_v, 1)

                def X_(k):
                    wait(pe, fx_o, u0 + 8 * (k + 1), r, 8)
                    wait(pe, act_ready, 32 + 4 * half + k, r, 1)
                    for i in range(TT):
                        ins = nc.tensor.transpose(banks[7][:, i * P:(i + 1) * P], o_stage[:, i, :], ident)
                    ins.then_inc(fx_x, 1)

                if first:
                    for j in range(3):
                        S_(j)
                for j in range(8):
                    T_(j)
                    if j == 1 and not first:
                        X_(-1)
                    if j or not first:
                        V_(j - 1)
                    if j + 3 < 8 or not last:
                        S_(j + 3)
                if last:
                    V_(7)
                    X_(0)

            def decay_gate():
                pe.wait_ge(gate_in, 16)
                pe.wait_ge(gate_w_split, 2)
                for k in range(KB):
                    ins = three(banks[0][0:16, :], gw_hi[:, k, :], gw_lo[:, k, :],
                                act_hi[:, k, :], act_lo[:, k, :], k == 0, k == KB - 1)
                ins.then_inc(gate_mm, 1)

            for half in range(2):
                n0, g0 = SL_L1 + 6 * half, G_L1 + 3 * half
                if half:
                    pe.wait_ge(act_ready, 36)
                    weights_left(g0, n0, 0, 2)
                else:
                    weights_left_first(g0, n0, 24)
                    pe.wait_ge(act_ready, 32)
                    decay_gate()
                weights_left(g0, n0 + 1, 1, 2)
                if half == 0:
                    pe.wait_ge(gate_z, 1)
                weights_left(g0 + 1, n0 + 2, 0, 2)
                weights_left(g0 + 1, n0 + 3, 1, 2)
                pe.wait_ge(evac_q1, 4 * half + 4)
                weights_right(g0 + 2, n0 + 4, 0, 2, act, 0)
                weights_right(g0 + 2, n0 + 5, 1, 2, act, SLAB_K)
                pe.wait_ge(evac_act, 4 + 4 * half + 4)
                pe.wait_ge(evac_k1, 4 * half + 4)
                fox_pair_pe(half, 0, True, False)
                with pe.Fori(1, 3) as r:
                    fox_pair_pe(half, r, False, False)
                fox_pair_pe(half, 3, False, True)
            pe.wait_ge(act_ready, 40)
            for h in range(2):
                weights_right(G_OUT1 + h, SL_OUT1 + 2 * h, 0, 2, (hid_hi, hid_lo), 0)
                weights_right(G_OUT1 + h, SL_OUT1 + 2 * h + 1, 1, 2, act, SLAB_K)
            norm_transposes(2)
            mlp(G_MLP1, SL_MLP1, 0, EVAC_DVE_LN[2], 32, 40)
            with pe.Fori(1, 4) as r:
                mlp(G_MLP1, SL_MLP1, r, EVAC_DVE_LN[2], 32, 40)

        class Steps:

            def __init__(self, eng, sem_):
                self.eng, self.sem, self.count, self.r, self.per = eng, sem_, 0, 0, 0

            def step(self, ins):
                self.count += 1
                ins.then_inc(self.sem, 1)

            def settle(self):
                wait(self.eng, self.sem, self.count, self.r, self.per)

            def pipelined(self, n, per_body, body):
                body(0, True, False)
                start = self.count
                with self.eng.Fori(1, n - 1) as r:
                    self.count, self.r, self.per = start - per_body, r, per_body
                    body(r, False, False)
                    assert self.count == start, self.count - start
                self.count, self.r, self.per = start + (n - 2) * per_body, 0, 0
                body(n - 1, False, True)

        @block.vector
        def _(dve):
            st = Steps(dve, dve_step)
            tt_, ts_, stt = nc.vector.tensor_tensor, nc.vector.tensor_scalar, nc.vector.scalar_tensor_tensor

            def split(n, r=0):
                wait(dve, slab_hi_ready, n + 1, r, 8)
                tt_(slab_lo[:, n % 2, :, :], slab_raw[:, n % 2, :, :], slab_hi[:, n % 2, :, :].bitcast(F32),
                    ALU.subtract).then_inc(slab_lo_ready, 1)

            dve.wait_ge(ssm_in, 32)
            a_re, a_im, ldt = (small[:, o:o + GROUPS] for o in (S_ARE, S_AIM, S_LDT))
            sl = [slot[:, i, :] for i in range(20)]

            def do(ins):
                st.step(ins)
                st.settle()

            def exp_parts(z, w, pm, f, k):
                do(ts_(f, z, -88.0, 88.7, ALU.max, ALU.min))
                do(ts_(k, f, 1.4426950408889634, 12582912.0, ALU.mult, ALU.add))
                do(ts_(k, k, -12582912.0, None, ALU.add))
                do(stt(f, k, -0.693359375, f, ALU.mult, ALU.add))
                do(stt(f, k, 2.12194440e-4, f, ALU.mult, ALU.add))
                do(ts_(pm, f, 1.0 / 5040, None, ALU.mult))
                for cf in (1.0 / 720, 1.0 / 120, 1.0 / 24, 1.0 / 6, 0.5, 1.0):
                    do(stt(pm, pm, cf, f, ALU.add, ALU.mult))
                do(ts_(slot_i, k, 127.0, None, ALU.add))
                do(ts_(slot_i, slot_i, 23, None, ALU.logical_shift_left))
                do(nc.vector.tensor_copy(w, slot_i.bitcast(F32)))

            dt, th, mag, magm1, s_, c_, cm1, ar, ai, gr, gi = sl[0:11]

            def cmul(dr, di, xr, xi, yr, yi, t1, t2):
                do(tt_(t1, xr, yr, ALU.mult))
                do(tt_(t2, xi, yi, ALU.mult))
                do(tt_(dr, t1, t2, ALU.subtract))
                do(tt_(t1, xr, yi, ALU.mult))
                do(tt_(t2, xi, yr, ALU.mult))
                do(tt_(di, t1, t2, ALU.add))

            def over_h(v):
                return v.unsqueeze(2).broadcast_to([P, GROUPS, GCH])

            cr, ci = phase[:, 0:6, :], phase[:, 6:12, :]

            def discretise_angles():
                exp_parts(ldt, sl[11], sl[12], sl[13], sl[14])
                do(stt(dt, sl[12], 1.0, sl[11], ALU.add, ALU.mult))
                do(tt_(sl[15], a_re, dt, ALU.mult))
                exp_parts(sl[15], sl[11], sl[12], sl[13], sl[14])
                do(tt_(magm1, sl[12], sl[11], ALU.mult))
                do(tt_(mag, magm1, sl[11], ALU.add))
                do(ts_(sl[13], sl[11], -1.0, None, ALU.add))
                do(tt_(magm1, magm1, sl[13], ALU.add))
                do(tt_(th, a_im, dt, ALU.mult))
                do(ts_(sl[14], th, 1.0 / (2 * math.pi), 12582912.0, ALU.mult, ALU.add))
                do(ts_(sl[14], sl[14], -12582912.0, None, ALU.add))
                for piece in (6.28125, 1.9340515e-3, 1.2556659e-6):
                    do(stt(th, sl[14], -piece, th, ALU.mult, ALU.add))
                do(ts_(th, th, -3.1415925, 3.1415925, ALU.max, ALU.min))
                ts_(sl[16], th, 0.5, None, ALU.mult).then_inc(ss_sin_in, 1)

            def discretise_inputs():
                dve.wait_ge(ss_sin, 2)
                do(stt(cm1, c_, -2.0, c_, ALU.mult, ALU.mult))
                do(ts_(c_, cm1, 1.0, None, ALU.add))
                do(tt_(ar, mag, c_, ALU.mult))
                do(tt_(ai, mag, s_, ALU.mult))
                do(tt_(sl[11], mag, cm1, ALU.mult))
                do(tt_(sl[11], sl[11], magm1, ALU.add))
                do(tt_(sl[12], a_re, a_re, ALU.mult))
                do(tt_(sl[13], a_im, a_im, ALU.mult))
                do(tt_(sl[12], sl[12], sl[13], ALU.add))
                do(nc.vector.reciprocal(sl[12], sl[12]))
                do(tt_(gr, sl[11], a_re, ALU.mult))
                do(tt_(sl[13], ai, a_im, ALU.mult))
                do(tt_(gr, gr, sl[13], ALU.add))
                do(tt_(gr, gr, sl[12], ALU.mult))
                do(tt_(gi, ai, a_re, ALU.mult))
                do(tt_(sl[13], sl[11], a_im, ALU.mult))
                do(tt_(gi, gi, sl[13], ALU.subtract))
                do(tt_(gi, gi, sl[12], ALU.mult))
                do(ts_(gi, gi, sgn[:, 0:1], None, ALU.mult))

                dve.wait_ge(bc_in, 16)
                flat = flat1.rearrange("p (g h) -> p g h", g=GROUPS)
                do(tt_(bb1, b_ri, over_h(gr), ALU.mult))
                do(tt_(flat, b_ir, over_h(gi), ALU.mult))
                do(tt_(bb1, bb1, flat, ALU.add))
                do(tt_(bb2, b_ir, over_h(gr), ALU.mult))
                do(tt_(flat, b_ri, over_h(gi), ALU.mult))
                do(tt_(bb2, bb2, flat, ALU.subtract))
                do(ts_(sl[17][:, 0:1], sgn[:, 0:1], -1.0, None, ALU.mult))
                do(ts_(c_ri, c_ri, sl[17][:, 0:1], None, ALU.mult))
                do(ts_(c_ir, c_ir, sl[17][:, 0:1], None, ALU.mult))


            def power_tables():
                do(nc.vector.memset(pow_r[:, :, 0], 1.0))
                do(nc.vector.memset(pow_i[:, :, 0], 0.0))
                do(nc.vector.tensor_copy(pow_r[:, :, 1], ar))
                do(nc.vector.tensor_copy(pow_i[:, :, 1], ai))
                for n in (1, 2, 4):
                    t1 = flat1[:, 0:GROUPS * n].rearrange("p (g e) -> p g e", g=GROUPS)
                    t2 = flat2[:, 0:GROUPS * n].rearrange("p (g e) -> p g e", g=GROUPS)
                    br = pow_r[:, :, n:n + 1].broadcast_to([P, GROUPS, n])
                    bi = pow_i[:, :, n:n + 1].broadcast_to([P, GROUPS, n])
                    cmul(pow_r[:, :, n + 1:2 * n + 1], pow_i[:, :, n + 1:2 * n + 1],
                         pow_r[:, :, 1:n + 1], pow_i[:, :, 1:n + 1], br, bi, t1, t2)
                do(ts_(pow_i, pow_i, sgn[:, 0:1], None, ALU.mult))
                for e in range(L):
                    nc.vector.tensor_copy(prev_r[:, :, e], pow_r[:, :, L - e]).then_inc(ss_par, 1)
                    nc.vector.tensor_copy(prev_i[:, :, e], pow_i[:, :, L - e]).then_inc(ss_par, 1)

            def phase_powers():
                cmul(sl[11], sl[12], c_, s_, c_, s_, sl[13], sl[14])
                cmul(sl[15], sl[16], sl[11], sl[12], sl[11], sl[12], sl[13], sl[14])
                cmul(cr[:, 0, :], ci[:, 0, :], sl[15], sl[16], sl[15], sl[16], sl[13], sl[14])
                for n in range(5):
                    cmul(cr[:, n + 1, :], ci[:, n + 1, :], cr[:, n, :], ci[:, n, :], cr[:, n, :], ci[:, n, :], sl[13], sl[14])
                for _ in range(2):
                    do(tt_(mag, mag, mag, ALU.mult))
                tt_(mag8, mag, mag, ALU.mult).then_inc(ss_par, 1)

            discretise_angles()
            for kb in range(2):
                ks = slice(4 * kb, 4 * kb + 4)
                dve.wait_ge(stem_hi, kb + 1)
                tt_(act_lo[:, ks, :], xt[:, ks, :], act_hi[:, ks, :].bitcast(F32), ALU.subtract).then_inc(act_ready, 4)
                split(kb)
            discretise_inputs()
            split(2)
            power_tables()
            split(3)
            phase_powers()
            dve.wait_ge(const_in, 32)
            nc.vector.tensor_copy(ident_h, ident).then_inc(consth_ready, 1)
            for m in range(2):
                nc.vector.tensor_copy(mask_h[m], consth_f[:, m, :]).then_inc(consth_ready, 1)

            dve.wait_ge(lam_dma, 16)
            pairs = lam_in[:, :, :].rearrange("p (a b) d -> p a b d", b=2)
            st.step(tt_(lam_pr[:, :, :], pairs[:, :, 0, :], pairs[:, :, 1, :], ALU.mult))
            st.settle()
            nc.vector.tensor_reduce(lam[:, 0:2], lam_pr[:, :, :], AX.X, ALU.add).then_inc(lam_sum, 1)
            dve.wait_ge(lam_exp, 1)
            st.step(tt_(lam[:, 4:5], lam[:, 3:4], lam[:, 2:3], ALU.subtract))
            st.settle()
            st.step(ts_(lam[:, 5:6], lam[:, 4:5], -LAM_INIT, None, ALU.add))
            dve.wait_ge(subg_in, 16)
            st.step(ts_(sub_g[:, :], sub_g[:, :], 1.0 - LAM_INIT, None, ALU.mult))

            def rotary(g, j, dst):
                dve.wait_ge(rope_in, 16)
                for c in range(4):
                    dve.wait_ge(rot_swapped, 4 * j + c + 1)
                    st.step(tt_(rot_t[:, 0, :], rot_x[:, c, :], rot_c[:, 0, :], ALU.mult))
                    st.step(tt_(rot_t[:, 1, :], bank_set(g)[c][:, :], rot_c[:, 1, :], ALU.mult))
                    st.settle()
                    st.step(tt_(dst[0:DH, 2 * c, :], rot_t[0:DH, 0, :], rot_t[0:DH, 1, :], ALU.add))
                    tt_(dst[0:DH, 2 * c + 1, :], rot_t[DH:P, 0, :], rot_t[DH:P, 1, :], ALU.add).then_inc(rot_done, 1)
                    dve.wait_ge(rot_done, 4 * j + c + 1)

            split(4)
            split(5)
            rotary(G_Q, 0, q_all)
            split(6)
            split(7)
            rotary(G_K, 1, k_all)
            split(8)

            def rsqrt_seed(y, x):
                do(ts_(y.bitcast(I32), x.bitcast(I32), -0.5, float(0x5F3759DF), ALU.mult, ALU.add))

            def rsqrt_newton(y, x, tmp, out):
                st.step(tt_(tmp, y, y, ALU.mult))
                st.settle()
                st.step(stt(tmp, tmp, -0.5, x, ALU.mult, ALU.mult))
                st.settle()
                return stt(out, tmp, 1.5, y, ALU.add, ALU.mult)

            def diff_head(r, first, last):
                def M_(i):
                    wait(dve, at_s, i + 1, r, 4)
                    for m in range(2):
                        col = 2 * (i % TT) + m
                        nc.vector.tensor_reduce(neg_max[:, col:col + 1], banks[2 * (i % 2) + m][:, 0:P * (i % TT + 1)],
                                                AX.X, ALU.max, negate=True).then_inc(at_m, 1)

                def D_(i):
                    wait(dve, at_e, 2 * i + 2, r, 8)
                    c, n = 2 * (i % TT), P * (i % TT + 1)
                    st.step(nc.vector.reciprocal(z_rec[:, c:c + 2], z_sum[:, c:c + 2]))
                    st.settle()
                    st.step(stt(coef[:, i % TT:i % TT + 1], z_sum[:, c:c + 1], z_rec[:, c + 1:c + 2], lam[:, 5:6],
                                ALU.mult, ALU.mult))
                    st.settle()
                    stt(e_buf[:, 2 * (i % 2), 0:n], e_buf[:, 2 * (i % 2) + 1, 0:n], coef[:, i % TT:i % TT + 1],
                        e_buf[:, 2 * (i % 2), 0:n], ALU.mult, ALU.add).then_inc(at_p, 1)

                def C_(i):
                    wait(dve, at_t, i + 1, r, 4)
                    wait(dve, at_v, i - 1, r, 4)
                    n = P * (i + 1)
                    nc.vector.tensor_copy(pt_buf[:, i % 2, 0:n], banks[4 + i % 2][:, 0:n]).then_inc(at_c, 1)

                def O_(i):
                    wait(dve, at_v, i + 1, r, 4)
                    if i >= 0:
                        wait(dve, at_x, 0, r, 1)
                    st.settle()
                    ts_(o_stage[:, i % TT, :], banks[6][:, 0:P], z_rec[:, 2 * (i % TT):2 * (i % TT) + 1], None,
                        ALU.mult).then_inc(at_o, 1)

                def N_(k):
                    wait(dve, at_sq, TT * (k + 1), r, TT)
                    do(ts_(rms[:, 2, :], rms[:, 0, :], 1.0 / (2 * DH), RMS_EPS, ALU.mult, ALU.add))
                    rsqrt_seed(rms[:, 4, :], rms[:, 2, :])
                    for _ in range(3):
                        do(rsqrt_newton(rms[:, 4, :], rms[:, 2, :], rms[:, 3, :], rms[:, 4, :]))
                    for i in range(TT):
                        stt(o_stage[:, i, :], o_stage[:, i, :], rms[:, 4, i:i + 1], sub_g[:, bass.ds(r * P + k * P, P)],
                            ALU.mult, ALU.mult).then_inc(at_n, 1)

                def L_(k):
                    wait(dve, at_ns, k + 1, r, 1)
                    tt_(act_lo[:, bass.ds(r + k, 1), :], banks[7][:, :].unsqueeze(1),
                        act_hi[:, bass.ds(r + k, 1), :].bitcast(F32), ALU.subtract).then_inc(act_ready, 1)

                if first:
                    M_(0)
                    M_(1)
                    D_(0)
                for i in range(TT):
                    C_(i)
                    if i + 1 < TT or not last:
                        D_(i + 1)
                    if i + 2 < TT or not last:
                        M_(i + 2)
                    if i or not first:
                        O_(i - 1)
                    if i == 0 and not first:
                        N_(-1)
                    if i == 3 and not first:
                        L_(-1)
                if last:
                    O_(TT - 1)
                    N_(0)
                    L_(0)

            st.pipelined(4, 4 * 2 + 11, diff_head)

            def chunk_inputs(b):
                bs = slice(b * GB, (b + 1) * GB)
                if b:
                    dve.wait_ge(ss_scan, b)
                dve.wait_ge(ss_sw, b + 1)
                st.step(tt_(work1, s_buf[:, bs, :], e_cos[:, bs, :], ALU.mult))
                st.step(tt_(work2, banks[4 + b][:, :].rearrange("p (g c) -> p g c", g=GB), e_sin[:, bs, :], ALU.mult))
                st.settle()
                do(tt_(work1, work1, work2, ALU.add))
                nc.vector.tensor_tensor_scan(y_buf[:, bs, :].rearrange("p g c -> p (g c)"),
                                             r_tab[:, bs, :].rearrange("p g c -> p (g c)"),
                                             work1.rearrange("p g c -> p (g c)"), 0.0, ALU.mult, ALU.add).then_inc(ss_scan, 1)

            def entering_states(b):
                bs, n = slice(b * GB, (b + 1) * GB), NCH - 1
                if b:
                    dve.wait_ge(ss_x, b)
                dve.wait_ge(ss_scan, b + 1)
                dve.wait_ge(ss_yw, b + 1)
                st.step(tt_(work3[:, :, 0:n], y_buf[:, bs, 0:n], e_cos[:, bs, 0:n], ALU.mult))
                st.step(tt_(work4[:, :, 0:n], banks[b][:, :].rearrange("p (g c) -> p g c", g=GB)[:, :, 0:n],
                            e_sin[:, bs, 0:n], ALU.mult))
                st.settle()
                tt_(x_buf[:, bs, 1:NCH], work3[:, :, 0:n], work4[:, :, 0:n], ALU.subtract).then_inc(ss_x, 1)

            dve.wait_ge(ss_par, 2 * L + 1)
            do(nc.vector.memset(r_tab[:, :, 0], 0.0))
            do(nc.vector.tensor_copy(r_tab[:, :, 1:NCH], mag8.unsqueeze(2).broadcast_to([P, GROUPS, NCH - 1])))
            for h in range(2):
                dve.wait_ge(k_out[h], 16)
            do(nc.vector.memset(x_buf[:, :, 0], 0.0))
            dve.wait_ge(ss_ph, 1)
            chunk_inputs(0)
            for b in range(NB):
                if b + 1 < NB:
                    chunk_inputs(b + 1)
                entering_states(b)
            dve.wait_ge(ss_x, NB)
            split(9)

            for b in range(4):
                dve.wait_ge(y_in[b], 16 * GB)
                stt(y_t[:, b, :], u_t[:, b, :], small[:, S_D + b:S_D + b + 1], y_t[:, b, :],
                    ALU.mult, ALU.add).then_inc(glu_in, 1)
            for b in range(4):
                dve.wait_ge(glu_hi, b + 1)
                tt_(hid_lo[:, b, :], y_t[:, b, :], hid_hi[:, b, :].bitcast(F32), ALU.subtract).then_inc(glu_rhs, 1)
            for b in range(4):
                dve.wait_ge(glu_sig, b + 1)
                dve.wait_ge(glu_act, max(b - 1, 0)) if b > 1 else None
                yv = y_t[:, b, :].rearrange("p (i c) -> p c i", i=L)
                sv = tmp_a[:, b % 2, :].rearrange("p (i c) -> p c i", i=L)
                tt_(tmp_b[:, b % 2, :].rearrange("p (c i) -> p c i", i=L), yv, sv, ALU.mult).then_inc(glu_full, 1)
                dve.wait_ge(glu_act, b + 1)
                tt_(act_lo[:, 4 + b, :], tmp_b[:, b % 2, :], act_hi[:, 4 + b, :].bitcast(F32), ALU.subtract).then_inc(act_ready, 1)

            def evac_and_norm(l, evac):
                for i in range(TT):
                    evac(i)
                    dve.wait_ge(evac_dve, EVAC_DVE_LN[l] - TT + i + 1)
                    for h in range(2):
                        st.step(nc.vector.bn_stats(stats[:, i, 6 * h:6 * h + 6], acc[:, i, h * 512:(h + 1) * 512]))
                    st.settle()
                    nc.vector.bn_aggr(mv[:, i, :], stats[:, i, :]).then_inc(ln_var, 1)
                    if i == TT - 1:
                        s2 = slice(i - 1, i + 1)
                        dve.wait_ge(ln_var, 4 * l + i + 1)
                        do(ts_(lns[:, 2, s2], mv[:, s2, 1], LN_EPS, None, ALU.add))
                        rsqrt_seed(lns[:, 4, s2], lns[:, 2, s2])
                        for _ in range(3):
                            do(rsqrt_newton(lns[:, 4, s2], lns[:, 2, s2], lns[:, 3, s2], lns[:, 4, s2]))
                        stt(lns[:, 1, s2], mv[:, s2, 0], -1.0, lns[:, 4, s2], ALU.mult, ALU.mult).then_inc(ln_rstd[1], 1)

            def evac_out(g, h, i):
                dve.wait_ge(pe_event, BANK_EVENT[g, i])
                cs = slice(h * COLS, (h + 1) * COLS)
                stt(acc[:, i, cs], resid[:, i, cs], ALPHA, bank_set(g)[i][:, :], ALU.mult, ALU.add).then_inc(evac_dve, 1)

            def out_projection(l, g0, n0):
                split(n0 + 2)
                for i in range(TT):
                    evac_out(g0, 0, i)
                split(n0 + 3)
                evac_and_norm(l, lambda i: evac_out(g0 + 1, 1, i))
                split(n0 + 4)
                split(n0 + 5)

            split(SL_OUT0 + 2)
            dve.wait_ge(x_in, 16)
            out_projection(0, G_OUT0, SL_OUT0 + 1)

            def norm_split(l):
                for k in range(KB):
                    dve.wait_ge(act_hi_done, 8 * l + k + 1)
                    do(ts_(tmp_a[:, k % 2, :], norm_bank(k)[:, :], small[:, S_LNG + 8 * l + k:S_LNG + 8 * l + k + 1],
                           small[:, S_LNB + 8 * l + k:S_LNB + 8 * l + k + 1], ALU.mult, ALU.add))
                    tt_(act_lo[:, k, :], tmp_a[:, k % 2, :], act_hi[:, k, :].bitcast(F32), ALU.subtract).then_inc(act_ready, 1)

            def mlp(g0, n0, h0, r, norm=None):
                for c in range(2):
                    g, n = g0 + 3 * c, n0 + 4 * c
                    split(n + 2, r)
                    for k in range(4):
                        wait(dve, relu_done, h0 + 4 * c + k + 1, r, 8)
                        tt_(tmp_b[:, k % 2, :], tmp_a[:, k % 2, :], tmp_a[:, k % 2, :], ALU.mult).then_inc(sq_done, 1)
                        wait(dve, sq_done, h0 + 4 * c + k + 1, r, 8)
                        wait(dve, hid_hi_done, h0 + 4 * c + k + 1, r, 8)
                        tt_(hid_lo[:, k, :], tmp_b[:, k % 2, :], hid_hi[:, k, :].bitcast(F32),
                            ALU.subtract).then_inc(hid_ready, 1)
                    split(n + 3, r)
                    for half in range(2):
                        ends = norm is not None and c == 1
                        if not ends:
                            split(n + 4 + half, r)
                        if isinstance(r, int) and r == 0 and c == 0 and half == 0:
                            dve.wait_ge(acc_init, 4 + h0 // 8)

                        def evac(i):
                            wait(dve, pe_event, BANK_EVENT[g + 1 + half, i], r, 2 * CHUNK_EVENTS)
                            cs = slice(half * COLS, (half + 1) * COLS)
                            tt_(acc[:, i, cs], acc[:, i, cs], bank_set(g + 1 + half)[i][:, :], ALU.add).then_inc(evac_dve, 1)

                        if ends and half == 1:
                            evac_and_norm(norm, evac)
                            if norm == 1:
                                split(n + 4, r)
                                split(n + 5, r)
                        else:
                            for i in range(TT):
                                evac(i)

            norm_split(0)
            mlp(G_MLP0, SL_MLP0, 0, 0)
            with dve.Fori(1, 3) as r:
                mlp(G_MLP0, SL_MLP0, 0, r)
            mlp(G_MLP0, SL_MLP0, 0, 3, norm=1)
            norm_split(1)

            dve.wait_ge(gate_w_hi, 1)
            tt_(gw_lo[:, :, :], gate_w[:, :, :], gw_hi[:, :, :].bitcast(F32), ALU.subtract).then_inc(gate_w_split, 2)
            st.step(nc.vector.memset(ones[0:16, :], 1.0))
            split(SL_L1 + 2)
            z, zl = logf[0:16, 0, :], logf[0:16, 1, :]
            dve.wait_ge(gate_mm, 1)
            do(ts_(z, banks[0][0:16, :], small[0:16, S_BF:S_BF + 1], None, ALU.add))
            stt(zl, z, -1.0, z, ALU.mult, ALU.max).then_inc(gate_z, 1)
            dve.wait_ge(gate_z, 3)
            do(stt(z, z, 0.0, zl, ALU.min, ALU.subtract))
            nc.vector.tensor_tensor_scan(fcum[0:16, 0, :], ones[0:16, :], z, 0.0, ALU.mult, ALU.add).then_inc(gate_cum, 1)
            dve.wait_ge(gate_cum, 1)
            ts_(fcum[0:16, 1, :], fcum[0:16, 0, :], -1.0, None, ALU.mult).then_inc(gate_cum, 1)

            def fox_pair(half, r, first, last):
                u0 = 32 * half

                def M_(j):
                    wait(dve, fx_s, u0 + j + 1, r, 8)
                    nc.vector.tensor_reduce(neg_max[:, j % 8:j % 8 + 1], banks[j % 4][:, 0:P * (j % TT + 1)],
                                            AX.X, ALU.max, negate=True).then_inc(fx_m, 1)

                def C_(j):
                    wait(dve, fx_t, u0 + j + 1, r, 8)
                    wait(dve, fx_v, u0 + j - 1, r, 8)
                    n = P * (j % TT + 1)
                    nc.vector.tensor_copy(pt_buf[:, j % 2, 0:n], banks[4 + j % 2][:, 0:n]).then_inc(fx_c, 1)

                def O_(j):
                    wait(dve, fx_v, u0 + j + 1, r, 8)
                    if j >= 0:
                        wait(dve, fx_x, 4 * half, r, 1)
                    st.settle()
                    cs = slice((j // TT) % 2 * DH, ((j // TT) % 2 + 1) * DH)
                    ts_(o_stage[:, j % TT, cs], banks[6][:, 0:DH], z_rec[:, j % 8:j % 8 + 1], None,
                        ALU.mult).then_inc(fx_o, 1)

                def L_(k):
                    wait(dve, fx_h, 4 * half + k + 1, r, 1)
                    hi, lo, b0 = (hid_hi, hid_lo, 0) if half == 0 else (act_hi, act_lo, 4)
                    tt_(lo[:, bass.ds(r + (k + b0), 1), :], banks[7][:, :].unsqueeze(1),
                        hi[:, bass.ds(r + (k + b0), 1), :].bitcast(F32), ALU.subtract).then_inc(act_ready, 1)

                if first:
                    for j in range(3):
                        M_(j)
                for j in range(8):
                    C_(j)
                    if j or not first:
                        O_(j - 1)
                    st.step(nc.vector.reciprocal(z_rec[:, j:j + 1], z_sum[:, j:j + 1]))
                    if j + 3 < 8 or not last:
                        M_(j + 3)
                    if j == 3 and not first:
                        L_(-1)
                if last:
                    O_(7)
                    L_(0)

            for half in range(2):
                n0, g0 = SL_L1 + 6 * half, G_L1 + 3 * half
                if half:
                    split(n0 + 2)
                split(n0 + 3)
                split(n0 + 4)
                for c in range(4):
                    dve.wait_ge(pe_event, BANK_EVENT[g0 + 1, c])
                    st.step(nc.vector.tensor_copy(k_all[0:DH, 2 * c, :], bank_set(g0 + 1)[c][0:DH, :]))
                    nc.vector.tensor_copy(k_all[0:DH, 2 * c + 1, :], bank_set(g0 + 1)[c][DH:P, :]).then_inc(evac_k1, 1)
                split(n0 + 5)
                split(n0 + 6)
                split(n0 + 7)
                st.settle()
                st.pipelined(4, 8, lambda r, first, last: fox_pair(half, r, first, last))

            dve.wait_ge(resid_ready, 4)
            out_projection(2, G_OUT1, SL_OUT1)
            norm_split(2)
            mlp(G_MLP1, SL_MLP1, 32, 0)
            with dve.Fori(1, 3) as r:
                mlp(G_MLP1, SL_MLP1, 32, r)
            mlp(G_MLP1, SL_MLP1, 32, 3, norm=3)
            dve.wait_ge(row_in, 32 * 4)
            for i in (2, 3):
                dve.wait_ge(xhat_ready, 12 + i + 1)
                do(tt_(acc[:, i, :], resid[:, i, :], ln_row[:, 0, :], ALU.mult))
                tt_(acc[:, i, :], acc[:, i, :], ln_row[:, 1, :], ALU.add).then_inc(out_ready, 1)

        @block.scalar
        def _(sc):
            act = nc.scalar.activation

            def split(n, r=0):
                if isinstance(r, int):
                    sc.wait_ge(slab_landed[n % 2], 16 * ((n + 8 * r) // 2 + 1))
                else:
                    wait(sc, slab_landed[n % 2], 16 * (n // 2 + 1), r, 64)
                if n >= 2:
                    wait(sc, pe_event, SLAB_EVENT[n - 2], r, 2 * CHUNK_EVENTS)
                act(slab_hi[:, n % 2, :, :], slab_raw[:, n % 2, :, :], ACT.Copy).then_inc(slab_hi_ready, 1)

            for kb in range(2):
                ks = slice(4 * kb, 4 * kb + 4)
                sc.wait_ge(xt_in[kb], 16)
                act(act_hi[:, ks, :], xt[:, ks, :], ACT.Copy).then_inc(stem_hi, 1)
                split(kb)
                if kb == 0:
                    sc.wait_ge(ss_sin_in, 1)
                    act(slot[:, 4, :], slot[:, 1, :], ACT.Sin).then_inc(ss_sin, 1)
                    act(slot[:, 5, :], slot[:, 16, :], ACT.Sin).then_inc(ss_sin, 1)
            split(2)
            for c in range(4):
                sc.wait_ge(pe_event, BANK_EVENT[G_U, c])
                act(u_t[:, c, :].rearrange("p (j n) -> p j n", j=L),
                    bank_set(G_U)[c][:, :].rearrange("p (n j) -> p j n", j=L), ACT.Copy).then_inc(u_ready, 1)
            split(3)
            sc.wait_ge(lam_sum, 1)
            act(lam[:, 2:4], lam[:, 0:2], ACT.Exp).then_inc(lam_exp, 1)
            split(4)
            sc.wait_ge(act_ready, 8)
            for c in range(4):
                sc.wait_ge(pe_event, BANK_EVENT[G_Q, c])
                act(rot_x[:, c, :], bank_set(G_Q)[c][:, :], ACT.Copy, scale=DH ** -0.5).then_inc(rot_copied, 1)
            split(5)
            split(6)
            for c in range(4):
                sc.wait_ge(pe_event, BANK_EVENT[G_K, c])
                sc.wait_ge(rot_done, c + 1)
                act(rot_x[:, c, :], bank_set(G_K)[c][:, :], ACT.Copy).then_inc(rot_copied, 1)
            for q in range(8):
                sc.wait_ge(ss_tr, q + 1)
                act(f_half[q // 4][:, (q % 4) * 512:(q % 4 + 1) * 512], bank_set(G_Q)[q % 4][:, :],
                    ACT.Copy).then_inc(ss_bst, 1)
            split(7)
            split(8)
            for i in range(TT):
                sc.wait_ge(pe_event, BANK_EVENT[G_V, i])
                act(v_nat[:, i, :], bank_set(G_V)[i][:, :], ACT.Copy).then_inc(evac_act, 1)

            def diff_head(r, first, last):
                def E_(i):
                    n = P * (i % TT + 1)
                    for m in range(2):
                        wait(sc, at_m, 2 * i + m + 1, r, 8)
                        wait(sc, at_t, i - 1, r, 4)
                        col = 2 * (i % TT) + m
                        act(e_buf[:, 2 * (i % 2) + m, 0:n], banks[2 * (i % 2) + m][:, 0:n], ACT.Exp,
                            bias=neg_max[:, col:col + 1], accum_out=z_sum[:, col:col + 1]).then_inc(at_e, 1)

                def Q_(i):
                    wait(sc, at_o, i + 1, r, 4)
                    wait(sc, at_sq, i, r, 4)
                    act(sq_scr[:, :], o_stage[:, i % TT, :], ACT.Square,
                        accum_out=rms[:, 0, i % TT:i % TT + 1]).then_inc(at_sq, 1)

                def H_(k):
                    wait(sc, at_x, k + 1, r, 1)
                    act(act_hi[:, bass.ds(r + k, 1), :], banks[7][:, :].unsqueeze(1), ACT.Copy).then_inc(at_ns, 1)

                if first:
                    E_(0)
                    E_(1)
                for i in range(TT):
                    if i or not first:
                        Q_(i - 1)
                    if i == 2 and not first:
                        H_(-1)
                    if i + 2 < TT or not last:
                        E_(i + 2)
                if last:
                    Q_(TT - 1)
                    for q in range(8):
                        sc.wait_ge(ss_k, q + 1)
                        act(k_sb[0:GCH, 4 * q:4 * q + 4, :].rearrange("p g n -> p (g n)"), banks[q % 4][0:GCH, :],
                            ACT.Copy).then_inc(ss_kc, 1)
                    H_(0)

            diff_head(0, True, False)
            with sc.Fori(1, 3) as r:
                diff_head(r, False, False)
            diff_head(3, False, True)

            for b in range(NB):
                sc.wait_ge(ss_s, b + 1)
                act(s_buf[:, b * GB:(b + 1) * GB, :].rearrange("p g c -> p (g c)"), banks[b][:, :],
                    ACT.Copy).then_inc(ss_sc, 1)
            for b in range(NB):
                sc.wait_ge(ss_y, b + 1)
                act(y8[:, b * GB:(b + 1) * GB, :].rearrange("p g c -> p (g c)"), banks[4 + b][:, :],
                    ACT.Copy).then_inc(ss_out, 1)
            sc.wait_ge(ss_x, NB)
            split(9)

            for b in range(4):
                sc.wait_ge(glu_in, b + 1)
                act(y_t[:, b, :], y_t[:, b, :], ACT.Gelu_apprx_tanh).then_inc(glu_y, 1)
            for b in range(4):
                sc.wait_ge(glu_y, b + 1)
                act(hid_hi[:, b, :], y_t[:, b, :], ACT.Copy).then_inc(glu_hi, 1)
            for b in range(4):
                sc.wait_ge(pe_event, BANK_EVENT[G_GLU, b])
                if b > 1:
                    sc.wait_ge(glu_full, b - 1)
                act(tmp_a[:, b % 2, :], bank_set(G_GLU)[b][:, :], ACT.Sigmoid,
                    bias=small[:, S_GLUB + b:S_GLUB + b + 1]).then_inc(glu_sig, 1)
                sc.wait_ge(glu_full, b + 1)
                act(act_hi[:, 4 + b, :], tmp_b[:, b % 2, :], ACT.Copy).then_inc(glu_act, 1)
            for n in range(SL_OUT0 + 2, SL_MLP0 + 1):
                split(n)

            def normalise(l, pair):
                sc.wait_ge(ln_rstd[pair], l + 1)
                for i in (2 * pair, 2 * pair + 1):
                    act(resid[:, i, :], acc[:, i, :], ACT.Identity, scale=lns[:, 4, i:i + 1],
                        bias=lns[:, 1, i:i + 1]).then_inc(xhat_ready, 1)

            def norm_hi(l):
                for k in range(KB):
                    sc.wait_ge(ln_psum, 8 * l + k + 1)
                    act(act_hi[:, k, :], norm_bank(k)[:, :], ACT.Identity,
                        scale=small[:, S_LNG + 8 * l + k:S_LNG + 8 * l + k + 1],
                        bias=small[:, S_LNB + 8 * l + k:S_LNB + 8 * l + k + 1]).then_inc(act_hi_done, 1)

            def mlp(g0, n0, h0, r, norm=None):
                for c in range(2):
                    g, n = g0 + 3 * c, n0 + 4 * c
                    split(n + 2, r)
                    for k in range(4):
                        m = h0 + 4 * c + k + 1
                        wait(sc, pe_event, BANK_EVENT[g, k], r, 2 * CHUNK_EVENTS)
                        wait(sc, sq_done, m - 2, r, 8)
                        wait(sc, hid_hi_done, m - 2, r, 8)
                        act(tmp_a[:, k % 2, :], bank_set(g)[k][:, :], ACT.Relu).then_inc(relu_done, 1)
                        wait(sc, relu_done, m, r, 8)
                        act(hid_hi[:, k, :], tmp_a[:, k % 2, :], ACT.Square).then_inc(hid_hi_done, 1)
                    split(n + 3, r)
                    ends = norm is not None and c == 1
                    if norm != 3 or not ends:
                        split(n + 4, r)
                    if ends:
                        normalise(norm, 0)
                    if norm != 3 or not ends:
                        split(n + 5, r)
                    if ends:
                        normalise(norm, 1)

            normalise(0, 0)
            split(SL_MLP0 + 1)
            normalise(0, 1)
            norm_hi(0)
            mlp(G_MLP0, SL_MLP0, 0, 0)
            with sc.Fori(1, 3) as r:
                mlp(G_MLP0, SL_MLP0, 0, r)
            mlp(G_MLP0, SL_MLP0, 0, 3, norm=1)
            norm_hi(1)

            sc.wait_ge(gate_in, 16)
            act(gw_hi[:, :, :], gate_w[:, :, :], ACT.Copy).then_inc(gate_w_hi, 1)
            split(SL_L1 + 2)
            zl = logf[0:16, 1, :]
            sc.wait_ge(gate_z, 1)
            act(zl, zl, ACT.Exp, scale=-1.0).then_inc(gate_z, 1)
            sc.wait_ge(gate_z, 2)
            act(zl, zl, ACT.Ln, bias=1.0).then_inc(gate_z, 1)

            def fox_pair(half, r, first, last):
                u0 = 32 * half

                def H_(k):
                    wait(sc, fx_x, 4 * half + k + 1, r, 1)
                    hi, b0 = (hid_hi, 0) if half == 0 else (act_hi, 4)
                    act(hi[:, bass.ds(r + (k + b0), 1), :], banks[7][:, :].unsqueeze(1), ACT.Copy).then_inc(fx_h, 1)

                for j in range(8):
                    n = P * (j % TT + 1)
                    wait(sc, fx_m, u0 + j + 1, r, 8)
                    wait(sc, fx_t, u0 + j - 3, r, 8)
                    act(e_buf[:, j % 4, 0:n], banks[j % 4][:, 0:n], ACT.Exp, bias=neg_max[:, j:j + 1],
                        accum_out=z_sum[:, j:j + 1]).then_inc(fx_e, 1)
                    if j == 4 and not first:
                        H_(-1)
                if last:
                    H_(0)

            for half in range(2):
                n0, g0 = SL_L1 + 6 * half, G_L1 + 3 * half
                if half:
                    split(n0 + 2)
                for c in range(4):
                    sc.wait_ge(pe_event, BANK_EVENT[g0, c])
                    act(q_all[0:DH, 2 * c, :], bank_set(g0)[c][0:DH, :], ACT.Copy, scale=DH ** -0.5).then_inc(act_step, 1)
                    act(q_all[0:DH, 2 * c + 1, :], bank_set(g0)[c][DH:P, :], ACT.Copy, scale=DH ** -0.5).then_inc(evac_q1, 1)
                split(n0 + 3)
                split(n0 + 4)
                split(n0 + 5)
                split(n0 + 6)
                for i in range(TT):
                    sc.wait_ge(pe_event, BANK_EVENT[g0 + 2, i])
                    act(v_nat[:, i, :], bank_set(g0 + 2)[i][:, :], ACT.Copy).then_inc(evac_act, 1)
                split(n0 + 7)
                fox_pair(half, 0, True, False)
                with sc.Fori(1, 3) as r:
                    fox_pair(half, r, False, False)
                fox_pair(half, 3, False, True)
            for n in range(SL_OUT1 + 2, SL_MLP1 + 1):
                split(n)
            normalise(2, 0)
            split(SL_MLP1 + 1)
            normalise(2, 1)
            norm_hi(2)
            mlp(G_MLP1, SL_MLP1, 32, 0)
            with sc.Fori(1, 3) as r:
                mlp(G_MLP1, SL_MLP1, 32, r)
            mlp(G_MLP1, SL_MLP1, 32, 3, norm=3)

        @block.gpsimd
        def _(pool):
            st = Steps(pool, pool_step)

            def q_slots(q_sem, used, per_used, rows, used0, r):
                for m in range(2):
                    wait(pool, used, used0[m], r, per_used)
                    nc.gpsimd.tensor_copy(q_slot[0:rows, m, :].unsqueeze(1),
                                          q_all[0:rows, bass.ds(r * 2 + m, 1), :]).then_inc(q_sem, 1)

            def power_product(pr, pi, m1, m2, out, scratch):
                full = [P, HG, L, GCH]
                ov, sv = (v.rearrange("p (g e h) -> p g e h", g=HG, e=L) for v in (out, scratch))
                st.settle()
                for prod, pw, m in ((ov, pr, m1), (sv, pi, m2)):
                    st.step(nc.gpsimd.tensor_tensor(prod, pw.unsqueeze(3).broadcast_to(full),
                                                    m.unsqueeze(2).broadcast_to(full), ALU.mult))
                st.settle()
                return nc.gpsimd.tensor_tensor(ov, ov, sv, ALU.add)

            def output_table(h):
                gs = slice(h * HG, (h + 1) * HG)
                power_product(pow_r[:, gs, 0:L], pow_i[:, gs, 0:L], c_ri[:, gs, :], c_ir[:, gs, :],
                              ca_half[h], pool_scr).then_inc(ss_ca, 1)
                pool.wait_ge(ss_ca, h + 1)

            def chunk_phases(levels):
                for lv in levels:
                    n = 1 << lv
                    t1, t2 = (pool_scr[:, o:o + GROUPS * n].rearrange("p (g e) -> p g e", g=GROUPS) for o in (0, 1024))
                    cr = phase[:, lv, :].unsqueeze(2).broadcast_to([P, GROUPS, n])
                    ci = phase[:, 6 + lv, :].unsqueeze(2).broadcast_to([P, GROUPS, n])
                    xr, xi = e_cos[:, :, 0:n], e_sin[:, :, 0:n]
                    for dst, b1, b2, op in ((e_cos, cr, ci, ALU.subtract), (e_sin, ci, cr, ALU.add)):
                        st.settle()
                        st.step(nc.gpsimd.tensor_tensor(t1, xr, b1, ALU.mult))
                        st.step(nc.gpsimd.tensor_tensor(t2, xi, b2, ALU.mult))
                        st.settle()
                        st.step(nc.gpsimd.tensor_tensor(dst[:, :, n:2 * n], t1, t2, op))

            zeros = f_half[0][0:GCH, 0:HG * (L - 1) * GCH]
            nc.gpsimd.memset(zeros, 0.0).then_inc(zero_set, 1)
            pool.wait_ge(zero_set, 1)
            for h in range(2):
                pool.dma_start(t["k_scratch"][:, h * HG:(h + 1) * HG, 0:(L - 1) * GCH],
                               zeros.rearrange("p (g n) -> p g n", g=HG)).then_inc(zero_out, 16)
            pool.wait_ge(zero_out, 32)
            pool.wait_ge(ss_par, 2 * L)
            pool.wait_ge(act_ready, 8)
            for h in range(2):
                gs = slice(h * HG, (h + 1) * HG)
                power_product(prev_r[:, gs, :], prev_i[:, gs, :], bb1[:, gs, :], bb2[:, gs, :],
                              f_half[h], f_scr).then_inc(ss_f, 1)
                pool.wait_ge(ss_f, h + 1)

            pool.wait_ge(rot_done, 8)
            q_slots(at_q, at_s, 4, DH, (0, 0), 0)
            pool.wait_ge(pe_event, SLAB_EVENT[SL_V + 1])
            pool.wait_ge(ss_par, 2 * L + 1)
            output_table(0)
            q_slots(at_q, at_s, 4, DH, (0, 0), 1)
            output_table(1)
            q_slots(at_q, at_s, 4, DH, (0, 0), 2)
            pool.wait_ge(ss_par, 2 * L + 1)
            st.step(nc.gpsimd.memset(e_cos[:, :, 0:1], 1.0))
            st.step(nc.gpsimd.memset(e_sin[:, :, 0:1], 0.0))
            chunk_phases(range(4))
            q_slots(at_q, at_s, 4, DH, (0, 0), 3)
            chunk_phases(range(4, 6))
            st.settle()
            nc.gpsimd.memset(pool_scr[:, 0:1], 0.0).then_inc(ss_ph, 1)

            def rows_in(l):
                st.settle()
                for j, name in enumerate(("g", "b")):
                    row = t["ln%d_%s" % (1 + l % 2, name)][l // 2:l // 2 + 1, :].broadcast_to([P, D])
                    pool.dma_start(ln_row[:, j, :], row).then_inc(row_in, 16)
                pool.wait_ge(row_in, 32 * (l + 1))

            def rstd(l):
                ts_, tt_ = nc.gpsimd.tensor_scalar, nc.gpsimd.tensor_tensor

                def do(ins):
                    st.step(ins)
                    st.settle()

                s2 = slice(0, 2)
                x, y, w = lns[:, 2, s2], lns[:, 4, s2], lns[:, 3, s2]
                pool.wait_ge(ln_var, 4 * l + 2)
                do(ts_(x, mv[:, s2, 1], LN_EPS, None, ALU.add))
                do(ts_(y.bitcast(I32), x.bitcast(I32), -0.5, float(0x5F3759DF), ALU.mult, ALU.add))
                for _ in range(3):
                    do(tt_(w, y, y, ALU.mult))
                    do(tt_(w, w, x, ALU.mult))
                    do(ts_(w, w, -0.5, 1.5, ALU.mult, ALU.add))
                    do(tt_(y, y, w, ALU.mult))
                do(tt_(w, mv[:, s2, 0], y, ALU.mult))
                ts_(lns[:, 1, s2], w, -1.0, None, ALU.mult).then_inc(ln_rstd[0], 1)

            def scaled_residual(l):
                rows_in(l)
                st.step(nc.gpsimd.tensor_scalar(ln_row[:, :, :], ln_row[:, :, :], ALPHA, None, ALU.mult))
                st.settle()
                rstd(l)
                for i in range(TT):
                    pool.wait_ge(xhat_ready, 4 * l + i + 1)
                    st.step(nc.gpsimd.tensor_tensor(acc[:, i, :], resid[:, i, :], ln_row[:, 0, :], ALU.mult))
                    st.settle()
                    nc.gpsimd.tensor_tensor(acc[:, i, :], acc[:, i, :], ln_row[:, 1, :], ALU.add).then_inc(acc_init, 1)

            pool.wait_ge(act_ready, 16)
            scaled_residual(0)
            pool.wait_ge(acc_init, 4)
            rows_in(1)
            rstd(1)
            pool.wait_ge(ln_psum, 16)
            for i in range(TT):
                st.step(nc.gpsimd.tensor_tensor(resid[:, i, :], resid[:, i, :], ln_row[:, 0, :], ALU.mult))
                st.settle()
                nc.gpsimd.tensor_tensor(resid[:, i, :], resid[:, i, :], ln_row[:, 1, :], ALU.add).then_inc(resid_ready, 1)
            pool.wait_ge(resid_ready, 4)
            nc.gpsimd.memset(q_all[DH:DH + 2, :, :], 1.0).then_inc(ones_set, 1)
            nc.gpsimd.memset(k_all[DH:DH + 2, :, :], 1.0).then_inc(ones_set, 1)
            for half in range(2):
                pool.wait_ge(evac_q1, 4 * half + 4)
                pool.wait_ge(decay_in, 32 * half + 32)
                q_slots(fx_q, fx_s, 8, DH + 2, (32 * half, 32 * half), 0)
                with pool.Fori(1, 4) as r:
                    q_slots(fx_q, fx_s, 8, DH + 2, (32 * half - 4, 32 * half), r)
            scaled_residual(2)
            pool.wait_ge(acc_init, 8)
            rows_in(3)
            rstd(3)
            for i in range(2):
                pool.wait_ge(xhat_ready, 12 + i + 1)
                st.step(nc.gpsimd.tensor_tensor(acc[:, i, :], resid[:, i, :], ln_row[:, 0, :], ALU.mult))
                st.settle()
                nc.gpsimd.tensor_tensor(acc[:, i, :], acc[:, i, :], ln_row[:, 1, :], ALU.add).then_inc(out_ready_pool, 1)


ROPE_THETA = 10000.0


def constants():
    c = np.zeros((P, C_N), np.float32)
    i = np.arange(P)
    c[i, C_ID + i] = 1
    c[i, C_SW64 + (i + 64) % P] = np.where(i < 64, -1, 1)
    c[i, C_SW32 + (i ^ 32)] = 1
    c[:, C_MASK0:C_MASK0 + P] = np.where((i[None, :] // DH) > (i[:, None] // DH), NEG, 0)
    c[:, C_MASK1:C_MASK1 + P] = np.where(i[None, :] > i[:, None], NEG, 0)
    inv = (np.float32(ROPE_THETA) ** (-np.arange(0, DH, 2, dtype=np.float32) / np.float32(DH))).astype(np.float32)
    ang = np.arange(S, dtype=np.float32)[:, None] * inv[None, :]
    cos, sin = np.cos(ang).T.astype(np.float32), np.sin(ang).T.astype(np.float32)
    c[:, C_CC:C_CC + S] = np.tile(cos, (4, 1))
    c[:, C_SS:C_SS + S] = np.concatenate([-sin, sin, -sin, sin])
    c[:, C_SGN] = np.where(i < 64, -1, 1)
    return c


def kernel(**inputs):
    import numpy as _np
    import concourse.bacc as _bacc
    from concourse import mybir as _mybir
    from concourse.bass_utils import run_bass_kernel_spmd as _run

    nc = _bacc.Bacc("TRN2", target_bir_lowering=False, num_devices=1)
    a = {k: _np.asarray(v) for k, v in inputs.items()}

    def cols(v):
        return v.reshape(-1, P).T

    def per_state(v):
        return _np.concatenate([v.T, v.T])

    ln_g = _np.stack([a["ln1_g"], a["ln2_g"]], 1)
    ln_b = _np.stack([a["ln1_b"], a["ln2_b"]], 1)
    small = _np.concatenate([
        cols(ln_g), cols(ln_b), per_state(a["ssm_a_re"][0]), per_state(a["ssm_a_im"][0]),
        _np.broadcast_to(a["ssm_log_dt"][0], (P, GROUPS)), cols(a["ssm_d"][0]), cols(a["ssm_glu_b"][0]),
        _np.pad(a["fox_b_f"][0], (0, P - 16))[:, None]], axis=1)
    b_re, b_im = (a[n][0].transpose(1, 0, 2).reshape(NSTATE, -1) for n in ("ssm_b_re", "ssm_b_im"))
    c_re, c_im = (a[n][0].transpose(2, 0, 1).reshape(NSTATE, -1) for n in ("ssm_c_re", "ssm_c_im"))
    ssm_bc = _np.stack([_np.concatenate(p) for p in ((b_re, b_im), (b_im, b_re), (c_re, c_im), (c_im, c_re))], 1)
    arrays = {
        "x": a["x"], "xt": a["x"][0].T.reshape(KB, P, S).transpose(1, 0, 2), "const": constants(), "small": small,
        "ssm_bc": ssm_bc, "ab_w_in": a["ab_w_in"][0], "ab_lambda": a["ab_lambda"], "ab_subln_g": a["ab_subln_g"],
        "ssm_glu_w": a["ssm_glu_w"][0], "ab_w_out": a["ab_w_out"][0], "fox_w_in": a["fox_w_in"][0],
        "fox_w_out": a["fox_w_out"][0], "ln1_g": a["ln1_g"], "ln1_b": a["ln1_b"], "ln2_g": a["ln2_g"],
        "ln2_b": a["ln2_b"], "ffn_w1": a["ffn_w1"], "ffn_w2": a["ffn_w2"],
    }
    arrays = {k: _np.ascontiguousarray(v) for k, v in arrays.items()}
    t = {k: nc.dram_tensor("in_" + k, v.shape, _mybir.dt.from_np(v.dtype), kind="ExternalInput").ap()
         for k, v in arrays.items()}
    t["u_scratch"] = nc.dram_tensor("u_scratch", (GROUPS * GCH, S), _mybir.dt.float32).ap()
    t["k_scratch"] = nc.dram_tensor("k_scratch", (GCH, GROUPS, KD * GCH), _mybir.dt.float32).ap()
    t["y_scratch"] = nc.dram_tensor("y_scratch", (NB, P, GB * NCH), _mybir.dt.float32).ap()
    t["out"] = nc.dram_tensor("out_0", (S, D), _mybir.dt.float32, kind="ExternalOutput").ap()
    trunk(nc, t)
    r = _run(nc, [{"in_" + k: v for k, v in arrays.items()}], core_ids=[0])
    return r.results[0]["out_0"].reshape(1, S, D)
```
